# Optimizing a Trainium2 kernel written in Bass

```python
import math
import jax, jax.numpy as jnp
from jax import lax
import numpy as np

D_MODEL = 1024
BATCH = 1
SEQ = 1024
DEPTH = 1
DEC_BATCH = 8
DEC_SEQ = 4
PAST_LEN = 512
PAGE_SIZE = 128

CONV_W = D_MODEL // 4
POOL_W = D_MODEL // 4
N_HEADS = 8
HEAD_DIM = (D_MODEL - CONV_W - POOL_W) // N_HEADS
NSA_W = N_HEADS * HEAD_DIM
KV_HEADS = 2
GQA_GROUP = N_HEADS // KV_HEADS
KV_W = KV_HEADS * HEAD_DIM
CONV_WIDTH = 31
CONV_BUF = CONV_WIDTH - 1
POOL_WINDOWS = (2, 4, 8, 16)
POOL_GROUP_W = POOL_W // len(POOL_WINDOWS)
POOL_BUF = max(POOL_WINDOWS) - 1
CMP_STRIDE = 16
CMP_BLOCK = 2 * CMP_STRIDE
SLC_BLOCK = 64
SLC_TOPK = 16
WINDOW = 512
Q_BLOCK = 128
NUM_BUCKETS = 32
MAX_DISTANCE = 128
D_FF = -(-(8 * D_MODEL) // (3 * 256)) * 256
EPS = 1e-6
NEG = -1e30
FORCE = 1e4

OFF_POOL = 2 * CONV_W
OFF_Q = OFF_POOL + POOL_W
OFF_KV = OFF_Q + NSA_W
OFF_GATE = OFF_KV + 6 * KV_W
IN_W = OFF_GATE + 3 * N_HEADS

kernel_name = 'hybrid_conv_pool_nsa_decoder_step'

def rmsnorm(x, g):
    xf = x.astype(jnp.float32)
    y = xf * lax.rsqrt(jnp.mean(xf * xf, axis=-1, keepdims=True) + EPS)
    return (y * g.astype(jnp.float32)).astype(x.dtype)

def layernorm(x, g, b):
    xf = x.astype(jnp.float32)
    mu = jnp.mean(xf, axis=-1, keepdims=True)
    xc = xf - mu
    var = jnp.mean(xc * xc, axis=-1, keepdims=True)
    return (xc * lax.rsqrt(var + EPS) * g.astype(jnp.float32) + b.astype(jnp.float32)).astype(x.dtype)

def t5_bucket(dist):
    n = jnp.maximum(dist, 0)
    max_exact = NUM_BUCKETS // 2
    nf = jnp.maximum(n, 1).astype(jnp.float32)
    large = max_exact + (jnp.log(nf / max_exact) / math.log(MAX_DISTANCE / max_exact)
                         * (NUM_BUCKETS - max_exact)).astype(jnp.int32)
    large = jnp.minimum(large, NUM_BUCKETS - 1)
    return jnp.where(n < max_exact, n, large)

def masked_softmax(s, mask):
    s = jnp.where(mask, s.astype(jnp.float32), NEG)
    p = jax.nn.softmax(s, axis=-1)
    return p * jnp.any(mask, axis=-1, keepdims=True)

def project(h, w_in):
    B, T, _ = h.shape
    z = h @ w_in
    glu = z[..., :CONV_W] * jax.nn.sigmoid(z[..., CONV_W:OFF_POOL])
    u = z[..., OFF_POOL:OFF_Q]
    q = z[..., OFF_Q:OFF_KV].reshape(B, T, KV_HEADS, GQA_GROUP, HEAD_DIM)
    kv = z[..., OFF_KV:OFF_GATE].reshape(B, T, 3, 2, KV_HEADS, HEAD_DIM)
    gates = jax.nn.sigmoid(z[..., OFF_GATE:]).reshape(B, T, 3, KV_HEADS, GQA_GROUP, 1)
    return glu, u, q, kv, gates

def conv_mix(glu_ext, dw, b, ln_g, ln_b):
    y = lax.conv_general_dilated(glu_ext, dw[:, None, :], window_strides=(1,), padding='VALID',
                                 dimension_numbers=('NWC', 'WIO', 'NWC'),
                                 feature_group_count=CONV_W)
    return jax.nn.silu(layernorm(y + b, ln_g, ln_b))

def pool_mix(u_ext, pos0, w_pool, scale):
    B, L, _ = u_ext.shape
    T = L - POOL_BUF
    cs = jnp.pad(jnp.cumsum(u_ext.astype(jnp.float32), axis=1), ((0, 0), (1, 0), (0, 0)))
    end = cs[:, POOL_BUF + 1:POOL_BUF + 1 + T]
    u = u_ext[:, POOL_BUF:].astype(jnp.float32)
    t = pos0 + jnp.arange(T, dtype=jnp.int32)
    diffs = []
    for g, w in enumerate(POOL_WINDOWS):
        sl = slice(g * POOL_GROUP_W, (g + 1) * POOL_GROUP_W)
        start = cs[:, POOL_BUF + 1 - w:POOL_BUF + 1 - w + T, sl]
        cnt = jnp.minimum(w, t + 1).astype(jnp.float32)[:, None]
        diffs.append((end[..., sl] - start) / cnt - u[..., sl])
    d = jnp.stack(diffs, axis=2)
    y = jnp.einsum('btgc,gce->btge', d, w_pool.astype(jnp.float32)).reshape(B, T, POOL_W)
    return (y * scale.astype(jnp.float32)).astype(u_ext.dtype)

def compress(k, pe, w):
    B, L = k.shape[:2]
    Lp = -(-L // CMP_STRIDE) * CMP_STRIDE
    k = jnp.pad(k, ((0, 0), (0, Lp - L), (0, 0), (0, 0)))
    sub = k.reshape(B, Lp // CMP_STRIDE, CMP_STRIDE, KV_HEADS, HEAD_DIM)
    blocks = jnp.concatenate([sub[:, :-1], sub[:, 1:]], axis=2)
    return jnp.einsum('bnlgd,lde->bnge', blocks + pe[:, None, :], w)

def to_blocks(k):
    B, L = k.shape[:2]
    Lp = -(-L // SLC_BLOCK) * SLC_BLOCK
    k = jnp.pad(k, ((0, 0), (0, Lp - L), (0, 0), (0, 0)))
    return k.reshape(B, Lp // SLC_BLOCK, SLC_BLOCK, KV_HEADS, HEAD_DIM).transpose(0, 3, 1, 2, 4)

def nsa_attend(q, q_pos, kc, vc, ks, vs, kw, vw, kw_pos, tbl):
    B, Q = q.shape[:2]
    scale = HEAD_DIM ** -0.5
    n_cmp, n_slc = kc.shape[1], ks.shape[2]
    c_end = jnp.arange(n_cmp, dtype=jnp.int32) * CMP_STRIDE + (CMP_BLOCK - 1)
    dist = q_pos[:, None] - c_end[None, :]
    s = jnp.einsum('bqgrd,bngd->bgrqn', q, kc).astype(jnp.float32) * scale + tbl[:, :, t5_bucket(dist)]
    p_cmp = masked_softmax(s, dist >= 0)
    o_cmp = jnp.einsum('bgrqn,bngd->bqgrd', p_cmp.astype(vc.dtype), vc)
    c_start = jnp.arange(n_cmp, dtype=jnp.int32) * CMP_STRIDE
    s_start = jnp.arange(n_slc, dtype=jnp.int32) * SLC_BLOCK
    overlap = ((c_start[:, None] < s_start[None, :] + SLC_BLOCK)
               & (c_start[:, None] + CMP_BLOCK > s_start[None, :])).astype(jnp.float32)
    p_slc = jnp.einsum('bgrqn,nj->bgqj', p_cmp, overlap)
    blk = jnp.arange(n_slc, dtype=jnp.int32)[None, :]
    cur = (q_pos // SLC_BLOCK)[:, None]
    forced = (blk == 0) | (blk == cur) | (blk == cur - 1)
    score = jnp.where(forced, FORCE, jnp.where(blk <= cur, p_slc, NEG))
    _, idx = lax.top_k(score, min(SLC_TOPK, n_slc))
    n_sel = idx.shape[-1]
    M = n_sel * SLC_BLOCK
    bi = jnp.arange(B)[:, None, None, None]
    gi = jnp.arange(KV_HEADS)[None, :, None, None]
    kg = ks[bi, gi, idx].reshape(B, KV_HEADS, Q, M, HEAD_DIM)
    vg = vs[bi, gi, idx].reshape(B, KV_HEADS, Q, M, HEAD_DIM)
    pos = (idx[..., None] * SLC_BLOCK + jnp.arange(SLC_BLOCK, dtype=jnp.int32)).reshape(B, KV_HEADS, Q, M)
    dist = q_pos[None, None, :, None] - pos
    bias = tbl[gi[..., None], jnp.arange(GQA_GROUP)[None, None, :, None, None], t5_bucket(dist)[:, :, None]]
    s = jnp.einsum('bqgrd,bgqmd->bgrqm', q, kg).astype(jnp.float32) * scale + bias
    p = masked_softmax(s, (dist >= 0)[:, :, None])
    o_slc = jnp.einsum('bgrqm,bgqmd->bqgrd', p.astype(vg.dtype), vg)
    dist = q_pos[:, None] - kw_pos[None, :]
    mask = (dist >= 0) & (dist < WINDOW) & (kw_pos[None, :] >= 0)
    s = jnp.einsum('bqgrd,bkgd->bgrqk', q, kw).astype(jnp.float32) * scale + tbl[:, :, t5_bucket(dist)]
    p = masked_softmax(s, mask)
    o_win = jnp.einsum('bgrqk,bkgd->bqgrd', p.astype(vw.dtype), vw)
    return o_cmp, o_slc, o_win

def gate_sum(gates, o_cmp, o_slc, o_win):
    return gates[:, :, 0] * o_cmp + gates[:, :, 1] * o_slc + gates[:, :, 2] * o_win

def nsa_prompt(q, kv, gates, pe_k, wk, pe_v, wv, tbl):
    B, T = q.shape[:2]
    kc = compress(kv[:, :, 0, 0], pe_k, wk)
    vc = compress(kv[:, :, 0, 1], pe_v, wv)
    ks = to_blocks(kv[:, :, 1, 0])
    vs = to_blocks(kv[:, :, 1, 1])
    pad = ((0, 0), (WINDOW, 0), (0, 0), (0, 0))
    kw = jnp.pad(kv[:, :, 2, 0], pad)
    vw = jnp.pad(kv[:, :, 2, 1], pad)

    def block(i):
        q0 = i * Q_BLOCK
        qb = lax.dynamic_slice_in_dim(q, q0, Q_BLOCK, axis=1)
        gb = lax.dynamic_slice_in_dim(gates, q0, Q_BLOCK, axis=1)
        kwb = lax.dynamic_slice_in_dim(kw, q0, WINDOW + Q_BLOCK, axis=1)
        vwb = lax.dynamic_slice_in_dim(vw, q0, WINDOW + Q_BLOCK, axis=1)
        q_pos = q0 + jnp.arange(Q_BLOCK, dtype=jnp.int32)
        kw_pos = q0 - WINDOW + jnp.arange(WINDOW + Q_BLOCK, dtype=jnp.int32)
        return gate_sum(gb, *nsa_attend(qb, q_pos, kc, vc, ks, vs, kwb, vwb, kw_pos, tbl))

    o = lax.map(block, jnp.arange(T // Q_BLOCK, dtype=jnp.int32))
    return jnp.moveaxis(o, 0, 1).reshape(B, T, NSA_W)

def nsa_sample(q, kv, gates, cmp_pages, slc_pages, win_buf, page_table, pe_k, wk, pe_v, wv, tbl):
    B, S = q.shape[:2]
    past = page_table.shape[1] * cmp_pages.shape[1]
    cmp_full = jnp.concatenate([cmp_pages[page_table].reshape(B, past, 2, KV_HEADS, HEAD_DIM), kv[:, :, 0]], axis=1)
    slc_full = jnp.concatenate([slc_pages[page_table].reshape(B, past, 2, KV_HEADS, HEAD_DIM), kv[:, :, 1]], axis=1)
    win = jnp.concatenate([win_buf, kv[:, :, 2]], axis=1)
    wb = win_buf.shape[1]
    kc = compress(cmp_full[:, :, 0], pe_k, wk)
    vc = compress(cmp_full[:, :, 1], pe_v, wv)
    ks = to_blocks(slc_full[:, :, 0])
    vs = to_blocks(slc_full[:, :, 1])
    q_pos = past + jnp.arange(S, dtype=jnp.int32)
    kw_pos = past - wb + jnp.arange(wb + S, dtype=jnp.int32)
    o = gate_sum(gates, *nsa_attend(q, q_pos, kc, vc, ks, vs, win[:, :, 0], win[:, :, 1], kw_pos, tbl))
    return o.reshape(B, S, NSA_W), win[:, S:]

def residual_update(x, conv_o, pool_o, nsa_o, w_out, g2, w_gu, w_down):
    x = x + jnp.concatenate([conv_o, pool_o, nsa_o], axis=-1) @ w_out
    gu = rmsnorm(x, g2) @ w_gu
    return x + (jax.nn.silu(gu[..., :D_FF]) * gu[..., D_FF:]) @ w_down

def setup_inputs(seed: int = 0) -> dict:
    key = jax.random.key(seed)
    k = jax.random.split(key, 26)
    f32 = jnp.float32

    def nrm(kk, shape, s):
        return jax.random.normal(kk, shape, f32) * s

    n_pages = PAST_LEN // PAGE_SIZE
    n_used = DEC_BATCH * n_pages
    n_phys = n_used + max(1, n_used // 4)
    win_len = min(WINDOW, PAST_LEN)
    page_table = jax.random.permutation(k[7], n_phys)[:n_used].reshape(DEC_BATCH, n_pages).astype(jnp.int32)
    return {
        'x_prompt': nrm(k[0], (BATCH, SEQ, D_MODEL), 1.0),
        'x_sample': nrm(k[1], (DEC_BATCH, DEC_SEQ, D_MODEL), 1.0),
        'cache_cmp_kv': nrm(k[2], (DEPTH, n_phys, PAGE_SIZE, 2, KV_HEADS, HEAD_DIM), 1.0),
        'cache_slc_kv': nrm(k[3], (DEPTH, n_phys, PAGE_SIZE, 2, KV_HEADS, HEAD_DIM), 1.0),
        'cache_win_kv': nrm(k[4], (DEPTH, DEC_BATCH, win_len, 2, KV_HEADS, HEAD_DIM), 1.0),
        'state_conv': nrm(k[5], (DEPTH, DEC_BATCH, CONV_BUF, CONV_W), 0.5),
        'state_pool': nrm(k[6], (DEPTH, DEC_BATCH, POOL_BUF, POOL_W), 1.0),
        'page_table': page_table,
        'rel_bias': nrm(k[8], (NUM_BUCKETS, N_HEADS), 0.5),
        'norm1': 1.0 + nrm(k[9], (DEPTH, D_MODEL), 0.02),
        'w_in': nrm(k[10], (DEPTH, D_MODEL, IN_W), D_MODEL ** -0.5),
        'conv_dw': nrm(k[11], (DEPTH, CONV_WIDTH, CONV_W), CONV_WIDTH ** -0.5),
        'conv_b': nrm(k[12], (DEPTH, CONV_W), 0.02),
        'conv_ln_g': 1.0 + nrm(k[13], (DEPTH, CONV_W), 0.02),
        'conv_ln_b': nrm(k[14], (DEPTH, CONV_W), 0.02),
        'pool_w': nrm(k[15], (DEPTH, len(POOL_WINDOWS), POOL_GROUP_W, POOL_GROUP_W), POOL_GROUP_W ** -0.5),
        'pool_scale': 1.0 + nrm(k[16], (DEPTH, POOL_W), 0.1),
        'cmp_pe_k': nrm(k[17], (DEPTH, CMP_BLOCK, HEAD_DIM), 0.02),
        'cmp_wk': nrm(k[18], (DEPTH, CMP_BLOCK, HEAD_DIM, HEAD_DIM), (CMP_BLOCK * HEAD_DIM) ** -0.5),
        'cmp_pe_v': nrm(k[19], (DEPTH, CMP_BLOCK, HEAD_DIM), 0.02),
        'cmp_wv': nrm(k[20], (DEPTH, CMP_BLOCK, HEAD_DIM, HEAD_DIM), (CMP_BLOCK * HEAD_DIM) ** -0.5),
        'w_out': nrm(k[21], (DEPTH, CONV_W + POOL_W + NSA_W, D_MODEL), D_MODEL ** -0.5),
        'norm2': 1.0 + nrm(k[22], (DEPTH, D_MODEL), 0.02),
        'w_gu': nrm(k[23], (DEPTH, D_MODEL, 2 * D_FF), D_MODEL ** -0.5),
        'w_down': nrm(k[24], (DEPTH, D_FF, D_MODEL), D_FF ** -0.5),
        'final_norm': 1.0 + nrm(k[25], (D_MODEL,), 0.02),
    }

def reference(x_prompt, x_sample, cache_cmp_kv, cache_slc_kv, cache_win_kv, state_conv, state_pool,
              page_table, rel_bias, norm1, w_in, conv_dw, conv_b, conv_ln_g, conv_ln_b, pool_w,
              pool_scale, cmp_pe_k, cmp_wk, cmp_pe_v, cmp_wv, w_out, norm2, w_gu, w_down, final_norm):
    tbl = rel_bias.reshape(NUM_BUCKETS, KV_HEADS, GQA_GROUP).transpose(1, 2, 0)
    T = x_prompt.shape[1]
    past = page_table.shape[1] * cache_cmp_kv.shape[2]
    xp, xs = x_prompt, x_sample
    p_cmp, p_slc, p_win, p_conv, p_pool = [], [], [], [], []
    s_cmp, s_slc, s_win, s_conv, s_pool = [], [], [], [], []
    for l in range(DEPTH):
        glu, u, q, kv, gates = project(rmsnorm(xp, norm1[l]), w_in[l])
        glu_ext = jnp.pad(glu, ((0, 0), (CONV_BUF, 0), (0, 0)))
        u_ext = jnp.pad(u, ((0, 0), (POOL_BUF, 0), (0, 0)))
        conv_o = conv_mix(glu_ext, conv_dw[l], conv_b[l], conv_ln_g[l], conv_ln_b[l])
        pool_o = pool_mix(u_ext, 0, pool_w[l], pool_scale[l])
        nsa_o = nsa_prompt(q, kv, gates, cmp_pe_k[l], cmp_wk[l], cmp_pe_v[l], cmp_wv[l], tbl)
        xp = residual_update(xp, conv_o, pool_o, nsa_o, w_out[l], norm2[l], w_gu[l], w_down[l])
        p_cmp.append(kv[:, :, 0])
        p_slc.append(kv[:, :, 1])
        p_win.append(kv[:, T - min(WINDOW, T):, 2])
        p_conv.append(glu_ext[:, -CONV_BUF:])
        p_pool.append(u_ext[:, -POOL_BUF:])
        glu, u, q, kv, gates = project(rmsnorm(xs, norm1[l]), w_in[l])
        glu_ext = jnp.concatenate([state_conv[l], glu], axis=1)
        u_ext = jnp.concatenate([state_pool[l], u], axis=1)
        conv_o = conv_mix(glu_ext, conv_dw[l], conv_b[l], conv_ln_g[l], conv_ln_b[l])
        pool_o = pool_mix(u_ext, past, pool_w[l], pool_scale[l])
        nsa_o, new_win = nsa_sample(q, kv, gates, cache_cmp_kv[l], cache_slc_kv[l], cache_win_kv[l],
                                    page_table, cmp_pe_k[l], cmp_wk[l], cmp_pe_v[l], cmp_wv[l], tbl)
        xs = residual_update(xs, conv_o, pool_o, nsa_o, w_out[l], norm2[l], w_gu[l], w_down[l])
        s_cmp.append(kv[:, :, 0])
        s_slc.append(kv[:, :, 1])
        s_win.append(new_win)
        s_conv.append(glu_ext[:, -CONV_BUF:])
        s_pool.append(u_ext[:, -POOL_BUF:])
    y_prompt = rmsnorm(xp, final_norm)
    y_sample = rmsnorm(xs, final_norm)
    return (y_prompt, y_sample,
            jnp.stack(p_cmp), jnp.stack(p_slc), jnp.stack(p_win), jnp.stack(p_conv), jnp.stack(p_pool),
            jnp.stack(s_cmp), jnp.stack(s_slc), jnp.stack(s_win), jnp.stack(s_conv), jnp.stack(s_pool))


_drawn_inputs = setup_inputs


def setup_inputs(seed=0):
    import zlib

    import numpy as np

    out = dict(_drawn_inputs(seed))
    spreads = {}
    factors = {'norm1': 2.668,
     'conv_b': 5.052,
     'conv_ln_g': 7.649,
     'conv_ln_b': 8.0,
     'cmp_pe_k': 8.0,
     'cmp_pe_v': 8.0,
     'norm2': 4.223,
     'final_norm': 2.776}
    for name, (base, spread) in spreads.items():
        noise = np.random.default_rng([zlib.crc32(name.encode()), seed]).standard_normal(out[name].shape)
        drawn = base * np.exp(spread * noise) if base else spread * noise
        out[name] = __import__('jax').numpy.asarray(drawn.astype(out[name].dtype))
    for name, factor in factors.items():
        out[name] = (out[name] * factor).astype(out[name].dtype)
    return out
```

```python
import math
from contextlib import ExitStack

import numpy as np

import concourse.bass as bass
from concourse import mybir

F32 = mybir.dt.float32
I32 = mybir.dt.int32
ALU = mybir.AluOpType
ACT = mybir.ActivationFunctionType
AX = mybir.AxisListType.X

P = 128
D = 1024
T = 1024
NB, NS = 8, 4
TS = NB * NS
TT = T + TS
NT = T // P
KD = D // P
PAST, PAGE = 512, 128
NPG = PAST // PAGE
CONV_W, POOL_W, NH, HD, KVH = 256, 256, 8, 64, 2
GQ = NH // KVH
CW, CB = 31, 30
PB = 15
WINS = (2, 4, 8, 16)
STRIDE, CBLK, WINDOW = 16, 32, 512
NCMP = T // STRIDE - 1
BUCKETS, MAXD = 32, 128
DFF = 2816
KF = DFF // P
EPS, NEG = 1e-6, -1e30
OFF_POOL, OFF_Q = 2 * CONV_W, 2 * CONV_W + POOL_W
OFF_KV = OFF_Q + NH * HD
KVC = 6 * KVH * HD
KVG = KVC + 3 * NH
IN_W = OFF_KV + KVG
NCH = TT // 3
GE, UE = CB + NS, PB + NS
GLU_L = CB + T + NB * GE
U_L = PB + T + NB * UE
Y_L = GLU_L - CB
NF = 2
FT = KF // NF
DLO, DHI = -160, 256
ND = DHI - DLO + 1
BAND = 3 * P
C_ID, C_OH, C_MN, C_MW, C_MC = 0, 128, 416, 480, 484
C_GM, C_VA, C_IW, C_FX, C_SEL, C_END = 612, 636, 637, 639, 669, 925
CMPN = 15
KC_L = NB * PAST + TT
KC_N = KC_L // STRIDE - 1


def bucket(n):
    n = np.asarray(n)
    e = BUCKETS // 2
    big = e + (np.log(np.maximum(n, 1).astype(np.float32) / e) / math.log(MAXD / e) * (BUCKETS - e)).astype(np.int32)
    return np.where(n < e, n, np.minimum(big, BUCKETS - 1))


def onehot(d):
    m = np.zeros((BUCKETS + 1, len(d)), np.float32)
    for j, x in enumerate(d):
        if x >= 0:
            m[bucket(x), j] += 1
            m[BUCKETS - 1, j] -= 1
        else:
            m[BUCKETS, j] = NEG
    return m


def constants():
    dist = np.concatenate([onehot(np.arange(DLO, DHI + 1)), onehot(2 * P - 1 - np.arange(BAND))], axis=1)
    c = np.zeros((P, C_END), np.float32)
    c[:, C_ID:C_ID + P] = np.eye(P)
    for t in range(NS):
        r = slice(32 * t, 32 * t + 32)
        c[r, C_OH:C_OH + 128] = onehot(PAST + t - (384 + np.arange(128)))[:32]
        c[r, C_OH + 128:C_OH + 160] = onehot(t - np.tile(np.arange(NS), NB))[:32]
        n = np.tile(np.arange(32), 4)
        o = onehot(PAST + t - (STRIDE * n + CBLK - 1))[:32]
        c[r, C_OH + 160:C_OH + 288] = o
    for row in range(P):
        b, h, t = row // 32, row // 4 % 8, row % 4
        for G in range(2):
            for col in range(32):
                if col // 4 != 4 * G + b or col % 4 > t:
                    c[row, C_MN + 32 * G + col] = NEG
            c[4 * 4 * G + 4 * b + t, C_SEL + 128 * G + row] = 1
        c[row, C_MW:C_MW + 4] = np.where(np.arange(4) <= t, NEG, 0)
        col = np.arange(128)
        c[row, C_MC:C_MC + 128] = np.where((col // 32 != b) | (col % 32 == 31), NEG, 0)
        for br in range(3):
            c[row, C_GM + 8 * br + h] = 1
    c[:, C_VA] = np.arange(P) >= CBLK - 1
    for k in range(2):
        w = np.where(np.arange(P) < 64, WINS[2 * k], WINS[2 * k + 1])
        c[:, C_IW + k] = 1.0 / w
        c[:, C_FX + 15 * k:C_FX + 15 * k + 15] = w[:, None] / np.minimum(w[:, None], np.arange(15)[None] + 1)
    tri = np.where(np.arange(P)[:, None] >= np.arange(P)[None, :], NEG, 0).astype(np.float32)
    return {"c_dist": dist, "c_pack": c, "c_tri": tri}


def tile_rows(i):
    return P if i < NT else TS


def jobs_list():
    js = [("s", G, 0, br) for G in range(2) for br in range(3)]
    return js + [("p", i, h, br) for i in range(NT) for h in range(NH) for br in range(3)]


def job_width(job):
    kind, i, h, br = job
    if kind == "s":
        return 128 if br == 0 else PAST + TS
    return 8 * i + 7 if br == 0 else P * (i + 1) if br == 1 else P * min(i + 1, 5)


def job_groups(job):
    w = job_width(job)
    cols = [(c, min(P, w - c)) for c in range(0, w, P)]
    return [cols[k:k + 4] for k in range(0, len(cols), 4)]


JOBS = jobs_list()
NJ = len(JOBS)
ZTILES = [CONV_W, 0, CONV_W + P, P, OFF_POOL, OFF_POOL + P]
NZ = len(ZTILES) + GQ


def turn_units():
    keys = [("pe", 0), ("pe", 1), ("knew", 0), ("knew", 1)]
    keys += [("kT", ty, hf) for ty in range(4) for hf in range(2)]
    keys += [("cp", b, kv) for b in range(NB) for kv in range(2)]
    keys += [("vc", x) for x in range(3)]
    for j in range(-2, NJ):
        if j + 2 < NJ and JOBS[j + 2][0] == "s" and JOBS[j + 2][3] > 0:
            keys += [("kp", j + 2, b) for b in range(4)]
        if j >= 0:
            keys += [("P", j, k) for k in range(len(job_groups(JOBS[j])))]
            if pair_out(j) is not None:
                keys.append(("o", pair_out(j)))
    keys.append(("o", NT - 1 + 2))
    return {k: n for n, k in enumerate(keys)}


def pair_out(j):
    if j in (3, 6):
        return j // 3 - 1
    if j > 6 and (j - 6) % (3 * NH) == 0:
        return 2 + (j - 6) // (3 * NH) - 1
    return None


UNIT = turn_units()
PUNIT = {k: n for n, k in enumerate([k for k in UNIT if k[0] == "P"])}
KUNIT = {k: n for n, k in enumerate([k for k in UNIT if k[0] == "kp"])}


def build(nc, A, out):
    ctx = ExitStack()
    with ctx:
        def sem(name):
            return ctx.enter_context(nc.semaphore(name))

        def sb(name, shape, at=ctx, dt=F32):
            return at.enter_context(nc.sbuf_tensor(name, shape, dt))

        psA = ctx.enter_context(nc.psum_tensor("psA", [P, 1024], F32))
        psB = ctx.enter_context(nc.psum_tensor("psB", [P, 1024], F32))
        psC = ctx.enter_context(nc.psum_tensor("psC", [P, 1024], F32))
        psD = ctx.enter_context(nc.psum_tensor("psD", [P, 1024], F32))
        bank = [t[:, 512 * k:512 * k + 512] for t in (psA, psB, psC, psD) for k in range(2)]
        scores = [psA, psB]

        cpk = sb("cpk", [P, C_END])
        avg = sb("avg", [P, P])
        featT = sb("featT", [P, KD, TT])
        gB = sb("gB", [P, D])
        small = sb("small", [P, 64])
        mhalf, epsc = small[:, 0:1], small[:, 1:2]
        stat, ms, rstd = small[:, 2:11], small[:, 11:20], small[:, 20:29]
        convb, lng, lnb, pscale = (small[:, 29 + 2 * k:31 + 2 * k] for k in range(4))
        posk = small[:, 37:39]
        nmax = small[:, 39:41]
        sums = [small[:, 41:44], small[:, 44:47]]
        rec = [small[:, 47:50], small[:, 50:53]]
        sgate = small[:, 53:59]
        ident = cpk[:, C_ID:C_ID + P]

        mid = ExitStack()
        kvtok = sb("kvtok", [P, NT + 1, KVG], mid)
        qT = sb("qT", [P, GQ, TT], mid)
        kslcT = sb("kslcT", [P, T], mid)
        kwinT = sb("kwinT", [P, T], mid)
        knewT = sb("knewT", [P, 2, TS], mid)
        btab = sb("btab", [P, NH, 256], mid)
        ctab = sb("ctab", [P, NH, CMPN], mid)
        stab = sb("stab", [P, 320], mid)
        tri = sb("tri", [P, P], mid)
        convw = sb("convw", [P, 2, CW], mid)

        early = ExitStack()
        kvw = sb("kvw", [P, KD, KVG], early)
        wring = sb("wring", [P, 3, KD, P], early)
        xring = sb("xring", [P, 2, D], early)
        ybuf = sb("ybuf", [P, 2, GLU_L], early)
        glu = sb("glu", [P, 2, GLU_L], early)
        uex = sb("uex", [P, 2, U_L], early)
        pl = sb("pl", [P, 2, U_L], early)
        dT = sb("dT", [P, 2, TT], early)
        poolbd = sb("poolbd", [P, 2, P], early)
        stin = sb("stin", [P, 4, 256], early)
        newcols = sb("newcols", [P, 4, TS], early)
        kflat = kvw[:, :, :].rearrange("p k n -> p (k n)")
        yc = kflat[:, 0:2 * TT].rearrange("p (c t) -> p c t", c=2)
        ysq = kflat[:, 2 * TT:4 * TT].rearrange("p (c t) -> p c t", c=2)
        ystd = kflat[:, 4 * TT:5 * TT]
        yflat = ybuf[:, :, :].rearrange("p c n -> p (c n)")
        xn = [yflat[:, 0:D], yflat[:, D:2 * D]]
        sig = pl[:, 0, 0:TT]
        sqjunk = pl[:, 1, 0:D]
        dflat = dT[:, :, :].rearrange("p c t -> p (c t)")
        rbias, rbias4 = dflat[0:33, 0:NH], dflat[:, 16:16 + NH]
        fvec = dflat[0:NH, 64:64 + BAND]
        tsel = dflat[:, 448:576]
        distt = dflat[0:33, 576:576 + ND + BAND]
        lastT = stin[0:32, :, :]

        early.close()
        late = ExitStack()
        ckT = sb("ckT", [P, KC_L], late)
        cvT = sb("cvT", [P, KC_L], late)
        cmpw = sb("cmpw", [P, 2, 8, P], late)
        pages = sb("pages", [P, 8, NPG, 256], late)
        qbd = sb("qbd", [P, 2, P], late)
        kcT = sb("kcT", [P, KC_N - 1], late)
        vcT = sb("vcT", [P, KC_N - 1], late)
        vctok = sb("vctok", [P, 3, P], late)
        posr = sb("posr", [32, 2, P], late)
        prob = [ckT[:, 1024 * k:1024 * k + 1024] for k in range(2)]
        probT = [ckT[:, 2048 + 512 * k:2560 + 512 * k] for k in range(2)]
        oacc = [ckT[:, 3072 + 512 * k:3584 + 512 * k] for k in range(2)]
        kpT = [cvT[:, 512 * k:512 * k + 512] for k in range(2)]
        gjunk = cvT[:, 1024:1072]
        osmp = [cvT[:, 1152 + P * k:1152 + P * k + P] for k in range(2)]
        late.close()
        mid.close()

        xt = sb("xt", [P, NT + 1, D])
        act = sb("act", [P, FT, TT])
        guw = sb("guw", [P, 2, 2, KD, P])
        silu = sb("silu", [P, 3, NCH])
        backT = sb("backT", [P, 2, TT])
        bw = sb("bw", [P, 3, FT, P])
        xn2 = sb("xn2", [P, 2, D])

        scratch = nc.dram_tensor("bias_scratch", [NH, P, BAND], F32, kind="Internal")

        names = (
            "const_in table_in gain_in x_in0 x_in1 state_in w_in0 w_in1 w_in2 kvw_in ptab_in chan_in poolw_in "
            "tri_in table_mm table_ev fvec_ev fvec_out btab_in tsel_done prep "
            "sq_done ms_done rstd_done xn_done turn_x evac_xa evac_xd state_turn state_ev "
            "z_mm sig_done glu_done zc_done kv_mm kv_ev gates_done valid_done "
            "dve pool pairsum pool_used pool_d conv_done mean_mm yc_done sq2_done var_mm std_done inv_done norm_done "
            "mix_done pool_mm newcols_done last_turn last_ev stores pzero "
            "late_zero turn_fill turn_drain page_in0 page_in1 cmpw_in0 cmpw_in1 cmpw_used cmp_mm pos_done cmp_ev posr_in "
            "gate_mm gate_ev qbd_done score_mm score_in exp_done probT_used keys_used pv_done out_done "
            "oacc_free x2_in back_in0 back_in1 back_in2 back_mm back_ev backT_turn x_add "
            "sq3 ms3 rstd3 xn3 turn3 evac3a evac3d gu_in0 gu_in1 gu_mm silu_done act_done gain2_in gain3_in "
            "y_done y_out0 y_out1").split()
        s = {n: sem(n) for n in names}
        cpage = [sem(f"cmp_page{b}") for b in range(NB)]
        block = ctx.enter_context(nc.Block())

        chunks = [(NCH * n, NCH) for n in range(3)]
        lnchunks = [(0, 512), (512, 512), (T, TS)]

        def smp(t, L, ext, lo, n):
            return t[:, L:].rearrange("p (b g) -> p b g", g=ext)[:, :, lo:lo + n]

        def ext_cols(t, c, at, w, start, ext, lo):
            parts = []
            if at < T:
                n = min(w, T - at)
                parts.append((0, n, t[:, c, start + at:start + at + n]))
            if at + w > T:
                parts.append((T - at, w, smp(t[:, c, :], start + T, ext, lo, NS)))
            return parts

        @block.sync
        def _(sp):
            sp.dma_start(cpk[:, :], A["c_pack"]).then_inc(s["const_in"], 16)
            sp.dma_start(distt, A["c_dist"]).then_inc(s["table_in"], 16)
            sp.dma_start(rbias[0:32, :], A["rel_bias"]).then_inc(s["table_in"], 16)
            for t in range(NS):
                sp.dma_start(rbias4[32 * t:32 * t + 32, :], A["rel_bias"]).then_inc(s["table_in"], 16)
            sp.dma_start(gB[:, :], A["norm1"].to_broadcast([P, D])).then_inc(s["gain_in"], 16)

            def load_x(dst, i):
                n = tile_rows(i)
                src = A["x_prompt"][0, P * i:P * i + P, :] if i < NT else A["x_sample"].rearrange("b t d -> (b t) d")
                return sp.dma_start(dst[0:n, :], src)

            w_in = A["w_in"][0].rearrange("(k p) n -> p k n", p=P)

            def load_z(m):
                slot, q = wring[:, m % 3], m - len(ZTILES)
                if m >= 3:
                    sp.wait_ge(s["z_mm"], m - 2)
                if q < 0:
                    sp.dma_start(slot, w_in[:, :, ZTILES[m]:ZTILES[m] + P]).then_inc(s[f"w_in{m % 3}"], 32)
                else:
                    for g in range(KVH):
                        c = OFF_Q + HD * (GQ * g + q)
                        sp.dma_start(slot[:, :, HD * g:HD * g + HD], w_in[:, :, c:c + HD]).then_inc(s[f"w_in{m % 3}"], 16)

            for i in range(2):
                load_x(xring[:, i], i).then_inc(s[f"x_in{i}"], 16)
            for k in range(2):
                sp.dma_start(stin[0:120, k, :], A["state_conv"][0, 4 * k:4 * k + 4].rearrange("b t c -> (b t) c")
                             ).then_inc(s["state_in"], 16)
            sp.dma_start(stin[0:120, 2, :], A["state_pool"][0].rearrange("b t c -> (b t) c")).then_inc(s["state_in"], 16)
            load_z(0)
            load_z(1)
            load_z(2)
            with nc.allow_non_contiguous_dma(reason="per-channel vectors"):
                for t, name in ((convb, "conv_b"), (lng, "conv_ln_g"), (lnb, "conv_ln_b"), (pscale, "pool_scale")):
                    sp.dma_start(t, A[name][0].rearrange("(c p) -> p c", p=P)).then_inc(s["chan_in"], 16)
                for c in range(2):
                    sp.dma_start(convw[:, c, :], A["conv_dw"][0].rearrange("k (c p) -> c p k", p=P)[c]
                                 ).then_inc(s["chan_in"], 16)
            for i in range(2, NT + 1):
                sp.wait_ge(s["xn_done"], i - 1)
                load_x(xring[:, i % 2], i).then_inc(s[f"x_in{i % 2}"], 16)
            sp.dma_start(kvw[:, :, :], w_in[:, :, OFF_KV:]).then_inc(s["kvw_in"], 16)
            sp.wait_ge(s["pzero"], 1)
            for g in range(4):
                r = slice(HD * (g % 2), HD * (g % 2) + HD)
                sp.dma_start(poolbd[r, g // 2, r], A["pool_w"][0, g]).then_inc(s["poolw_in"], 16)
            sp.dma_start(tri[:, :], A["c_tri"]).then_inc(s["tri_in"], 16)
            sp.wait_ge(s["fvec_out"], 16)
            band = bass.AP(tensor=scratch, offset=P - 1, ap=[[BAND - 1, P], [P * BAND, NH], [1, 2 * P]])
            sp.dma_start(btab[:, :, :], band).then_inc(s["btab_in"], 16)
            for m in range(3, NZ):
                load_z(m)

            sp.wait_ge(s["mix_done"], 4)
            sp.wait_ge(s["stores"], 16 * STORES_E)
            sp.dma_start(posr[:, 0, 0:HD], A["cmp_pe_k"][0]).then_inc(s["posr_in"], 16)
            sp.dma_start(posr[:, 0, HD:P], A["cmp_pe_k"][0]).then_inc(s["posr_in"], 16)
            sp.dma_start(posr[:, 1, 0:HD], A["cmp_pe_v"][0]).then_inc(s["posr_in"], 16)
            sp.dma_start(posr[:, 1, HD:P], A["cmp_pe_v"][0]).then_inc(s["posr_in"], 16)
            for b in range(NB):
                for n in range(NPG):
                    k = sp.value_load(A["page_table"][b:b + 1, n:n + 1], min_val=0, max_val=NPHYS - 1)
                    sp.dma_start(pages[:, b, n, :], A["cache_cmp_kv"][0].rearrange("f p a g d -> f p (a g d)")[
                        bass.ds(k, 1), :, :].rearrange("f p n -> (f p) n")).then_inc(cpage[b], 16)
            sp.wait_ge(s["late_zero"], 2)
            for q in range(8):
                kv, l0 = q // 4, 8 * (q % 4)
                if q >= 2:
                    sp.wait_ge(s["cmpw_used"], q - 1)
                w = A["cmp_wv" if kv else "cmp_wk"][0, l0:l0 + 8].rearrange("l d e -> d l e")
                for g in range(KVH):
                    r = slice(HD * g, HD * g + HD)
                    sp.dma_start(cmpw[r, q % 2, :, r], w).then_inc(s[f"cmpw_in{q % 2}"], 16)
            for pj in range(4):
                G, br = pj // 2, 1 + pj % 2
                if pj < 2:
                    sp.wait_ge(s["turn_fill"], UNIT[("cp", 4 * pj + 3, 1)] + 1)
                else:
                    sp.wait_ge(s["probT_used"], PUNIT[("P", br, 0)] + 1)
                for b in range(4):
                    slot = pages[:, 4 * (pj % 2) + b]
                    if br == 1:
                        for n in range(NPG):
                            k = sp.value_load(A["page_table"][4 * G + b:4 * G + b + 1, n:n + 1], min_val=0, max_val=NPHYS - 1)
                            sp.dma_start(slot[:, n, :], A["cache_slc_kv"][0].rearrange("f p a g d -> f p (a g d)")[
                                bass.ds(k, 1), :, :].rearrange("f p n -> (f p) n")).then_inc(s["page_in0"], 16)
                    else:
                        sp.dma_start(slot[:, :, :], A["cache_win_kv"][0, 4 * G + b].rearrange(
                            "(n p) a g d -> p n (a g d)", p=PAGE)).then_inc(s["page_in1"], 16)

            sp.wait_ge(s["turn_drain"], len(UNIT))
            sp.wait_ge(s["stores"], 16 * STORES_M)
            for i in range(NT + 1):
                load_x(xt[:, i, :], i).then_inc(s["x2_in"], 16)
            sp.dma_start(gB[:, :], A["norm2"].to_broadcast([P, D])).then_inc(s["gain2_in"], 16)

            def load_back(mg, nk, src):
                slot = bw[:, mg % 3]
                if mg >= 3:
                    sp.wait_ge(s["back_mm"], mg - 2)
                if nk == FT:
                    sp.dma_start(slot, src).then_inc(s[f"back_in{mg % 3}"], 48)
                else:
                    cols = slice(P * mg, P * mg + P)
                    sp.dma_start(slot[:, 0:4, :], A["w_out"][0, 0:512, cols].rearrange("(k p) n -> p k n", p=P)
                                 ).then_inc(s[f"back_in{mg % 3}"], 16)
                    for g in range(KVH):
                        rows = 512 + GQ * HD * g
                        sp.dma_start(slot[HD * g:HD * g + HD, 4:8, :], A["w_out"][0, rows:rows + GQ * HD, cols].rearrange(
                            "(r d) n -> d r n", d=HD)).then_inc(s[f"back_in{mg % 3}"], 16)

            for m in range(KD):
                load_back(m, KD, None)
            w_gu = A["w_gu"][0].rearrange("(k p) n -> p k n", p=P)
            for f in range(NF):
                for j in range(FT):
                    ft = FT * f + j
                    if ft >= 2:
                        sp.wait_ge(s["gu_mm"], 3 * (ft - 1))
                    for side in range(2):
                        c = side * DFF + P * ft
                        sp.dma_start(guw[:, ft % 2, side], w_gu[:, :, c:c + P]).then_inc(s[f"gu_in{ft % 2}"], 16)
                for m in range(KD):
                    rows = A["w_down"][0, P * FT * f:P * FT * (f + 1), P * m:P * m + P]
                    load_back(KD * (f + 1) + m, FT, rows.rearrange("(k p) n -> p k n", p=P))
            sp.wait_ge(s["sq3"], 0 + NT + 1)
            sp.wait_ge(s["xn3"], NT + 1)
            sp.dma_start(gB[:, :], A["final_norm"][None, :].to_broadcast([P, D])).then_inc(s["gain3_in"], 16)
            for i in range(NT + 1):
                sp.wait_ge(s["y_done"], i + 1)
                n = tile_rows(i)
                dst = out["y_prompt"][0, P * i:P * i + P, :] if i < NT else out["y_sample"].rearrange("b t d -> (b t) d")
                sp.dma_start(dst, xn2[0:n, i % 2, :]).then_inc(s[f"y_out{i % 2}"], 16)
            sp.wait_ge(s["y_out0"], 16 * (NT // 2 + 1))
            sp.wait_ge(s["y_out1"], 16 * (NT // 2))
            sp.wait_ge(s["stores"], 16 * STORES)

        @block.tensor
        def _(pe):
            def turn_tile(dst, src, n):
                return pe.transpose(dst, src, ident[0:n, 0:n])

            pe.wait_ge(s["const_in"], 16)
            pe.wait_ge(s["table_in"], 16 * 6)
            pe.wait_ge(s["prep"], 1)
            pe.matmul(bank[0][0:NH, 0:BAND], rbias, distt[:, ND:ND + BAND], start=True, stop=True).then_inc(s["table_mm"], 1)
            for c in range(CMPN):
                at = -(CBLK - 1) - STRIDE * (c - 8) - DLO
                mm = pe.matmul(bank[1][:, NH * c:NH * c + NH], distt[:, at:at + P], rbias, start=True, stop=True)
            mm.then_inc(s["table_mm"], 1)
            pe.wait_ge(s["tsel_done"], 1)
            pe.matmul(bank[2][:, 0:288], tsel, cpk[:, C_OH:C_OH + 288], start=True, stop=True).then_inc(s["table_mm"], 1)
            pe.wait_ge(s["state_in"], 48)
            for k in range(2):
                for c in range(2):
                    q = 2 * k + c
                    turn_tile(bank[6][:, 120 * q:120 * q + 120], stin[0:120, k, P * c:P * c + P], 120)
            for c in range(2):
                mm = turn_tile(bank[7][:, 120 * c:120 * c + 120], stin[0:120, 2, P * c:P * c + P], 120)
            mm.then_inc(s["state_turn"], 1)
            pe.wait_ge(s["table_ev"], 2)
            pe.wait_ge(s["fvec_ev"], 1)

            def turn_norm(xs, done, filled, eva, evd):
                for i in range(NT + 1):
                    n = tile_rows(i)
                    pe.wait_ge(s[done], i + 1)
                    if i >= 2:
                        pe.wait_ge(s[eva], i - 1)
                        pe.wait_ge(s[evd], i - 1)
                    for k in range(KD):
                        b = bank[2 * (i % 2) + k // 4]
                        mm = turn_tile(b[:, P * (k % 4):P * (k % 4) + n], xs[i % 2][0:n, P * k:P * k + P], n)
                    mm.then_inc(s[filled], 1)

            turn_norm(xn, "xn_done", "turn_x", "evac_xa", "evac_xd")
            pe.wait_ge(s["evac_xa"], NT + 1)
            pe.wait_ge(s["evac_xd"], NT + 1)
            for m in range(NZ):
                pe.wait_ge(s[f"w_in{m % 3}"], 32 * (m // 3 + 1))
                if m >= 2:
                    p = m - 2
                    if p < 4:
                        pe.wait_ge(s["glu_done" if p % 2 else "sig_done"], p // 2 + 1)
                    else:
                        pe.wait_ge(s["zc_done"], p - 3)
                for n, (at, w) in enumerate(chunks):
                    for k in range(KD):
                        mm = pe.matmul(bank[3 * (m % 2) + n][:, 0:w], wring[:, m % 3, k, :], featT[:, k, at:at + w],
                                       start=(k == 0), stop=(k == KD - 1))
                mm.then_inc(s["z_mm"], 1)
            pe.wait_ge(s["kvw_in"], 16)
            pe.wait_ge(s["zc_done"], NZ - 4)
            hk = KVG // 2
            for i in range(NT + 1):
                n = tile_rows(i)
                if i >= 3:
                    pe.wait_ge(s["kv_ev"], i - 2)
                for hf in range(2):
                    for k in range(KD):
                        mm = pe.matmul(bank[2 * (i % 3) + hf][0:n, 0:hk], featT[:, k, P * i:P * i + n],
                                       kvw[:, k, hk * hf:hk * hf + hk], start=(k == 0), stop=(k == KD - 1))
                mm.then_inc(s["kv_mm"], 1)
            pe.wait_ge(s["state_ev"], 2)
            pe.wait_ge(s["newcols_done"], 1)
            for c in range(2):
                turn_tile(bank[6][0:30, P * c:P * c + P], glu[:, c, T:CB + T], P)
                turn_tile(bank[6][0:15, 256 + P * c:256 + P * c + P], uex[:, c, T:PB + T], P)
            for c in range(2):
                turn_tile(bank[7][0:TS, P * c:P * c + P], newcols[:, c, :], P)
                mm = turn_tile(bank[7][0:TS, 256 + P * c:256 + P * c + P], newcols[:, 2 + c, :], P)
            mm.then_inc(s["last_turn"], 1)
            pe.wait_ge(s["kv_ev"], NT + 1)
            pe.wait_ge(s["conv_done"], 1)
            for n, (at, w) in enumerate(lnchunks):
                for c in range(2):
                    y = ybuf[:, c, at:at + w] if at < T else smp(ybuf[:, c, :], CB + T, GE, 0, NS)
                    mm = pe.matmul(bank[n][:, 0:w], avg[:, :], y, start=(c == 0), stop=(c == 1))
            mm.then_inc(s["mean_mm"], 1)
            pe.wait_ge(s["sq2_done"], 1)
            for n, (at, w) in enumerate(lnchunks):
                for c in range(2):
                    mm = pe.matmul(bank[3 + n][:, 0:w], avg[:, :], ysq[:, c, at:at + w], start=(c == 0), stop=(c == 1))
            mm.then_inc(s["var_mm"], 1)
            pe.wait_ge(s["poolw_in"], 64)
            pe.wait_ge(s["pool_d"], 2)
            for c in range(2):
                if c == 0:
                    pe.wait_ge(s["yc_done"], 1)
                else:
                    pe.wait_ge(s["std_done"], 1)
                for n, (at, w) in enumerate(chunks):
                    mm = pe.matmul(bank[3 * c + n][:, 0:w], poolbd[:, c, :], dT[:, c, at:at + w], start=True, stop=True)
                mm.then_inc(s["pool_mm"], 1)

            nturn = [0]

            def turn(key, parts, first=None):
                u = UNIT[key]
                assert u == nturn[0]
                nturn[0] += 1
                if u >= 2:
                    pe.wait_ge(s["turn_drain"], u - 1)
                for at, n, srcap in parts:
                    m = srcap.free_size()
                    mm = turn_tile(bank[4 + u % 2][0:m, at:at + n], srcap, n)
                mm.then_inc(s["turn_fill"], 1)

            pe.wait_ge(s["last_ev"], 1)
            pe.wait_ge(s["mix_done"], 4)
            pe.wait_ge(s["posr_in"], 64)
            for kv in range(2):
                turn(("pe", kv), [(0, 32, posr[:, kv, :])])
            for w in range(2):
                turn(("knew", w), [(0, TS, kvtok[0:TS, NT, 256 * (w + 1):256 * (w + 1) + P])])
            for ty in range(4):
                col = (0, 128, 256, 512)[ty]
                for hf in range(2):
                    turn(("kT", ty, hf), [(P * x, P, kvtok[:, 4 * hf + x, col:col + P]) for x in range(4)])
            for b in range(NB):
                pe.wait_ge(cpage[b], 16 * NPG)
                for kv in range(2):
                    turn(("cp", b, kv), [(P * x, P, pages[:, b, x, P * kv:P * kv + P]) for x in range(NPG)])
            pe.wait_ge(s["turn_drain"], nturn[0])
            for kv in range(2):
                srcT = cvT if kv else ckT
                for l in range(CBLK):
                    q = 4 * kv + l // 8
                    if l % 8 == 0:
                        pe.wait_ge(s[f"cmpw_in{q % 2}"], 32 * (q // 2 + 1))
                    mm = pe.matmul(bank[kv][:, 0:KC_N], cmpw[:, q % 2, l % 8, :],
                                   srcT[:, l:l + STRIDE * (KC_N - 1) + 1:STRIDE], start=(l == 0), stop=(l == CBLK - 1))
                    if l % 8 == 7:
                        mm.then_inc(s["cmpw_used"], 1)
            for G in range(2):
                mm = pe.matmul(bank[2 + G][:, 0:24], cpk[0:TS, C_SEL + P * G:C_SEL + P * G + P], kvtok[0:TS, NT, KVC:KVG],
                               start=True, stop=True)
            mm.then_inc(s["gate_mm"], 1)
            pe.wait_ge(s["cmp_ev"], 2)
            turn(("vc", 0), [(0, P, vcT[:, NB * 32:NB * 32 + NCMP])])
            for G in range(2):
                turn(("vc", 1 + G), [(0, P, vcT[:, P * G:P * G + P])])
            pe.wait_ge(s["turn_drain"], nturn[0])
            pe.wait_ge(s["gate_ev"], 1)
            pe.wait_ge(s["qbd_done"], 1)

            def score(j):
                kind, i, h, br = JOBS[j]
                sc = scores[j % 2]
                if j >= 2:
                    pe.wait_ge(s["exp_done"], j - 1)
                if kind == "s" and br == 0:
                    mm = pe.matmul(sc[:, 0:P], qbd[:, i, :], kcT[:, P * i:P * i + P], start=True, stop=True)
                elif kind == "s":
                    pj = 2 * i + br - 1
                    pe.wait_ge(s[f"page_in{br - 1}"], (i + 1) * (256 if br == 1 else 64))
                    for b in range(5):
                        if b < 4:
                            turn(("kp", j, b), [(P * x, P, pages[:, 4 * (pj % 2) + b, x, 0:P]) for x in range(NPG)])
                        if b >= 1:
                            kb = KUNIT[("kp", j, b - 1)]
                            pe.wait_ge(s["turn_drain"], UNIT[("kp", j, b - 1)] + 1)
                            r = slice(32 * (b - 1), 32 * b)
                            pe.matmul(sc[r, 0:PAST], qbd[:, i, r], kpT[kb % 2], start=True, stop=True
                                      ).then_inc(s["keys_used"], 1)
                            mm = pe.matmul(sc[r, PAST:PAST + TS], qbd[:, i, r], knewT[:, br - 1, :], start=True, stop=True)
                else:
                    g, r = h // GQ, h % GQ
                    gp = slice(HD * g, HD * g + HD)
                    w = job_width(JOBS[j])
                    keys = kcT[gp, NB * 32:NB * 32 + w] if br == 0 else kslcT[gp, 0:w] if br == 1 else \
                        kwinT[gp, P * (i + 1) - w:P * (i + 1)]
                    for c in range(0, w, 512):
                        mm = pe.matmul(sc[:, c:min(w, c + 512)], qT[gp, r, P * i:P * i + P], keys[:, c:min(w, c + 512)],
                                       start=True, stop=True)
                mm.then_inc(s["score_mm"], 1)

            def values(j, k):
                kind, i, h, br = JOBS[j]
                pair = j // 3
                grp = job_groups(JOBS[j])
                pt = probT[PUNIT[("P", j, k)] % 2]
                o = bank[6 + pair % 2]
                pe.wait_ge(s["turn_drain"], UNIT[("P", j, k)] + 1)
                if br == 0 and k == 0 and pair >= 2:
                    pe.wait_ge(s["out_done"], pair - 1)
                last = k == len(grp) - 1
                if kind == "s" and br == 0:
                    mm = pe.matmul(o[:, 0:P], pt[:, 0:P], vctok[:, 1 + i, :], start=True, stop=True)
                elif kind == "s":
                    for b in range(4):
                        r = slice(32 * b, 32 * b + 32)
                        ob = o[r, P * br:P * br + P]
                        if k == 0:
                            slot = 4 * ((2 * i + br - 1) % 2) + b
                            for x in range(NPG):
                                mm = pe.matmul(ob, pt[:, P * x + 32 * b:P * x + 32 * b + 32], pages[:, slot, x, P:2 * P],
                                               start=(x == 0), stop=False)
                        else:
                            c = 256 * br + P
                            mm = pe.matmul(ob, pt[0:TS, 32 * b:32 * b + 32], kvtok[0:TS, NT, c:c + P],
                                           start=False, stop=True)
                else:
                    g = h // GQ
                    for x, (c, n) in enumerate(grp[k]):
                        if br == 0:
                            v = vctok[0:n, 0, HD * g:HD * g + HD]
                        else:
                            kt = c // P if br == 1 else i + 1 - job_width(JOBS[j]) // P + c // P
                            vc = 256 * br + P + HD * g
                            v = kvtok[:, kt, vc:vc + HD]
                        mm = pe.matmul(o[:, HD * br:HD * br + HD], pt[0:n, P * x:P * x + P], v,
                                       start=(c == 0), stop=(last and x == len(grp[k]) - 1))
                mm.then_inc(s["probT_used"], 1)
                if last and br == 2:
                    return True
                return False

            def turn_out(o):
                pe.wait_ge(s["out_done"], 1 + o if o < 2 else 2 + NH * (o - 1))
                src = [osmp[o]] if o < 2 else [oacc[o % 2][:, P * r:P * r + P] for r in range(GQ)]
                turn(("o", o), [(P * x, P, t) for x, t in enumerate(src)])

            pend = []
            for j in range(-2, NJ):
                if j + 2 < NJ:
                    score(j + 2)
                if j < 0:
                    continue
                pe.wait_ge(s["exp_done"], j + 1)
                for k, grp in enumerate(job_groups(JOBS[j])):
                    turn(("P", j, k), [(P * x, P, prob[j % 2][:, c:c + n]) for x, (c, n) in enumerate(grp)])
                    if pend:
                        values(*pend.pop())
                    pend.append((j, k))
                if pair_out(j) is not None:
                    turn_out(pair_out(j))
            values(*pend.pop())
            turn_out(NT + 1)
            pe.wait_ge(s["turn_drain"], len(UNIT))

            def back(call, nk, rhs):
                for m in range(KD + 1):
                    mg = KD * call + m
                    if m < KD:
                        pe.wait_ge(s[f"back_in{mg % 3}"], 48 * (mg // 3 + 1))
                        if mg >= 2:
                            pe.wait_ge(s["back_ev"], mg - 1)
                        for n, (at, w) in enumerate(chunks):
                            for k in range(nk):
                                mm = pe.matmul(bank[3 * (mg % 2) + n][:, 0:w], bw[:, mg % 3, k, :], rhs[:, k, at:at + w],
                                               start=(k == 0), stop=(k == nk - 1))
                        mm.then_inc(s["back_mm"], 1)
                    if m >= 1:
                        mt = mg - 1
                        pe.wait_ge(s["back_ev"], mt + 1)
                        for q in range(3):
                            u = 3 * mt + q
                            if u >= 2:
                                pe.wait_ge(s["x_add"], u - 1)
                            for x in range(3):
                                i = 3 * q + x
                                n = tile_rows(i)
                                mm = turn_tile(bank[6 + u % 2][0:n, P * x:P * x + P], backT[:, mt % 2, P * i:P * i + n], P)
                            mm.then_inc(s["backT_turn"], 1)

            back(0, KD, featT)
            turn_norm([xn2[:, 0, :], xn2[:, 1, :]], "xn3", "turn3", "evac3a", "evac3d")
            pe.wait_ge(s["evac3a"], NT + 1)
            pe.wait_ge(s["evac3d"], NT + 1)
            for f in range(NF):
                for jt in range(FT):
                    ft = FT * f + jt
                    pe.wait_ge(s[f"gu_in{ft % 2}"], 32 * (ft // 2 + 1))
                    for n, (at, w) in enumerate(chunks):
                        u = 3 * ft + n
                        if jt >= 1:
                            pe.wait_ge(s["act_done"], u - 2)
                        for side in range(2):
                            for k in range(KD):
                                mm = pe.matmul(bank[2 * n + side][:, 0:w], guw[:, ft % 2, side, k, :],
                                               featT[:, k, at:at + w], start=(k == 0), stop=(k == KD - 1))
                        mm.then_inc(s["gu_mm"], 1)
                pe.wait_ge(s["act_done"], 3 * FT * (f + 1))
                back(1 + f, FT, act)
                if f + 1 < NF:
                    pe.wait_ge(s["back_ev"], KD * (f + 2))

        @block.scalar
        def _(sc_):
            for i in range(NT + 1):
                n = tile_rows(i)
                sc_.wait_ge(s[f"x_in{i % 2}"], 16 * (i // 2 + 1))
                if i >= 1:
                    sc_.wait_ge(s["sq_done"], i)
                sc_.activation(sqjunk[0:n, :], xring[0:n, i % 2, :], ACT.Square, accum_out=stat[0:n, i:i + 1]
                               ).then_inc(s["sq_done"], 1)
                if i >= 1:
                    p = i - 1
                    sc_.wait_ge(s["turn_x"], p + 1)
                    sc_.copy(featT[:, 0:4, P * p:P * p + P], bank[2 * (p % 2)].rearrange("p (k t) -> p k t", k=4)
                             ).then_inc(s["evac_xa"], 1)
            sc_.wait_ge(s["turn_x"], NT + 1)
            sc_.copy(featT[:, 0:4, T:TT], bank[2 * (NT % 2)].rearrange("p (k t) -> p k t", k=4)[:, :, 0:TS]
                     ).then_inc(s["evac_xa"], 1)
            for m in range(NZ):
                if m in (1, 3):
                    continue
                sc_.wait_ge(s["z_mm"], m + 1)
                if m == 2:
                    sc_.wait_ge(s["glu_done"], 1)
                for n, (at, w) in enumerate(chunks):
                    b = bank[3 * (m % 2) + n]
                    if m in (0, 2):
                        op = sc_.activation(sig[:, at:at + w], b[:, 0:w], ACT.Sigmoid)
                    elif m < len(ZTILES):
                        for lo, hi, dst in ext_cols(uex, m - 4, at, w, PB, UE, PB):
                            srcap = b[:, lo:hi]
                            if lo:
                                srcap = srcap.rearrange("p (b t) -> p b t", t=NS)
                            op = sc_.copy(dst, srcap)
                    else:
                        op = sc_.mul(qT[:, m - len(ZTILES), at:at + w], b[:, 0:w], HD ** -0.5)
                op.then_inc(s["sig_done" if m in (0, 2) else "zc_done"], 1)
            hk = KVG // 2
            for i in range(NT + 1):
                n = tile_rows(i)
                sc_.wait_ge(s["kv_mm"], i + 1)
                for hf in range(2):
                    op = sc_.copy(kvtok[0:n, i, hk * hf:hk * hf + hk], bank[2 * (i % 3) + hf][0:n, 0:hk])
                op.then_inc(s["kv_ev"], 1)
            sc_.wait_ge(s["kv_ev"], NT + 1)
            sc_.activation(kvtok[:, 0:NT, KVC:KVG], kvtok[:, 0:NT, KVC:KVG], ACT.Sigmoid).then_inc(s["gates_done"], 1)
            sc_.activation(kvtok[0:TS, NT, KVC:KVG], kvtok[0:TS, NT, KVC:KVG], ACT.Sigmoid).then_inc(s["gates_done"], 1)
            sc_.wait_ge(s["yc_done"], 1)
            for c in range(2):
                op = sc_.activation(ysq[:, c, :], yc[:, c, :], ACT.Square)
            op.then_inc(s["sq2_done"], 1)
            sc_.wait_ge(s["var_mm"], 1)
            sc_.wait_ge(s["prep"], 1)
            for n, (at, w) in enumerate(lnchunks):
                op = sc_.activation(ystd[:, at:at + w], bank[3 + n][:, 0:w], ACT.Sqrt, bias=epsc)
            op.then_inc(s["std_done"], 1)
            sc_.wait_ge(s["norm_done"], 2)
            sc_.wait_ge(s["chan_in"], 96)
            for c in range(2):
                sc_.activation(featT[:, c, :], yc[:, c, :], ACT.Silu, bias=lnb[:, c:c + 1], scale=lng[:, c:c + 1]
                               ).then_inc(s["mix_done"], 1)
            for c in range(2):
                sc_.wait_ge(s["pool_mm"], c + 1)
                for n, (at, w) in enumerate(chunks):
                    op = sc_.activation(featT[:, 2 + c, at:at + w], bank[3 * c + n][:, 0:w], ACT.Copy,
                                        scale=pscale[:, c:c + 1])
                op.then_inc(s["mix_done"], 1)

            nturn = [0]

            def drain(key, copies):
                u = UNIT[key]
                assert u == nturn[0]
                nturn[0] += 1
                sc_.wait_ge(s["turn_fill"], u + 1)
                for dst, srcfn in copies:
                    op = sc_.copy(dst, srcfn(bank[4 + u % 2]))
                op.then_inc(s["turn_drain"], 1)

            sc_.wait_ge(s["mix_done"], 4)
            sc_.wait_ge(s["stores"], 16 * STORES_E)
            for kv in range(2):
                drain(("pe", kv), [((cvT if kv else ckT)[:, KC_L - 32:KC_L], lambda b: b[:, 0:32])])
            for w in range(2):
                drain(("knew", w), [(knewT[:, w, :], lambda b: b[:, 0:TS])])
            for ty in range(4):
                for hf in range(2):
                    dst = (ckT[:, NB * PAST:], cvT[:, NB * PAST:], kslcT, kwinT)[ty]
                    drain(("kT", ty, hf), [(dst[:, 512 * hf:512 * hf + 512], lambda b: b)])
            for b_ in range(NB):
                for kv in range(2):
                    drain(("cp", b_, kv), [((cvT if kv else ckT)[:, PAST * b_:PAST * b_ + PAST], lambda b: b)])
            drain(("vc", 0), [(vctok[0:NCMP, 0, :], lambda b: b[0:NCMP, 0:P])])
            for G in range(2):
                drain(("vc", 1 + G), [(vctok[:, 1 + G, :], lambda b: b[:, 0:P])])

            def drain_keys(j):
                for b_ in range(4):
                    kb = KUNIT[("kp", j, b_)]
                    if kb >= 2:
                        sc_.wait_ge(s["keys_used"], kb - 1)
                    drain(("kp", j, b_), [(kpT[kb % 2], lambda b: b)])

            def drain_prob(j, k):
                pu = PUNIT[("P", j, k)]
                if pu >= 2:
                    sc_.wait_ge(s["probT_used"], pu - 1)
                grp = job_groups(JOBS[j])[k]
                n, w = grp[0][1], P * len(grp)
                if grp[-1][1] < n:
                    n = P
                drain(("P", j, k), [(probT[pu % 2][0:n, 0:w], lambda b: b[0:n, 0:w])])

            def expo(j):
                w = job_width(JOBS[j])
                pair, br = j // 3, j % 3
                sc_.wait_ge(s["score_in"], j + 1)
                if j >= 2:
                    last = ("P", j - 2, len(job_groups(JOBS[j - 2])) - 1)
                    sc_.wait_ge(s["turn_fill"], UNIT[last] + 1)
                if pair >= 2 and br == 0:
                    sc_.wait_ge(s["out_done"], pair - 1)
                sc_.activation(prob[j % 2][:, 0:w], scores[j % 2][:, 0:w], ACT.Exp, bias=nmax[:, j % 2:j % 2 + 1],
                               accum_out=sums[pair % 2][:, br:br + 1]).then_inc(s["exp_done"], 1)

            def drain_out(o):
                if o < 2:
                    copies = []
                    for g in range(KVH):
                        gp = slice(HD * g, HD * g + HD)
                        dst = featT[gp, 4:8, T + 16 * o:T + 16 * o + 16].rearrange("p r (b t) -> p b r t", t=NS)
                        copies.append((dst, lambda b, gp=gp, g=g: b[gp, 0:P].rearrange(
                            "p (b g r t) -> p b g r t", b=4, g=KVH, r=GQ)[:, :, g]))
                    drain(("o", o), copies)
                else:
                    i = o - 2
                    drain(("o", o), [(featT[:, 4:8, P * i:P * i + P], lambda b: b.rearrange("p (r t) -> p r t", r=GQ))])

            for j in range(-2, NJ):
                if j + 2 < NJ and JOBS[j + 2][0] == "s" and JOBS[j + 2][3] > 0:
                    drain_keys(j + 2)
                if j < 0:
                    if j == -1:
                        expo(0)
                    continue
                for k in range(len(job_groups(JOBS[j]))):
                    drain_prob(j, k)
                    if k == 0 and j + 1 < NJ:
                        expo(j + 1)
                if pair_out(j) is not None:
                    drain_out(pair_out(j))
            drain_out(NT + 1)

            def back(call):
                for m in range(KD):
                    mg = KD * call + m
                    sc_.wait_ge(s["back_mm"], mg + 1)
                    if mg >= 2:
                        sc_.wait_ge(s["backT_turn"], 3 * (mg - 1))
                    for n, (at, w) in enumerate(chunks):
                        op = sc_.copy(backT[:, mg % 2, at:at + w], bank[3 * (mg % 2) + n][:, 0:w])
                    op.then_inc(s["back_ev"], 1)

            def squares(base, sem_):
                sc_.wait_ge(s["x_add"], 3 * KD * base)
                for i in range(NT + 1):
                    n = tile_rows(i)
                    at = (NT + 1) * (base > 1) + i
                    if at:
                        sc_.wait_ge(s[sem_], at)
                    sc_.activation(backT[0:n, 0, 0:D], xt[0:n, i, :], ACT.Square, accum_out=stat[0:n, i:i + 1]
                                   ).then_inc(s[sem_], 1)

            sc_.wait_ge(s["stores"], 16 * STORES_M)
            back(0)
            squares(1, "sq3")
            for i in range(NT + 1):
                n = tile_rows(i)
                sc_.wait_ge(s["turn3"], i + 1)
                sc_.copy(featT[:, 0:4, P * i:P * i + n], bank[2 * (i % 2)].rearrange("p (k t) -> p k t", k=4)[:, :, 0:n]
                         ).then_inc(s["evac3a"], 1)
            for f in range(NF):
                for u in range(3 * FT * f, 3 * FT * (f + 1)):
                    sc_.wait_ge(s["gu_mm"], u + 1)
                    if u >= 3:
                        sc_.wait_ge(s["act_done"], u - 2)
                    sc_.activation(silu[:, u % 3, :], bank[2 * (u % 3)][:, 0:NCH], ACT.Silu).then_inc(s["silu_done"], 1)
                back(1 + f)
            squares(3, "sq3")

        @block.vector
        def _(dve):
            chain = [0]

            def link(op):
                chain[0] += 1
                op.then_inc(s["dve"], 1)
                dve.wait_ge(s["dve"], chain[0])

            dve.memset(mhalf, -0.5)
            dve.memset(epsc, EPS)
            dve.memset(avg[:, :], 1.0 / CONV_W)
            dve.memset(rbias[32:33, :], 1.0).then_inc(s["prep"], 1)
            dve.wait_ge(s["table_mm"], 1)
            dve.tensor_copy(fvec, bank[0][0:NH, 0:BAND]).then_inc(s["fvec_ev"], 1)
            dve.wait_ge(s["table_mm"], 2)
            dve.tensor_copy(ctab[:, :, :], bank[1][:, 0:CMPN * NH].rearrange("p (c h) -> p h c", h=NH)
                            ).then_inc(s["table_ev"], 1)
            dve.wait_ge(s["table_mm"], 3)
            dve.tensor_copy(stab[:, 0:128], bank[2][:, 0:128])
            for G in range(2):
                dve.tensor_tensor(stab[:, 128 + 32 * G:160 + 32 * G], bank[2][:, 128:160],
                                  cpk[:, C_MN + 32 * G:C_MN + 32 * G + 32], ALU.add)
            dve.tensor_tensor(stab[:, 192:320], bank[2][:, 160:288], cpk[:, C_MC:C_MC + 128], ALU.add
                              ).then_inc(s["table_ev"], 1)
            dve.wait_ge(s["state_turn"], 1)
            for c in range(2):
                for k in range(2):
                    dst = smp(glu[:, c, :], CB + T, GE, 0, CB)[:, 4 * k:4 * k + 4]
                    q = 120 * (2 * k + c)
                    op = dve.tensor_copy(dst, bank[6][:, q:q + 120].rearrange("p (b t) -> p b t", t=CB))
            op.then_inc(s["state_ev"], 1)
            for c in range(2):
                op = dve.tensor_copy(smp(uex[:, c, :], PB + T, UE, 0, PB), bank[7][:, 120 * c:120 * c + 120].rearrange(
                    "p (b t) -> p b t", t=PB))
            op.then_inc(s["state_ev"], 1)

            def norm(xs, outs, sq_, ms_, rs_, xn_, filled, evd, gain, base, free):
                for i in range(NT + 2):
                    n = tile_rows(i)
                    if i <= NT:
                        dve.wait_ge(s[sq_], base + i + 1)
                        dve.tensor_scalar(ms[0:n, i:i + 1], stat[0:n, i:i + 1], 1.0 / D, EPS, ALU.mult, ALU.add
                                          ).then_inc(s[ms_], 1)
                    if i >= 1 and filled:
                        p, n1 = i - 1, tile_rows(i - 1)
                        dve.wait_ge(s[filled], p + 1)
                        dve.tensor_copy(featT[:, 4:8, P * p:P * p + n1],
                                        bank[2 * (p % 2) + 1].rearrange("p (k t) -> p k t", k=4)[:, :, 0:n1]
                                        ).then_inc(s[evd], 1)
                    if i <= NT:
                        dve.wait_ge(s[rs_], base + i + 1)
                        if i == 0:
                            dve.wait_ge(s[gain], 16)
                        free(i)
                        dve.scalar_tensor_tensor(out=outs[i % 2][0:n, :], in0=xs(i)[0:n, :], scalar=rstd[0:n, i:i + 1],
                                                 in1=gB[0:n, :], op0=ALU.mult, op1=ALU.mult).then_inc(s[xn_], 1)

            norm(lambda i: xring[:, i % 2, :], xn, "sq_done", "ms_done", "rstd_done", "xn_done", "turn_x", "evac_xd",
                 "gain_in", 0, lambda i: dve.wait_ge(s["turn_x"], i - 1) if i >= 2 else None)
            for c in range(2):
                dve.wait_ge(s["sig_done"], c + 1)
                dve.wait_ge(s["z_mm"], 2 * c + 2)
                for n, (at, w) in enumerate(chunks):
                    for lo, hi, dst in ext_cols(glu, c, at, w, CB, GE, CB):
                        a, b = bank[3 + n][:, lo:hi], sig[:, at + lo:at + hi]
                        if lo:
                            a, b = (v.rearrange("p (b t) -> p b t", t=NS) for v in (a, b))
                        op = dve.tensor_tensor(dst, a, b, ALU.mult)
                op.then_inc(s["glu_done"], 1)
            dve.wait_ge(s["glu_done"], 2)
            dve.wait_ge(s["chan_in"], 96)
            dve.wait_ge(s["pzero"], 1)
            dve.wait_ge(s["turn_x"], NT + 1)
            for k in range(CW):
                for c in range(2):
                    y, x, w = ybuf[:, c, 0:Y_L], glu[:, c, k:k + Y_L], convw[:, c, k:k + 1]
                    if k == 0:
                        op = dve.tensor_scalar(y, x, w, convb[:, c:c + 1], ALU.mult, ALU.add)
                    else:
                        dve.wait_ge(s["dve"], chain[0] - 1)
                        op = dve.scalar_tensor_tensor(out=y, in0=x, scalar=w, in1=y, op0=ALU.mult, op1=ALU.add)
                    chain[0] += 1
                    op.then_inc(s["dve"], 1)
            dve.wait_ge(s["dve"], chain[0])
            for c in range(2):
                dve.wait_ge(s["pairsum"], c + 1)
                for hp in range(2):
                    r = slice(HD * hp, HD * hp + HD)
                    S = pl[r, hp, :]
                    link(dve.tensor_tensor(S[:, PB:2 * PB], S[:, PB:2 * PB], cpk[r, C_FX + PB * c:C_FX + PB * c + PB], ALU.mult))
                    dve.scalar_tensor_tensor(out=dT[r, c, 0:T], in0=S[:, PB:PB + T], scalar=cpk[r, C_IW + c:C_IW + c + 1],
                                             in1=uex[r, c, PB:PB + T], op0=ALU.mult, op1=ALU.subtract)
                    op = dve.scalar_tensor_tensor(
                        out=dT[r, c, T:TT].rearrange("p (b t) -> p b t", t=NS), in0=smp(S, PB + T, UE, PB, NS),
                        scalar=cpk[r, C_IW + c:C_IW + c + 1], in1=smp(uex[r, c, :], PB + T, UE, PB, NS),
                        op0=ALU.mult, op1=ALU.subtract)
                op.then_inc(s["pool_d"], 1)
            dve.engine_nop().then_inc(s["conv_done"], 1)
            dve.wait_ge(s["last_turn"], 1)
            dve.wait_ge(s["state_turn"], 1)
            dve.tensor_copy(lastT[0:30, 0, :], bank[6][0:30, 0:256])
            dve.tensor_copy(lastT[0:15, 1, :], bank[6][0:15, 256:512])
            dve.tensor_copy(lastT[:, 2:4, :], bank[7][0:TS, :].rearrange("p (k n) -> p k n", k=2)).then_inc(s["last_ev"], 1)
            dve.wait_ge(s["gates_done"], 1)
            dve.tensor_scalar(kvtok[:, 0, KVC:KVC + NH], kvtok[:, 0, KVC:KVC + NH], cpk[:, C_VA:C_VA + 1], None, ALU.mult
                              ).then_inc(s["valid_done"], 1)
            dve.wait_ge(s["mean_mm"], 1)
            for n, (at, w) in enumerate(lnchunks):
                for c in range(2):
                    y, b, o = ybuf[:, c, at:at + w], bank[n][:, 0:w], yc[:, c, at:at + w]
                    if at == T:
                        y = smp(ybuf[:, c, :], CB + T, GE, 0, NS)
                        b, o = (v.rearrange("p (b t) -> p b t", t=NS) for v in (b, o))
                    op = dve.tensor_tensor(o, y, b, ALU.subtract)
            op.then_inc(s["yc_done"], 1)
            dve.wait_ge(s["std_done"], 1)
            link(dve.reciprocal(ystd, ystd))
            for c in range(2):
                dve.tensor_tensor(yc[:, c, :], yc[:, c, :], ystd, ALU.mult).then_inc(s["norm_done"], 1)

            for kv, dst in ((0, kcT), (1, vcT)):
                dve.wait_ge(s["cmpw_used"], 4 * (kv + 1))
                if kv == 0:
                    dve.wait_ge(s["late_zero"], 2)
                link(dve.tensor_copy(posk[:, kv:kv + 1], bank[kv][:, KC_N - 1:KC_N]))
                dve.tensor_scalar(dst[:, :], bank[kv][:, 0:KC_N - 1], posk[:, kv:kv + 1], None, ALU.add
                                  ).then_inc(s["cmp_ev"], 1)
            dve.wait_ge(s["gate_mm"], 1)
            for G in range(2):
                link(dve.tensor_tensor(gjunk[:, 24 * G:24 * G + 24], bank[2 + G][:, 0:24], cpk[:, C_GM:C_GM + 24], ALU.mult))
                op = dve.tensor_reduce(sgate[:, 3 * G:3 * G + 3], gjunk[:, 24 * G:24 * G + 24].rearrange(
                    "p (a h) -> p a h", h=NH), AX, ALU.add)
            op.then_inc(s["gate_ev"], 1)
            dve.wait_ge(s["gate_ev"], 1)
            dve.wait_ge(s["btab_in"], 16)
            dve.wait_ge(s["tri_in"], 16)

            def biased_max(j):
                kind, i, h, br = JOBS[j]
                sc, w = scores[j % 2], job_width(JOBS[j])
                dve.wait_ge(s["score_mm"], j + 1)
                adds = []
                if kind == "s" and br == 0:
                    adds.append((0, stab[:, 192:320]))
                elif kind == "s":
                    adds.append((384, stab[:, 0:128]))
                    adds.append((512, stab[:, 128 + 32 * i:160 + 32 * i]))
                    if br == 2:
                        adds.append((0, cpk[:, C_MW:C_MW + 4]))
                elif br == 0:
                    n = min(w, CMPN)
                    adds.append((w - n, ctab[:, h, CMPN - n:]))
                else:
                    n = min(w, 256)
                    adds.append((w - n, btab[:, h, 256 - n:]))
                    if br == 2 and i >= 4:
                        adds.append((0, tri[:, :]))
                for at, t in adds:
                    n = t.free_size()
                    op = dve.tensor_tensor(sc[:, at:at + n], sc[:, at:at + n], t, ALU.add)
                link(op)
                if j >= 2:
                    dve.wait_ge(s["exp_done"], j - 1)
                dve.tensor_reduce(nmax[:, j % 2:j % 2 + 1], sc[:, 0:w], AX, ALU.max, negate=True
                                  ).then_inc(s["score_in"], 1)

            def finish(pair):
                kind, i, h, _ = JOBS[3 * pair]
                su, rc, o = sums[pair % 2], rec[pair % 2], bank[6 + pair % 2]
                dve.wait_ge(s["exp_done"], 3 * pair + 3)
                link(dve.reciprocal(rc, su))
                if kind == "s":
                    gate, w, dst = sgate[:, 3 * i:3 * i + 3], P, osmp[i]
                else:
                    gate = kvtok[:, i, KVC + h:KVG:NH]
                    w, dst = HD, oacc[i % 2][:, P * (h % GQ) + HD * (h // GQ):P * (h % GQ) + HD * (h // GQ) + HD]
                    if h == 0 and i >= 2:
                        dve.wait_ge(s["turn_fill"], UNIT[("o", i)] + 1)
                link(dve.tensor_tensor(rc, rc, gate, ALU.mult))
                last = ("P", 3 * pair + 2, len(job_groups(JOBS[3 * pair + 2])) - 1)
                dve.wait_ge(s["probT_used"], PUNIT[last] + 1)
                link(dve.tensor_scalar(dst, o[:, 0:w], rc[:, 0:1], None, ALU.mult))
                link(dve.scalar_tensor_tensor(out=dst, in0=o[:, w:2 * w], scalar=rc[:, 1:2], in1=dst, op0=ALU.mult, op1=ALU.add))
                dve.scalar_tensor_tensor(out=dst, in0=o[:, 2 * w:3 * w], scalar=rc[:, 2:3], in1=dst, op0=ALU.mult,
                                         op1=ALU.add).then_inc(s["out_done"], 1)

            for j in range(-2, NJ):
                if j + 2 < NJ:
                    biased_max(j + 2)
                if j >= 1 and (j - 1) % 3 == 2:
                    finish((j - 1) // 3)
            finish(NJ // 3 - 1)

            def add_back(call):
                for mg in range(KD * call, KD * call + KD):
                    cols = slice(P * (mg % KD), P * (mg % KD) + P)
                    for q in range(3):
                        u = 3 * mg + q
                        dve.wait_ge(s["backT_turn"], u + 1)
                        b = bank[6 + u % 2].rearrange("p (x n) -> p x n", n=P)
                        m = 3 if q < 2 else 2
                        x = xt[:, 3 * q:3 * q + m, cols]
                        op = dve.tensor_tensor(x, x, b[:, 0:m], ALU.add)
                        if q == 2:
                            op = dve.tensor_tensor(xt[0:TS, NT, cols], xt[0:TS, NT, cols], b[0:TS, 2], ALU.add)
                        op.then_inc(s["x_add"], 1)

            xo = [xn2[:, 0, :], xn2[:, 1, :]]
            dve.wait_ge(s["x2_in"], 16 * (NT + 1))
            add_back(0)
            dve.wait_ge(s["x_add"], 3 * KD)
            norm(lambda i: xt[:, i, :], xo, "sq3", "ms3", "rstd3", "xn3", "turn3", "evac3d", "gain2_in", 0,
                 lambda i: dve.wait_ge(s["turn3"], i - 1) if i >= 2 else None)
            for f in range(NF):
                for jt in range(FT):
                    for n, (at, w) in enumerate(chunks):
                        u = 3 * (FT * f + jt) + n
                        dve.wait_ge(s["silu_done"], u + 1)
                        dve.tensor_tensor(act[:, jt, at:at + w], bank[2 * n + 1][:, 0:w], silu[:, n, :], ALU.mult
                                          ).then_inc(s["act_done"], 1)
                add_back(1 + f)
            dve.wait_ge(s["x_add"], 9 * KD)
            norm(lambda i: xt[:, i, :], xo, "sq3", "ms3", "rstd3", "y_done", None, None, "gain3_in", NT + 1,
                 lambda i: dve.wait_ge(s[f"y_out{i % 2}"], 16 * (i // 2)) if i >= 2 else dve.wait_ge(s["turn3"], NT + 1))

        @block.gpsimd
        def _(pool):
            nst = [0]

            def store(dst, src_):
                nst[0] += 1
                pool.dma_start(dst, src_).then_inc(s["stores"], 16)

            for c in range(2):
                pool.memset(glu[:, c, 0:CB], 0.0)
                pool.memset(uex[:, c, 0:PB], 0.0)
            pool.memset(poolbd[:, :, :], 0.0).then_inc(s["pzero"], 1)
            pool.memset(tsel, 0.0).then_inc(s["pool"], 1)
            pool.wait_ge(s["table_in"], 96)
            pool.wait_ge(s["pool"], 1)
            ts = tsel.rearrange("p (b h t) -> p b h t", b=4, h=NH)
            for t in range(NS):
                r = slice(32 * t, 32 * t + 32)
                for b in range(4):
                    op = pool.tensor_copy(ts[r, b, :, t], rbias4[r, :])
            op.then_inc(s["tsel_done"], 1)
            pool.wait_ge(s["fvec_ev"], 1)
            pool.dma_start(scratch.ap(), fvec[:, None, :].to_broadcast([NH, P, BAND])).then_inc(s["fvec_out"], 16)

            def rstds(ms_, rs_, base):
                pool.wait_ge(s["prep"], 1)
                for i in range(NT + 1):
                    n = tile_rows(i)
                    pool.wait_ge(s[ms_], base + i + 1)
                    pool.tensor_tensor(rstd[0:n, i:i + 1], ms[0:n, i:i + 1], mhalf[0:n, :], ALU.pow).then_inc(s[rs_], 1)

            rstds("ms_done", "rstd_done", 0)
            store(out["new_win_sample"][:, 0:WINDOW - NS], A["cache_win_kv"][0].rearrange("b t a g d -> b t (a g d)")[:, NS:])
            store(out["new_conv_sample"][:, 0:CB - NS], A["state_conv"][0][:, NS:])
            store(out["new_pool_sample"][:, 0:PB - NS], A["state_pool"][0][:, NS:])
            pool.wait_ge(s["zc_done"], 2)
            pool.wait_ge(s["state_ev"], 2)
            pool.wait_ge(s["glu_done"], 2)
            step = [1]
            for c in range(2):
                for k, src_ in ((c, smp(glu[:, c, :], CB + T, GE, CB, NS)), (2 + c, smp(uex[:, c, :], PB + T, UE, PB, NS))):
                    op = pool.tensor_copy(newcols[:, k, :].rearrange("p (b t) -> p b t", t=NS), src_)
            op.then_inc(s["newcols_done"], 1)

            def plink(op):
                step[0] += 1
                op.then_inc(s["pool"], 1)
                pool.wait_ge(s["pool"], step[0])

            a, b, hi = pl[:, 0, :], pl[:, 1, :], slice(HD, P)
            for c in range(2):
                if c:
                    pool.wait_ge(s["pool_d"], 1)
                u = uex[:, c, :]
                plink(pool.tensor_tensor(a[:, 1:], u[:, 1:], u[:, :-1], ALU.add))
                if c == 0:
                    pool.tensor_tensor(b[hi, 3:], a[hi, 3:], a[hi, 1:-2], ALU.add).then_inc(s["pairsum"], 1)
                else:
                    plink(pool.tensor_tensor(b[:, 3:], a[:, 3:], a[:, 1:-2], ALU.add))
                    plink(pool.tensor_tensor(a[:, 7:], b[:, 7:], b[:, 3:-4], ALU.add))
                    pool.tensor_tensor(b[hi, 15:], a[hi, 15:], a[hi, 7:-8], ALU.add).then_inc(s["pairsum"], 1)
            pool.wait_ge(s["kv_ev"], NT + 1)
            for br, name in ((0, "cmp"), (1, "slc")):
                store(out[f"new_{name}_prompt"].rearrange("(i p) n -> p i n", p=P), kvtok[:, 0:NT, 256 * br:256 * br + 256])
                store(out[f"new_{name}_sample"], kvtok[0:TS, NT, 256 * br:256 * br + 256])
            store(out["new_win_prompt"].rearrange("(i p) n -> p i n", p=P), kvtok[:, NT - WINDOW // P:NT, 512:768])
            for b_ in range(NB):
                store(out["new_win_sample"][b_, WINDOW - NS:], kvtok[NS * b_:NS * b_ + NS, NT, 512:768])
            pool.wait_ge(s["last_ev"], 1)
            store(out["new_conv_prompt"], lastT[0:CB, 0, :])
            store(out["new_pool_prompt"], lastT[0:PB, 1, :])
            for b_ in range(NB):
                store(out["new_conv_sample"][b_, CB - NS:], lastT[NS * b_:NS * b_ + NS, 2, :])
                store(out["new_pool_sample"][b_, PB - NS:], lastT[NS * b_:NS * b_ + NS, 3, :])
            assert nst[0] == STORES == STORES_M == STORES_E

            pool.wait_ge(s["mix_done"], 4)
            pool.wait_ge(s["stores"], 16 * STORES_E)
            pool.memset(cmpw[:, :, :, :], 0.0).then_inc(s["late_zero"], 1)
            pool.memset(qbd[:, :, :], 0.0).then_inc(s["late_zero"], 1)
            pool.wait_ge(s["late_zero"], 2)
            for g in range(KVH):
                gp = slice(HD * g, HD * g + HD)
                for G in range(2):
                    for b_ in range(4):
                        dst = qbd[gp, G, 32 * b_ + 16 * g:32 * b_ + 16 * g + 16].rearrange("p (r t) -> p r t", t=NS)
                        at = T + 16 * G + NS * b_
                        op = pool.tensor_copy(dst, qT[gp, :, at:at + NS])
            op.then_inc(s["qbd_done"], 1)
            rstds("ms3", "rstd3", 0)
            rstds("ms3", "rstd3", NT + 1)


STORES_E = STORES_M = STORES = 3 + 4 + 1 + NB + 2 + 2 * NB
NPHYS = 40

_INS = ["x_prompt", "x_sample", "cache_cmp_kv", "cache_slc_kv", "cache_win_kv", "state_conv", "state_pool",
        "page_table", "rel_bias", "norm1", "w_in", "conv_dw", "conv_b", "conv_ln_g", "conv_ln_b", "pool_w",
        "pool_scale", "cmp_pe_k", "cmp_wk", "cmp_pe_v", "cmp_wv", "w_out", "norm2", "w_gu", "w_down", "final_norm"]
_KVR = KVH * HD * 2
_OUTS = [("y_prompt", (1, T, D), None), ("y_sample", (NB, NS, D), None),
         ("new_cmp_prompt", (T, _KVR), (1, 1, T, 2, KVH, HD)), ("new_slc_prompt", (T, _KVR), (1, 1, T, 2, KVH, HD)),
         ("new_win_prompt", (WINDOW, _KVR), (1, 1, WINDOW, 2, KVH, HD)),
         ("new_conv_prompt", (CB, CONV_W), (1, 1, CB, CONV_W)), ("new_pool_prompt", (PB, POOL_W), (1, 1, PB, POOL_W)),
         ("new_cmp_sample", (TS, _KVR), (1, NB, NS, 2, KVH, HD)), ("new_slc_sample", (TS, _KVR), (1, NB, NS, 2, KVH, HD)),
         ("new_win_sample", (NB, WINDOW, _KVR), (1, NB, WINDOW, 2, KVH, HD)),
         ("new_conv_sample", (NB, CB, CONV_W), (1, NB, CB, CONV_W)),
         ("new_pool_sample", (NB, PB, POOL_W), (1, NB, PB, POOL_W))]


def kernel(**inputs):
    import concourse.bacc as bacc
    from concourse.bass_utils import run_bass_kernel_spmd

    nc = bacc.Bacc("TRN2", target_bir_lowering=False, num_devices=1)
    arrays = {n: np.ascontiguousarray(inputs[n]) for n in _INS}
    arrays.update(constants())
    feed, A = {}, {}
    for n, a in arrays.items():
        feed[f"in_{n}"] = a
        A[n] = nc.dram_tensor(f"in_{n}", a.shape, mybir.dt.from_np(a.dtype), kind="ExternalInput").ap()
    out = {n: nc.dram_tensor(f"out_{n}", shape, F32, kind="ExternalOutput").ap() for n, shape, _ in _OUTS}
    build(nc, A, out)
    r = run_bass_kernel_spmd(nc, [feed], core_ids=[0]).results[0]
    return tuple(r[f"out_{n}"].reshape(full or shape) for n, shape, full in _OUTS)
```

```python
import math
from contextlib import ExitStack

import numpy as np

import concourse.bass as bass
from concourse import mybir

F32 = mybir.dt.float32
F32R = mybir.dt.float32r
I32 = mybir.dt.int32
ALU = mybir.AluOpType
ACT = mybir.ActivationFunctionType
AX = mybir.AxisListType.X

P = 128
D = 1024
T = 1024
NB, NS = 8, 4
TS = NB * NS
TT = T + TS
NT = T // P
KD = D // P
PAST, PAGE = 512, 128
NPG = PAST // PAGE
CONV_W, POOL_W, NH, HD, KVH = 256, 256, 8, 64, 2
GQ = NH // KVH
CW, CB = 31, 30
PB = 15
WINS = (2, 4, 8, 16)
STRIDE, CBLK, WINDOW = 16, 32, 512
NCMP = T // STRIDE - 1
BUCKETS, MAXD = 32, 128
DFF = 2816
KF = DFF // P
EPS, NEG = 1e-6, -1e30
OFF_POOL, OFF_Q = 2 * CONV_W, 2 * CONV_W + POOL_W
OFF_KV = OFF_Q + NH * HD
KVC = 6 * KVH * HD
KVG = KVC + 3 * NH
IN_W = OFF_KV + KVG
NCH = TT // 3
GE, UE = CB + NS, PB + NS
GLU_L = CB + T + NB * GE
U_L = PB + T + NB * UE
Y_L = GLU_L - CB
FT = 2
NF = KF // FT
NLOOP = (NF - 3) // 2
WB = KD
WGU, WDN = 2 * FT, KD
DLO, DHI = -160, 256
ND = DHI - DLO + 1
BAND = 3 * P
C_ID, C_OH, C_MN, C_MW, C_MC = 0, 128, 416, 480, 484
C_GM, C_VA, C_IW, C_FX, C_SEL, C_END = 612, 636, 637, 639, 669, 925
CMPN = 15
KC_L = NB * PAST + TT
KC_N = KC_L // STRIDE - 1


def bucket(n):
    n = np.asarray(n)
    e = BUCKETS // 2
    big = e + (np.log(np.maximum(n, 1).astype(np.float32) / e) / math.log(MAXD / e) * (BUCKETS - e)).astype(np.int32)
    return np.where(n < e, n, np.minimum(big, BUCKETS - 1))


def onehot(d):
    m = np.zeros((BUCKETS + 1, len(d)), np.float32)
    for j, x in enumerate(d):
        if x >= 0:
            m[bucket(x), j] += 1
            m[BUCKETS - 1, j] -= 1
        else:
            m[BUCKETS, j] = NEG
    return m


def constants():
    dist = np.concatenate([onehot(np.arange(DLO, DHI + 1)), onehot(2 * P - 1 - np.arange(BAND))], axis=1)
    c = np.zeros((P, C_END), np.float32)
    c[:, C_ID:C_ID + P] = np.eye(P)
    for t in range(NS):
        r = slice(32 * t, 32 * t + 32)
        c[r, C_OH:C_OH + 128] = onehot(PAST + t - (384 + np.arange(128)))[:32]
        c[r, C_OH + 128:C_OH + 160] = onehot(t - np.tile(np.arange(NS), NB))[:32]
        n = np.tile(np.arange(32), 4)
        o = onehot(PAST + t - (STRIDE * n + CBLK - 1))[:32]
        c[r, C_OH + 160:C_OH + 288] = o
    for row in range(P):
        b, h, t = row // 32, row // 4 % 8, row % 4
        for G in range(2):
            for col in range(32):
                if col // 4 != 4 * G + b or col % 4 > t:
                    c[row, C_MN + 32 * G + col] = NEG
            c[4 * 4 * G + 4 * b + t, C_SEL + 128 * G + row] = 1
        c[row, C_MW:C_MW + 4] = np.where(np.arange(4) <= t, NEG, 0)
        col = np.arange(128)
        c[row, C_MC:C_MC + 128] = np.where((col // 32 != b) | (col % 32 == 31), NEG, 0)
        for br in range(3):
            c[row, C_GM + 8 * br + h] = 1
    c[:, C_VA] = np.arange(P) >= CBLK - 1
    for k in range(2):
        w = np.where(np.arange(P) < 64, WINS[2 * k], WINS[2 * k + 1])
        c[:, C_IW + k] = 1.0 / w
        c[:, C_FX + 15 * k:C_FX + 15 * k + 15] = w[:, None] / np.minimum(w[:, None], np.arange(15)[None] + 1)
    tri = np.where(np.arange(P)[:, None] >= np.arange(P)[None, :], NEG, 0).astype(np.float32)
    return {"c_dist": dist, "c_pack": c, "c_tri": tri}


def tile_rows(i):
    return P if i < NT else TS


SJOBS = [(G, br) for G in range(2) for br in range(3)]
NSJ = len(SJOBS)


def s_width(j):
    return P if SJOBS[j][1] == 0 else PAST + TS


def s_groups(j):
    w = s_width(j)
    cols = [(c, min(P, w - c)) for c in range(0, w, P)]
    return [cols[k:k + 4] for k in range(0, len(cols), 4)]


GROUPS = [(i, g, br) for i in range(NT) for g in range(KVH) for br in (1, 2, 0)]
NG = len(GROUPS)
LAG = 2
SLOTS = (LAG + 1) * GQ


def g_width(n):
    i, _, br = GROUPS[n]
    return 8 * i + 7 if br == 0 else P * (i + 1) if br == 1 else P * min(i + 1, 5)


def g_tiles(n):
    return [(c, min(P, g_width(n) - c)) for c in range(0, g_width(n), P)]


def steps():
    for n in range(NG + LAG):
        old = n - LAG
        tiles = g_tiles(old) if old >= 0 else []
        for r in range(GQ):
            yield (n, r) if n < NG else None, [(old, x) for x in range(len(tiles)) if x * GQ // len(tiles) == r]


ZTILES = [CONV_W, 0, CONV_W + P, P, OFF_POOL, OFF_POOL + P]
NZ = len(ZTILES) + GQ


EARLY_CP = 3


def turn_units():
    keys = [("cp", b, kv) for b in range(EARLY_CP) for kv in range(2)]
    keys += [("knew", 0), ("knew", 1)] + [("kT", ty, hf) for ty in range(4) for hf in range(2)]
    keys += [("pe", 0), ("pe", 1)] + [("cp", b, kv) for b in range(EARLY_CP, NB) for kv in range(2)]
    keys += [("vc", x) for x in range(3)]
    for j in range(-2, NSJ):
        if j + 2 < NSJ and SJOBS[j + 2][1] > 0:
            keys += [("kp", j + 2, b) for b in range(4)]
        if j >= 0:
            keys += [("P", j, k) for k in range(len(s_groups(j)))]
            if j == 3:
                keys.append(("o", 0))
    keys.append(("o", 1))
    for _, tiles in steps():
        keys += [("t",) + x for x in tiles]
    return {k: n for n, k in enumerate(keys)}


UNIT = turn_units()
PUNIT = {k: n for n, k in enumerate([k for k in UNIT if k[0] in "Pt"])}
KUNIT = {k: n for n, k in enumerate([k for k in UNIT if k[0] == "kp"])}
NPT = 3


def build(nc, A, out):
    ctx = ExitStack()
    with ctx:
        def sem(name):
            return ctx.enter_context(nc.semaphore(name))

        def sb(name, shape, at=ctx, dt=F32):
            return at.enter_context(nc.sbuf_tensor(name, shape, dt))

        psA = ctx.enter_context(nc.psum_tensor("psA", [P, 1024], F32))
        psB = ctx.enter_context(nc.psum_tensor("psB", [P, 1024], F32))
        psC = ctx.enter_context(nc.psum_tensor("psC", [P, 1024], F32))
        psD = ctx.enter_context(nc.psum_tensor("psD", [P, 1024], F32))
        bank = [t[:, 512 * k:512 * k + 512] for t in (psA, psB, psC, psD) for k in range(2)]
        scores = [psA, psB]

        cpk = sb("cpk", [P, C_END])
        avg = sb("avg", [P, P])
        featT = sb("featT", [P, KD, TT])
        gB = sb("gB", [P, D])
        small = sb("small", [P, 64])
        mhalf, epsc = small[:, 0:1], small[:, 1:2]
        stat, ms, rstd = small[:, 2:11], small[:, 11:20], small[:, 20:29]
        convb, lng, lnb, pscale = (small[:, 29 + 2 * k:31 + 2 * k] for k in range(4))
        posk = small[:, 37:39]
        nmax = small[:, 39:41]
        sums = [small[:, 41:45], small[:, 45:49]]
        rec = [small[:, 49:53], small[:, 60:64]]
        sgate = small[:, 53:59]
        ident = cpk[:, C_ID:C_ID + P]

        mid = ExitStack()
        kvtok = sb("kvtok", [P, NT + 1, KVG], mid)
        qT = sb("qT", [P, GQ, TT], mid)
        kslcT = sb("kslcT", [P, T], mid)
        kwinT = sb("kwinT", [P, T], mid)
        knewT = sb("knewT", [P, 2, TS], mid)
        btab = sb("btab", [P, NH, 256], mid)
        ctab = sb("ctab", [P, NH, CMPN], mid)
        stab = sb("stab", [P, 320], mid)
        tri = sb("tri", [P, P], mid)
        convw = sb("convw", [P, 2, CW], mid)
        posr = sb("posr", [32, 2, P], mid)
        qbd = sb("qbd", [P, 2, P], mid)

        early = ExitStack()
        ring = sb("ring", [P, 5 * TT], early)
        wring = ring[:, 0:3 * D].rearrange("p (s k n) -> p s k n", s=3, k=KD)
        xring = ring[:, 3 * D:5 * D].rearrange("p (s n) -> p s n", s=2)
        ysq = ring[:, 0:2 * TT].rearrange("p (c t) -> p c t", c=2)
        ystd = ring[:, 2 * TT:3 * TT]
        yc = ring[:, 3 * TT:5 * TT].rearrange("p (c t) -> p c t", c=2)
        kvw = sb("kvw", [P, KD, KVG], early)
        dT = sb("dT", [P, 2, TT], early)
        poolbd = sb("poolbd", [P, 2, P], early)
        ybuf = sb("ybuf", [P, 2, GLU_L], early)
        glu = sb("glu", [P, 2, GLU_L], early)
        uex = sb("uex", [P, 2, U_L], early)
        pl = sb("pl", [P, 2, U_L], early)
        stin = sb("stin", [P, 4, 256], early)
        newcols = sb("newcols", [P, 4, TS], early)
        yflat = ybuf[:, :, :].rearrange("p c n -> p (c n)")
        xn = [yflat[:, 0:D], yflat[:, D:2 * D]]
        sig = pl[:, 0, 0:TT]
        sqjunk = pl[:, 1, 0:D]
        dflat = dT[:, :, :].rearrange("p c t -> p (c t)")
        rbias, rbias4 = dflat[0:33, 0:NH], dflat[:, 16:16 + NH]
        fvec = dflat[0:NH, 64:64 + BAND]
        tsel = dflat[:, 448:576]
        distt = dflat[0:33, 576:576 + ND + BAND]
        lastT = stin[0:32, :, :]

        early.close()
        late = ExitStack()
        pages = sb("pages", [P, 8, NPG, 256], late)
        probTb = sb("probTb", [P, NPT, 512], late)
        kcT = sb("kcT", [P, KC_N - 1], late)
        vcT = sb("vcT", [P, KC_N - 1], late)
        vctok = sb("vctok", [P, 3, P], late)
        probT = [probTb[:, k, :] for k in range(NPT)]
        rawkv = ExitStack()
        cmpw = sb("cmpw", [P, 3, 8, P], rawkv)
        behind = (5 * TT + KD * KVG + 2 * TT + 2 * P) - (8 * NPG * 256 + NPT * 512 + 2 * (KC_N - 1) + 3 * P + 24 * P)
        sb("gap", [P, behind], rawkv)
        ckT = sb("ckT", [P, KC_L], rawkv)
        cvT = sb("cvT", [P, KC_L], rawkv)
        rawkv.close()
        late2 = ExitStack()
        probs = sb("probs", [P, SLOTS, T], late2)
        prob = [probs[:, k, :] for k in range(SLOTS)]
        sprob = [prob[4], prob[5]]
        kpT = [prob[6][:, 512 * k:512 * k + 512] for k in range(2)]
        osmp = [prob[7][:, P * k:P * k + P] for k in range(2)]
        gjunk = prob[7][:, 256:304]

        def page_slot(pj, b):
            return pages[:, 4 * pj + b] if pj < 2 else \
                prob[8 * (pj - 2) + b].rearrange("p (n c) -> p n c", n=NPG)

        late2.close()
        late.close()
        mid.close()

        xt = sb("xt", [P, NT + 1, D])
        fH = sb("fH", [P, KD, TT], dt=F32R)
        fL = sb("fL", [P, KD, TT], dt=F32R)
        wraw = sb("wraw", [P, 2, KD, P])
        wH = sb("wH", [P, 2, KD, P], dt=F32R)
        wL = sb("wL", [P, 2, KD, P], dt=F32R)
        hid = sb("hid", [P, 3, NCH])
        back0 = ExitStack()
        backT = sb("backT", [P, 2, TT], back0)
        xn2 = sb("xn2", [P, 2, D], back0)
        back0.close()
        aH = sb("aH", [P, 2, FT, TT], dt=F32R)
        aL = sb("aL", [P, 2, FT, TT], dt=F32R)
        yT = featT
        yo = [xflat for xflat in (hid[:, :, :].rearrange("p a b -> p (a b)")[:, 0:D],
                                  wraw[:, 0].rearrange("p k n -> p (k n)"))]
        aH_sq = yT[:, 0, 0:D]
        sqb = wraw[:, 1].rearrange("p k n -> p (k n)")

        scratch = nc.dram_tensor("bias_scratch", [NH, P, BAND], F32, kind="Internal")

        names = (
            "const_in table_in gain_in x_in0 x_in1 state_in w_in0 w_in1 w_in2 kvw_in ptab_in chan_in poolw_in "
            "tri_in table_mm table_ev fvec_ev fvec_out btab_in tsel_done prep "
            "sq_done ms_done rstd_done xn_done turn_x evac_xa evac_xd state_turn state_ev "
            "z_mm sig_done glu_done zc_done kv_mm kv_ev gates_done valid_done last_out "
            "dve pool pairsum pool_used pool_d conv_done mean_mm yc_done sq2_done var_mm std_done inv_done norm_done "
            "mix_done pool_mm newcols_done last_turn last_ev stores pzero "
            "late_zero turn_fill turn_drain page_in0 page_in1 page_in2 page_in3 cmpw_in0 cmpw_in1 cmpw_in2 cmpw_used cmp_mm pos_done cmp_ev posr_in "
            "gate_mm gate_ev qbd_done score_mm score_in exp_done probT_used keys_used out_done rec_done scaled o_ev "
            "x2_in mixH_done mixL_done raw_in0 raw_in1 wH_done wL_done unit_mm back_ev back_turn x_add "
            "sq3 ms3 rstd3 xn3 turn3 evac3a evac3d silu_done hid_done aH_done aL_done y_add gain2_in gain3_in "
            "y_done y_out0 y_out1").split()
        s = {n: sem(n) for n in names}
        cpage = [sem(f"cmp_page{b}") for b in range(NB)]
        block = ctx.enter_context(nc.Block())

        chunks = [(NCH * n, NCH) for n in range(3)]
        lnchunks = [(0, 512), (512, 512), (T, TS)]

        POOL_BANKS = ((0, 1, 2), (3, 6, 7))

        def smp(t, L, ext, lo, n):
            return t[:, L:].rearrange("p (b g) -> p b g", g=ext)[:, :, lo:lo + n]

        def ext_cols(t, c, at, w, start, ext, lo):
            parts = []
            if at < T:
                n = min(w, T - at)
                parts.append((0, n, t[:, c, start + at:start + at + n]))
            if at + w > T:
                parts.append((T - at, w, smp(t[:, c, :], start + T, ext, lo, NS)))
            return parts

        def half(w, par):
            return (w - par) // 2 if isinstance(w, int) else (w - par) // 2

        def ffn_order(eng, gu, dn):
            gu(0, WB)
            gu(1, WB + WGU)
            at = WB + 2 * WGU
            with eng.Fori(0, NLOOP) as t:
                for x in range(2):
                    w = t * (2 * (WGU + WDN)) + (at + (WGU + WDN) * x)
                    dn(t * 2 + x, w)
                    gu(t * 2 + (x + 2), w + WDN)
            f = 2 * NLOOP
            at += f * (WGU + WDN)
            dn(f, at)
            gu(f + 2, at + WDN)
            dn(f + 1, at + WDN + WGU)
            dn(f + 2, at + 2 * WDN + WGU)

        @block.sync
        def _(sp):
            sp.dma_start(cpk[:, :], A["c_pack"]).then_inc(s["const_in"], 16)
            sp.dma_start(distt, A["c_dist"]).then_inc(s["table_in"], 16)
            sp.dma_start(rbias[0:32, :], A["rel_bias"]).then_inc(s["table_in"], 16)
            for t in range(NS):
                sp.dma_start(rbias4[32 * t:32 * t + 32, :], A["rel_bias"]).then_inc(s["table_in"], 16)
            sp.dma_start(gB[:, :], A["norm1"].to_broadcast([P, D])).then_inc(s["gain_in"], 16)

            def load_x(dst, i):
                n = tile_rows(i)
                src = A["x_prompt"][0, P * i:P * i + P, :] if i < NT else A["x_sample"].rearrange("b t d -> (b t) d")
                return sp.dma_start(dst[0:n, :], src)

            w_in = A["w_in"][0].rearrange("(k p) n -> p k n", p=P)

            def load_z(m):
                slot, q = wring[:, m % 3], m - len(ZTILES)
                if m >= 3:
                    sp.wait_ge(s["z_mm"], m - 2)
                if q < 0:
                    sp.dma_start(slot, w_in[:, :, ZTILES[m]:ZTILES[m] + P]).then_inc(s[f"w_in{m % 3}"], 32)
                else:
                    for g in range(KVH):
                        c = OFF_Q + HD * (GQ * g + q)
                        sp.dma_start(slot[:, :, HD * g:HD * g + HD], w_in[:, :, c:c + HD]).then_inc(s[f"w_in{m % 3}"], 16)

            for i in range(2):
                load_x(xring[:, i], i).then_inc(s[f"x_in{i}"], 16)
            for k in range(2):
                sp.dma_start(stin[0:120, k, :], A["state_conv"][0, 4 * k:4 * k + 4].rearrange("b t c -> (b t) c")
                             ).then_inc(s["state_in"], 16)
            sp.dma_start(stin[0:120, 2, :], A["state_pool"][0].rearrange("b t c -> (b t) c")).then_inc(s["state_in"], 16)
            load_z(0)
            load_z(1)
            load_z(2)
            with nc.allow_non_contiguous_dma(reason="per-channel vectors"):
                for t, name in ((convb, "conv_b"), (lng, "conv_ln_g"), (lnb, "conv_ln_b"), (pscale, "pool_scale")):
                    sp.dma_start(t, A[name][0].rearrange("(c p) -> p c", p=P)).then_inc(s["chan_in"], 16)
                for c in range(2):
                    sp.dma_start(convw[:, c, :], A["conv_dw"][0].rearrange("k (c p) -> c p k", p=P)[c]
                                 ).then_inc(s["chan_in"], 16)
            for i in range(2, NT + 1):
                sp.wait_ge(s["xn_done"], i - 1)
                load_x(xring[:, i % 2], i).then_inc(s[f"x_in{i % 2}"], 16)
            sp.dma_start(kvw[:, :, :], w_in[:, :, OFF_KV:]).then_inc(s["kvw_in"], 16)
            sp.wait_ge(s["pzero"], 1)
            for g in range(4):
                r = slice(HD * (g % 2), HD * (g % 2) + HD)
                sp.dma_start(poolbd[r, g // 2, r], A["pool_w"][0, g]).then_inc(s["poolw_in"], 16)
            sp.dma_start(tri[:, :], A["c_tri"]).then_inc(s["tri_in"], 16)
            sp.wait_ge(s["fvec_out"], 16)
            band = bass.AP(tensor=scratch, offset=P - 1, ap=[[BAND - 1, P], [P * BAND, NH], [1, 2 * P]])
            sp.dma_start(btab[:, :, :], band).then_inc(s["btab_in"], 16)
            sp.dma_start(posr[:, 0, 0:HD], A["cmp_pe_k"][0]).then_inc(s["posr_in"], 16)
            sp.dma_start(posr[:, 0, HD:P], A["cmp_pe_k"][0]).then_inc(s["posr_in"], 16)
            sp.dma_start(posr[:, 1, 0:HD], A["cmp_pe_v"][0]).then_inc(s["posr_in"], 16)
            sp.dma_start(posr[:, 1, HD:P], A["cmp_pe_v"][0]).then_inc(s["posr_in"], 16)
            page = []
            for m in range(3, NZ):
                load_z(m)
                for b in range(len(page), min(NB, 2 * (m - 2))):
                    page.append([sp.value_load(A["page_table"][b:b + 1, n:n + 1], min_val=0, max_val=NPHYS - 1)
                                 for n in range(NPG)])

            for b in range(NB):
                if b == 0:
                    sp.wait_ge(s["norm_done"], 2)
                elif b == 3:
                    sp.wait_ge(s["mix_done"], 2)
                    sp.wait_ge(s["kv_mm"], NT + 1)
                for n in range(NPG):
                    sp.dma_start(pages[:, b, n, :], A["cache_cmp_kv"][0].rearrange("f p a g d -> f p (a g d)")[
                        bass.ds(page[b][n], 1), :, :].rearrange("f p n -> (f p) n")).then_inc(cpage[b], 16)
            sp.wait_ge(s["late_zero"], 2)

            def load_cmpw(q):
                kv, l0 = q // 4, 8 * (q % 4)
                if q >= 3:
                    sp.wait_ge(s["cmpw_used"], q - 2)
                w = A["cmp_wv" if kv else "cmp_wk"][0, l0:l0 + 8].rearrange("l d e -> d l e")
                for g in range(KVH):
                    r = slice(HD * g, HD * g + HD)
                    sp.dma_start(cmpw[r, q % 3, :, r], w).then_inc(s[f"cmpw_in{q % 3}"], 16)

            def load_pages(pj):
                G, br = pj // 2, 1 + pj % 2
                if pj == 2:
                    sp.wait_ge(s["cmpw_used"], 8)
                for b in range(4):
                    slot = page_slot(pj, b)
                    if pj < 2:
                        sp.wait_ge(s["turn_fill"], UNIT[("cp", 4 * pj + b, 1)] + 1)
                    if br == 1:
                        for n in range(NPG):
                            sp.dma_start(slot[:, n, :], A["cache_slc_kv"][0].rearrange("f p a g d -> f p (a g d)")[
                                bass.ds(page[4 * G + b][n], 1), :, :].rearrange("f p n -> (f p) n")).then_inc(s[f"page_in{pj}"], 16)
                    else:
                        sp.dma_start(slot[:, :, :], A["cache_win_kv"][0, 4 * G + b].rearrange(
                            "(n p) a g d -> p n (a g d)", p=PAGE)).then_inc(s[f"page_in{pj}"], 16)

            for q in range(3):
                load_cmpw(q)
            load_pages(0)
            for q in range(3, 8):
                load_cmpw(q)
            for pj in range(1, 4):
                load_pages(pj)

            sp.wait_ge(s["o_ev"], NT)
            sp.wait_ge(s["stores"], 16 * STORES)
            for i in range(NT + 1):
                load_x(xt[:, i, :], i).then_inc(s["x2_in"], 16)
            sp.dma_start(gB[:, :], A["norm2"].to_broadcast([P, D])).then_inc(s["gain2_in"], 16)

            def raw(w, par):
                if not (isinstance(w, int) and w < 2):
                    sp.wait_ge(s["wL_done"], w - 1)
                return wraw[:, par]

            for m in range(KD):
                slot = raw(m, m % 2)
                cols = slice(P * m, P * m + P)
                sp.dma_start(slot[:, 0:4, :], A["w_out"][0, 0:512, cols].rearrange("(k p) n -> p k n", p=P)
                             ).then_inc(s[f"raw_in{m % 2}"], 16)
                for g in range(KVH):
                    rows = 512 + GQ * HD * g
                    sp.dma_start(slot[HD * g:HD * g + HD, 4:8, :], A["w_out"][0, rows:rows + GQ * HD, cols].rearrange(
                        "(r d) n -> d r n", d=HD)).then_inc(s[f"raw_in{m % 2}"], 16)
            w_gu = A["w_gu"][0].rearrange("(k p) n -> p k n", p=P)
            w_dn = A["w_down"][0].rearrange("(k p) n -> p k n", p=P)

            def load_gu(f, w):
                for x in range(2 * FT):
                    c = (x % 2) * DFF + P * (x // 2)
                    sp.dma_start(raw(w + x, x % 2), w_gu[:, :, bass.ds(f * (FT * P) + c, P)]).then_inc(s[f"raw_in{x % 2}"], 48)

            def load_dn(f, w):
                for m in range(KD):
                    sp.dma_start(raw(w + m, m % 2)[:, 0:FT, :], w_dn[:, bass.ds(f * FT, FT), P * m:P * m + P]
                                 ).then_inc(s[f"raw_in{m % 2}"], 48)

            ffn_order(sp, load_gu, load_dn)
            sp.wait_ge(s["xn3"], NT + 1)
            sp.dma_start(gB[:, :], A["final_norm"][None, :].to_broadcast([P, D])).then_inc(s["gain3_in"], 16)
            for i in range(NT + 1):
                sp.wait_ge(s["y_done"], i + 1)
                n = tile_rows(i)
                dst = out["y_prompt"][0, P * i:P * i + P, :] if i < NT else out["y_sample"].rearrange("b t d -> (b t) d")
                sp.dma_start(dst, yo[i % 2][0:n, :]).then_inc(s[f"y_out{i % 2}"], 16)
            sp.wait_ge(s["y_out0"], 16 * (NT // 2 + 1))
            sp.wait_ge(s["y_out1"], 16 * (NT // 2))
            sp.wait_ge(s["stores"], 16 * STORES)
            sp.wait_ge(s["last_out"], 16 * LASTS)

        @block.tensor
        def _(pe):
            def turn_tile(dst, src, n):
                return pe.transpose(dst, src, ident[0:n, 0:n])

            pe.wait_ge(s["const_in"], 16)
            pe.wait_ge(s["table_in"], 16 * 6)
            pe.wait_ge(s["prep"], 1)
            pe.matmul(bank[0][0:NH, 0:BAND], rbias, distt[:, ND:ND + BAND], start=True, stop=True).then_inc(s["table_mm"], 1)
            for c in range(CMPN):
                at = -(CBLK - 1) - STRIDE * (c - 8) - DLO
                mm = pe.matmul(bank[1][:, NH * c:NH * c + NH], distt[:, at:at + P], rbias, start=True, stop=True)
            mm.then_inc(s["table_mm"], 1)
            pe.wait_ge(s["tsel_done"], 1)
            pe.matmul(bank[2][:, 0:288], tsel, cpk[:, C_OH:C_OH + 288], start=True, stop=True).then_inc(s["table_mm"], 1)
            pe.wait_ge(s["state_in"], 48)
            for k in range(2):
                for c in range(2):
                    q = 2 * k + c
                    turn_tile(bank[6][:, 120 * q:120 * q + 120], stin[0:120, k, P * c:P * c + P], 120)
            for c in range(2):
                mm = turn_tile(bank[7][:, 120 * c:120 * c + 120], stin[0:120, 2, P * c:P * c + P], 120)
            mm.then_inc(s["state_turn"], 1)
            pe.wait_ge(s["table_ev"], 2)
            pe.wait_ge(s["fvec_ev"], 1)

            def turn_norm(xs, done, filled, eva, evd):
                for i in range(NT + 1):
                    n = tile_rows(i)
                    pe.wait_ge(s[done], i + 1)
                    if i >= 2:
                        pe.wait_ge(s[eva], i - 1)
                        pe.wait_ge(s[evd], i - 1)
                    for k in range(KD):
                        b = bank[2 * (i % 2) + k // 4]
                        mm = turn_tile(b[:, P * (k % 4):P * (k % 4) + n], xs[i % 2][0:n, P * k:P * k + P], n)
                    mm.then_inc(s[filled], 1)

            turn_norm(xn, "xn_done", "turn_x", "evac_xa", "evac_xd")
            pe.wait_ge(s["evac_xa"], NT + 1)
            pe.wait_ge(s["evac_xd"], NT + 1)
            for m in range(NZ):
                pe.wait_ge(s[f"w_in{m % 3}"], 32 * (m // 3 + 1))
                if m >= 2:
                    p = m - 2
                    if p < 4:
                        pe.wait_ge(s["glu_done" if p % 2 else "sig_done"], p // 2 + 1)
                    else:
                        pe.wait_ge(s["zc_done"], p - 3)
                for n, (at, w) in enumerate(chunks):
                    for k in range(KD):
                        mm = pe.matmul(bank[3 * (m % 2) + n][:, 0:w], wring[:, m % 3, k, :], featT[:, k, at:at + w],
                                       start=(k == 0), stop=(k == KD - 1))
                mm.then_inc(s["z_mm"], 1)
                if m == 7:
                    pe.wait_ge(s["state_ev"], 2)
                    pe.wait_ge(s["newcols_done"], 1)
                    for c in range(2):
                        turn_tile(bank[6][0:30, P * c:P * c + P], glu[:, c, T:CB + T], P)
                        turn_tile(bank[6][0:15, 256 + P * c:256 + P * c + P], uex[:, c, T:PB + T], P)
                    for c in range(2):
                        turn_tile(bank[7][0:TS, P * c:P * c + P], newcols[:, c, :], P)
                        mm = turn_tile(bank[7][0:TS, 256 + P * c:256 + P * c + P], newcols[:, 2 + c, :], P)
                    mm.then_inc(s["last_turn"], 1)
            nturn = [0]

            def turn(key, parts, first=None):
                u = UNIT[key]
                assert u == nturn[0]
                nturn[0] += 1
                if u >= 2:
                    pe.wait_ge(s["turn_drain"], u - 1)
                for at, n, srcap in parts:
                    m = srcap.free_size()
                    mm = turn_tile(bank[4 + u % 2][0:m, at:at + n], srcap, n)
                mm.then_inc(s["turn_fill"], 1)

            pe.wait_ge(s["kvw_in"], 16)
            pe.wait_ge(s["zc_done"], NZ - 4)
            hk = KVG // 2

            def channel_mean(src, done):
                for n, (at, w) in enumerate(lnchunks):
                    for c in range(2):
                        mm = pe.matmul(bank[4 + n][:, 0:w], avg[:, :], src(c, at, w), start=(c == 0), stop=(c == 1))
                mm.then_inc(s[done], 1)

            def turn_pages(b):
                pe.wait_ge(cpage[b], 16 * NPG)
                for kv in range(2):
                    turn(("cp", b, kv), [(P * x, P, pages[:, b, x, P * kv:P * kv + P]) for x in range(NPG)])

            for i in range(NT + 1):
                n = tile_rows(i)
                if i >= 2:
                    pe.wait_ge(s["kv_ev"], i - 1)
                for hf in range(2):
                    for k in range(KD):
                        mm = pe.matmul(bank[2 * (i % 2) + hf][0:n, 0:hk], featT[:, k, P * i:P * i + n],
                                       kvw[:, k, hk * hf:hk * hf + hk], start=(k == 0), stop=(k == KD - 1))
                mm.then_inc(s["kv_mm"], 1)
                if i == 1:
                    pe.wait_ge(s["last_ev"], 1)
                    pe.wait_ge(s["conv_done"], 1)
                    channel_mean(lambda c, at, w: ybuf[:, c, at:at + w] if at < T else
                                 smp(ybuf[:, c, :], CB + T, GE, 0, NS), "mean_mm")
                elif i == 2:
                    pe.wait_ge(s["sq2_done"], 1)
                    channel_mean(lambda c, at, w: ysq[:, c, at:at + w], "var_mm")
                elif i == NT - EARLY_CP:
                    pe.wait_ge(s["std_done"], 1)
                if NT - EARLY_CP <= i < NT:
                    turn_pages(i - (NT - EARLY_CP))
            pe.wait_ge(s["poolw_in"], 64)
            pe.wait_ge(s["pool_d"], 2)
            pe.wait_ge(s["kv_ev"], NT + 1)
            for c in range(2):
                for n, (at, w) in enumerate(chunks):
                    mm = pe.matmul(bank[POOL_BANKS[c][n]][:, 0:w], poolbd[:, c, :], dT[:, c, at:at + w], start=True, stop=True)
                mm.then_inc(s["pool_mm"], 1)
            for w in range(2):
                turn(("knew", w), [(0, TS, kvtok[0:TS, NT, 256 * (w + 1):256 * (w + 1) + P])])
            for ty in range(4):
                col = (0, 128, 256, 512)[ty]
                for hf in range(2):
                    turn(("kT", ty, hf), [(P * x, P, kvtok[:, 4 * hf + x, col:col + P]) for x in range(4)])
            pe.wait_ge(s["posr_in"], 64)
            for kv in range(2):
                turn(("pe", kv), [(0, 32, posr[:, kv, :])])
            for b in range(EARLY_CP, NB):
                turn_pages(b)
            pe.wait_ge(s["turn_drain"], nturn[0])
            for kv in range(2):
                srcT = cvT if kv else ckT
                for l in range(CBLK):
                    q = 4 * kv + l // 8
                    if l % 8 == 0:
                        pe.wait_ge(s[f"cmpw_in{q % 3}"], 32 * (q // 3 + 1))
                    mm = pe.matmul(bank[kv][:, 0:KC_N], cmpw[:, q % 3, l % 8, :],
                                   srcT[:, l:l + STRIDE * (KC_N - 1) + 1:STRIDE], start=(l == 0), stop=(l == CBLK - 1))
                    if l % 8 == 7:
                        mm.then_inc(s["cmpw_used"], 1)
            for G in range(2):
                mm = pe.matmul(bank[2 + G][:, 0:24], cpk[0:TS, C_SEL + P * G:C_SEL + P * G + P], kvtok[0:TS, NT, KVC:KVG],
                               start=True, stop=True)
            mm.then_inc(s["gate_mm"], 1)
            pe.wait_ge(s["cmp_ev"], 2)
            turn(("vc", 0), [(0, P, vcT[:, NB * 32:NB * 32 + NCMP])])
            for G in range(2):
                turn(("vc", 1 + G), [(0, P, vcT[:, P * G:P * G + P])])
            pe.wait_ge(s["turn_drain"], nturn[0])
            pe.wait_ge(s["gate_ev"], 1)
            pe.wait_ge(s["qbd_done"], 1)

            def score(j):
                i, br = SJOBS[j]
                sc = scores[j % 2]
                if j >= 2:
                    pe.wait_ge(s["exp_done"], j - 1)
                if br == 0:
                    mm = pe.matmul(sc[:, 0:P], qbd[:, i, :], kcT[:, P * i:P * i + P], start=True, stop=True)
                else:
                    pj = 2 * i + br - 1
                    pe.wait_ge(s[f"page_in{pj}"], 256 if br == 1 else 64)
                    for b in range(5):
                        if b < 4:
                            turn(("kp", j, b), [(P * x, P, page_slot(pj, b)[:, x, 0:P]) for x in range(NPG)])
                        if b >= 1:
                            kb = KUNIT[("kp", j, b - 1)]
                            pe.wait_ge(s["turn_drain"], UNIT[("kp", j, b - 1)] + 1)
                            r = slice(32 * (b - 1), 32 * b)
                            pe.matmul(sc[r, 0:PAST], qbd[:, i, r], kpT[kb % 2], start=True, stop=True
                                      ).then_inc(s["keys_used"], 1)
                            mm = pe.matmul(sc[r, PAST:PAST + TS], qbd[:, i, r], knewT[:, br - 1, :], start=True, stop=True)
                mm.then_inc(s["score_mm"], 1)

            def values(j, k):
                i, br = SJOBS[j]
                pu = PUNIT[("P", j, k)]
                pt = probT[pu % NPT]
                o = bank[6 + i]
                pe.wait_ge(s["turn_drain"], UNIT[("P", j, k)] + 1)
                if br == 0:
                    mm = pe.matmul(o[:, 0:P], pt[:, 0:P], vctok[:, 1 + i, :], start=True, stop=True)
                else:
                    for b in range(4):
                        r = slice(32 * b, 32 * b + 32)
                        ob = o[r, P * br:P * br + P]
                        if k == 0:
                            slot = page_slot(2 * i + br - 1, b)
                            for x in range(NPG):
                                mm = pe.matmul(ob, pt[:, P * x + 32 * b:P * x + 32 * b + 32], slot[:, x, P:2 * P],
                                               start=(x == 0), stop=False)
                        else:
                            c = 256 * br + P
                            mm = pe.matmul(ob, pt[0:TS, 32 * b:32 * b + 32], kvtok[0:TS, NT, c:c + P],
                                           start=False, stop=True)
                mm.then_inc(s["probT_used"], 1)

            def turn_out(o):
                pe.wait_ge(s["out_done"], 1 + o)
                turn(("o", o), [(0, P, osmp[o])])

            pend = []
            for j in range(-2, NSJ):
                if j + 2 < NSJ:
                    score(j + 2)
                if j < 0:
                    continue
                pe.wait_ge(s["exp_done"], j + 1)
                for k, grp in enumerate(s_groups(j)):
                    turn(("P", j, k), [(P * x, P, sprob[j % 2][:, c:c + n]) for x, (c, n) in enumerate(grp)])
                    if pend:
                        values(*pend.pop())
                    pend.append((j, k))
                if j == 3:
                    turn_out(0)
            values(*pend.pop())
            turn_out(1)

            def p_score(n, r):
                i, g, br = GROUPS[n]
                job = NSJ + GQ * n + r
                pe.wait_ge(s["exp_done"], job - 1)
                sc, w, gp = scores[job % 2], g_width(n), slice(HD * g, HD * g + HD)
                keys = kcT[gp, NB * 32:NB * 32 + w] if br == 0 else kslcT[gp, 0:w] if br == 1 else \
                    kwinT[gp, P * (i + 1) - w:P * (i + 1)]
                for c in range(0, w, 512):
                    mm = pe.matmul(sc[:, c:min(w, c + 512)], qT[gp, r, P * i:P * i + P], keys[:, c:min(w, c + 512)],
                                   start=True, stop=True)
                mm.then_inc(s["score_mm"], 1)

            def p_values(n, x):
                i, g, br = GROUPS[n]
                c, m = g_tiles(n)[x]
                pe.wait_ge(s["turn_drain"], UNIT[("t", n, x)] + 1)
                if x == 0 and br == 1 and g == 0 and i >= 2:
                    pe.wait_ge(s["o_ev"], i - 1)
                if br == 0:
                    v = vctok[0:m, 0, HD * g:HD * g + HD]
                else:
                    kt = c // P if br == 1 else i + 1 - g_width(n) // P + c // P
                    vc = 256 * br + P + HD * g
                    v = kvtok[:, kt, vc:vc + HD]
                mm = pe.matmul(bank[6 + i % 2][HD * g:HD * g + HD, :], v, probT[PUNIT[("t", n, x)] % NPT][0:m, :],
                               start=(x == 0 and br == 1), stop=(br == 0))
                mm.then_inc(s["probT_used"], 1)

            for scored, tiles in steps():
                if scored:
                    p_score(*scored)
                for n, x in tiles:
                    if x == 0:
                        pe.wait_ge(s["scaled"], GQ * (n + 1))
                    c, m = g_tiles(n)[x]
                    turn(("t", n, x), [(P * r, P, prob[(GQ * n + r) % SLOTS][:, c:c + m]) for r in range(GQ)])
                    if pend:
                        p_values(*pend.pop())
                    pend.append((n, x))
            p_values(*pend.pop())

            def unit(w, par, nk, mH, mL, free):
                pe.wait_ge(s["wL_done"], w + 1)
                for n, (at, cw) in enumerate(chunks):
                    free(n)
                    for k in range(nk):
                        for wt, mv in ((wH, mH), (wH, mL), (wL, mH)):
                            mm = pe.matmul(bank[3 * par + n][:, 0:cw], wt[:, par, k, :], mv[:, k, at:at + cw],
                                           start=(k == 0 and mv is mH and wt is wH), stop=(k == nk - 1 and wt is wL))
                mm.then_inc(s["unit_mm"], 1)

            def turn_back(u0, srcT, m):
                for q in range(3):
                    u = u0 + q
                    if u >= 2:
                        pe.wait_ge(s["x_add"], u - 1)
                    for x in range(3):
                        i = 3 * q + x
                        n = tile_rows(i)
                        mm = turn_tile(bank[6 + q0[0] % 2][0:n, P * x:P * x + P], srcT[:, P * i:P * i + n], P)
                    q0[0] += 1
                    mm.then_inc(s["back_turn"], 1)

            q0 = [0]
            pe.wait_ge(s["o_ev"], NT)
            pe.wait_ge(s["mixH_done"], KD)
            pe.wait_ge(s["mixL_done"], KD)
            for m in range(KD + 1):
                if m < KD:
                    unit(m, m % 2, KD, fH, fL, lambda n: pe.wait_ge(s["back_ev"], m - 1) if m >= 2 and n == 0 else None)
                if m >= 1:
                    pe.wait_ge(s["back_ev"], m)
                    turn_back(3 * (m - 1), backT[:, (m - 1) % 2, :], m - 1)
            turn_norm([xn2[:, 0, :], xn2[:, 1, :]], "xn3", "turn3", "evac3a", "evac3d")
            pe.wait_ge(s["evac3d"], NT + 1)

            def gu(f, w):
                for x in range(2 * FT):
                    F = f * FT + x // 2
                    if x % 2 == 0:
                        free = lambda n: pe.wait_ge(s["silu_done"], F * 3 + (n - 2)) if x == 2 else before(f, 6, n)
                    else:
                        free = lambda n: pe.wait_ge(s["hid_done"], F * 3 + (n - 2)) if x == 3 else before(f, 7, n)
                    unit(w + x, x % 2, KD, fH, fL, free)

            def before(f, m, n):
                if isinstance(f, int) and f == 0:
                    return
                if isinstance(f, int) and f == 1:
                    pe.wait_ge(s["silu_done" if m == 6 else "hid_done"], 3 * (FT - 1) + n + 1)
                else:
                    pe.wait_ge(s["y_add"], ((f - 2) * KD + m) * 3 + (n + 2))

            def dn(f, w):
                last = not isinstance(f, int) or f < NF - 1
                pe.wait_ge(s["aL_done"], (f + 1) * (3 * FT))
                par = dn_par[0] % 2
                dn_par[0] += 1
                for m in range(KD):
                    if m >= 2 or not last:
                        D_ = f * KD + (m - 2)
                        free = lambda n: pe.wait_ge(s["y_add"], D_ * 3 + (n + 2))
                    else:
                        F = f * FT + (2 * FT - 1)
                        free = lambda n: pe.wait_ge(s["silu_done" if m == 0 else "hid_done"], F * 3 + (n + 1))
                    unit(w + m, m % 2, FT, aH[:, par], aL[:, par], free)

            dn_par = [0]
            ffn_order(pe, gu, dn)
            for m in range(KD):
                pe.wait_ge(s["y_add"], 3 * (KD * (NF - 1) + m + 1) + 1)
                turn_back(3 * (KD + m), yT[:, m, :], m)

        @block.scalar
        def _(sc_):
            for i in range(NT + 1):
                n = tile_rows(i)
                sc_.wait_ge(s[f"x_in{i % 2}"], 16 * (i // 2 + 1))
                if i >= 1:
                    sc_.wait_ge(s["sq_done"], i)
                sc_.activation(sqjunk[0:n, :], xring[0:n, i % 2, :], ACT.Square, accum_out=stat[0:n, i:i + 1]
                               ).then_inc(s["sq_done"], 1)
                if i >= 1:
                    p = i - 1
                    sc_.wait_ge(s["turn_x"], p + 1)
                    sc_.copy(featT[:, 0:4, P * p:P * p + P], bank[2 * (p % 2)].rearrange("p (k t) -> p k t", k=4)
                             ).then_inc(s["evac_xa"], 1)
            sc_.wait_ge(s["turn_x"], NT + 1)
            sc_.copy(featT[:, 0:4, T:TT], bank[2 * (NT % 2)].rearrange("p (k t) -> p k t", k=4)[:, :, 0:TS]
                     ).then_inc(s["evac_xa"], 1)
            for m in range(NZ):
                if m in (1, 3):
                    continue
                sc_.wait_ge(s["z_mm"], m + 1)
                if m == 2:
                    sc_.wait_ge(s["glu_done"], 1)
                for n, (at, w) in enumerate(chunks):
                    b = bank[3 * (m % 2) + n]
                    if m in (0, 2):
                        op = sc_.activation(sig[:, at:at + w], b[:, 0:w], ACT.Sigmoid)
                    elif m < len(ZTILES):
                        for lo, hi, dst in ext_cols(uex, m - 4, at, w, PB, UE, PB):
                            srcap = b[:, lo:hi]
                            if lo:
                                srcap = srcap.rearrange("p (b t) -> p b t", t=NS)
                            op = sc_.copy(dst, srcap)
                    else:
                        op = sc_.mul(qT[:, m - len(ZTILES), at:at + w], b[:, 0:w], HD ** -0.5)
                op.then_inc(s["sig_done" if m in (0, 2) else "zc_done"], 1)
                if m == 8:
                    sc_.wait_ge(s["last_turn"], 1)
                    sc_.wait_ge(s["state_turn"], 1)
                    sc_.copy(lastT[0:30, 0, :], bank[6][0:30, 0:256])
                    sc_.copy(lastT[0:15, 1, :], bank[6][0:15, 256:512])
                    sc_.copy(lastT[:, 2:4, :], bank[7][0:TS, :].rearrange("p (k n) -> p k n", k=2)).then_inc(s["last_ev"], 1)
            hk = KVG // 2
            nturn = [0]

            def drain(key, copies):
                u = UNIT[key]
                assert u == nturn[0]
                nturn[0] += 1
                sc_.wait_ge(s["turn_fill"], u + 1)
                for dst, srcfn in copies:
                    op = sc_.copy(dst, srcfn(bank[4 + u % 2]))
                op.then_inc(s["turn_drain"], 1)

            def drain_pages(b_):
                for kv in range(2):
                    drain(("cp", b_, kv), [((cvT if kv else ckT)[:, PAST * b_:PAST * b_ + PAST], lambda b: b)])

            for i in range(NT + 1):
                n = tile_rows(i)
                sc_.wait_ge(s["kv_mm"], i + 1)
                for hf in range(2):
                    op = sc_.copy(kvtok[0:n, i, hk * hf:hk * hf + hk], bank[2 * (i % 2) + hf][0:n, 0:hk])
                op.then_inc(s["kv_ev"], 1)
                if i == 1:
                    sc_.wait_ge(s["yc_done"], 1)
                    for c in range(2):
                        op = sc_.activation(ysq[:, c, :], yc[:, c, :], ACT.Square)
                    op.then_inc(s["sq2_done"], 1)
                elif i == 2:
                    sc_.wait_ge(s["var_mm"], 1)
                    sc_.wait_ge(s["prep"], 1)
                    for k, (at, w) in enumerate(lnchunks):
                        op = sc_.activation(ystd[:, at:at + w], bank[4 + k][:, 0:w], ACT.Sqrt, bias=epsc)
                    op.then_inc(s["std_done"], 1)
                elif i == NT - EARLY_CP:
                    sc_.wait_ge(s["yc_done"], 1)
                    sc_.wait_ge(s["newcols_done"], 1)
                    sc_.wait_ge(s["pool_d"], 2)
                    sc_.wait_ge(s["last_out"], 16 * LASTS)
                if NT - EARLY_CP <= i < NT:
                    drain_pages(i - (NT - EARLY_CP))
            sc_.wait_ge(s["kv_ev"], NT + 1)
            sc_.wait_ge(s["norm_done"], 2)
            sc_.wait_ge(s["chan_in"], 96)
            for c in range(2):
                sc_.activation(featT[:, c, :], yc[:, c, :], ACT.Silu, bias=lnb[:, c:c + 1], scale=lng[:, c:c + 1]
                               ).then_inc(s["mix_done"], 1)
            for c in range(2):
                sc_.wait_ge(s["pool_mm"], c + 1)
                for n, (at, w) in enumerate(chunks):
                    op = sc_.activation(featT[:, 2 + c, at:at + w], bank[POOL_BANKS[c][n]][:, 0:w], ACT.Copy,
                                        scale=pscale[:, c:c + 1])
                op.then_inc(s["mix_done"], 1)
            sc_.activation(kvtok[:, 0:NT, KVC:KVG], kvtok[:, 0:NT, KVC:KVG], ACT.Sigmoid).then_inc(s["gates_done"], 1)
            sc_.activation(kvtok[0:TS, NT, KVC:KVG], kvtok[0:TS, NT, KVC:KVG], ACT.Sigmoid).then_inc(s["gates_done"], 1)

            for w in range(2):
                drain(("knew", w), [(knewT[:, w, :], lambda b: b[:, 0:TS])])
            for ty in range(4):
                for hf in range(2):
                    dst = (ckT[:, NB * PAST:], cvT[:, NB * PAST:], kslcT, kwinT)[ty]
                    drain(("kT", ty, hf), [(dst[:, 512 * hf:512 * hf + 512], lambda b: b)])
            for kv in range(2):
                drain(("pe", kv), [((cvT if kv else ckT)[:, KC_L - 32:KC_L], lambda b: b[:, 0:32])])
            for b_ in range(EARLY_CP, NB):
                drain_pages(b_)
            drain(("vc", 0), [(vctok[0:NCMP, 0, :], lambda b: b[0:NCMP, 0:P])])
            for G in range(2):
                drain(("vc", 1 + G), [(vctok[:, 1 + G, :], lambda b: b[:, 0:P])])

            def drain_keys(j):
                for b_ in range(4):
                    kb = KUNIT[("kp", j, b_)]
                    if kb >= 2:
                        sc_.wait_ge(s["keys_used"], kb - 1)
                    drain(("kp", j, b_), [(kpT[kb % 2], lambda b: b)])

            def drain_prob(j, k):
                pu = PUNIT[("P", j, k)]
                if pu >= NPT:
                    sc_.wait_ge(s["probT_used"], pu - NPT + 1)
                grp = s_groups(j)[k]
                n, w = grp[0][1], P * len(grp)
                drain(("P", j, k), [(probT[pu % NPT][0:n, 0:w], lambda b: b[0:n, 0:w])])

            def expo(j):
                G, br = SJOBS[j]
                sc_.wait_ge(s["score_in"], j + 1)
                if j >= 2:
                    sc_.wait_ge(s["turn_fill"], UNIT[("P", j - 2, len(s_groups(j - 2)) - 1)] + 1)
                sc_.activation(sprob[j % 2][:, 0:s_width(j)], scores[j % 2][:, 0:s_width(j)], ACT.Exp,
                               bias=nmax[:, j % 2:j % 2 + 1], accum_out=sums[G][:, br:br + 1]).then_inc(s["exp_done"], 1)

            def drain_out(o):
                copies = []
                for g in range(KVH):
                    gp = slice(HD * g, HD * g + HD)
                    dst = featT[gp, 4:8, T + 16 * o:T + 16 * o + 16].rearrange("p r (b t) -> p b r t", t=NS)
                    copies.append((dst, lambda b, gp=gp, g=g: b[gp, 0:P].rearrange(
                        "p (b g r t) -> p b g r t", b=4, g=KVH, r=GQ)[:, :, g]))
                drain(("o", o), copies)

            for j in range(-2, NSJ):
                if j + 2 < NSJ and SJOBS[j + 2][1] > 0:
                    drain_keys(j + 2)
                if j < 0:
                    if j == -1:
                        expo(0)
                    continue
                for k in range(len(s_groups(j))):
                    drain_prob(j, k)
                    if k == 0 and j + 1 < NSJ:
                        expo(j + 1)
                if j == 3:
                    drain_out(0)
            drain_out(1)

            def p_exp(n, r):
                job = NSJ + GQ * n + r
                w = g_width(n)
                sc_.wait_ge(s["score_in"], job + 1)
                if n > LAG:
                    old = n - LAG - 1
                    sc_.wait_ge(s["turn_fill"], UNIT[("t", old, len(g_tiles(old)) - 1)] + 1)
                if r == 0 and n >= 2:
                    sc_.wait_ge(s["rec_done"], n - 1)
                elif r == 0:
                    sc_.wait_ge(s["out_done"], 2)
                sc_.activation(prob[(GQ * n + r) % SLOTS][:, 0:w], scores[job % 2][:, 0:w], ACT.Exp,
                               bias=nmax[:, job % 2:job % 2 + 1], accum_out=sums[n % 2][:, r:r + 1]).then_inc(s["exp_done"], 1)

            def out_tile(i):
                last = [k for k in PUNIT if k[0] == "t" and GROUPS[k[1]][0] == i][-1]
                sc_.wait_ge(s["probT_used"], PUNIT[last] + 1)
                sc_.copy(featT[:, 4:8, P * i:P * i + P], bank[6 + i % 2].rearrange("p (r t) -> p r t", r=GQ)
                         ).then_inc(s["o_ev"], 1)

            late_exp, done_tile = None, 0
            for scored, tiles in steps():
                if late_exp:
                    p_exp(*late_exp)
                late_exp = scored
                for n, x in tiles:
                    i = GROUPS[n][0]
                    if i > done_tile and (x >= 1 or n != 6 * i):
                        out_tile(done_tile)
                        done_tile += 1
                    pu = PUNIT[("t", n, x)]
                    m = g_tiles(n)[x][1]
                    sc_.wait_ge(s["probT_used"], pu - NPT + 1)
                    drain(("t", n, x), [(probT[pu % NPT][0:m, :], lambda b: b[0:m, :])])
            out_tile(NT - 1)

            def round_w(w, par, nk):
                sc_.wait_ge(s[f"raw_in{par}"], half(w, par) * 48 + 48)
                if not (isinstance(w, int) and w < 2):
                    sc_.wait_ge(s["unit_mm"], w - 1)
                sc_.copy(wH[:, par, 0:nk, :], wraw[:, par, 0:nk, :]).then_inc(s["wH_done"], 1)

            def squares(base):
                sc_.wait_ge(s["x_add"], 3 * KD * base)
                for i in range(NT + 1):
                    n = tile_rows(i)
                    at = (NT + 1) * (base - 1) + i
                    if at:
                        sc_.wait_ge(s["sq3"], at)
                    sc_.activation(sqb2[base - 1][0:n, :], xt[0:n, i, :], ACT.Square, accum_out=stat[0:n, i:i + 1]
                                   ).then_inc(s["sq3"], 1)

            sqb2 = [aH_sq, sqb]
            sc_.wait_ge(s["stores"], 16 * STORES)
            for k in range(KD):
                sc_.copy(fH[:, k, :], featT[:, k, :]).then_inc(s["mixH_done"], 1)
                if k == 0:
                    round_w(0, 0, KD)
            for m in range(KD):
                round_w(m + 1, (m + 1) % 2, KD)
                sc_.wait_ge(s["unit_mm"], m + 1)
                if m >= 2:
                    sc_.wait_ge(s["back_turn"], 3 * (m - 1))
                for n, (at, w) in enumerate(chunks):
                    op = sc_.copy(backT[:, m % 2, at:at + w], bank[3 * (m % 2) + n][:, 0:w])
                op.then_inc(s["back_ev"], 1)
            squares(1)
            for i in range(NT + 1):
                n = tile_rows(i)
                sc_.wait_ge(s["turn3"], i + 1)
                for hf in range(2):
                    op = sc_.copy(fH[:, 4 * hf:4 * hf + 4, P * i:P * i + n],
                                  bank[2 * (i % 2) + hf].rearrange("p (k t) -> p k t", k=4)[:, :, 0:n])
                op.then_inc(s["evac3a"], 1)

            def gu(f, w):
                par = gu_par[0] % 2
                gu_par[0] += 1
                for x in range(2 * FT):
                    F = f * FT + x // 2
                    nxt_dn = x == 2 * FT - 1 and not (isinstance(f, int) and f == 0)
                    round_w(w + (x + 1), (x + 1) % 2, FT if nxt_dn else KD)
                    sc_.wait_ge(s["unit_mm"], w + (x + 1))
                    for n in range(3):
                        if x % 2 == 0:
                            if not (isinstance(f, int) and f == 0 and x == 0):
                                sc_.wait_ge(s["aL_done"], F * 3 + (n - 2))
                            sc_.activation(hid[:, n, :], bank[n][:, 0:NCH], ACT.Silu).then_inc(s["silu_done"], 1)
                        else:
                            sc_.wait_ge(s["hid_done"], F * 3 + (n + 1))
                            at, cw = chunks[n]
                            sc_.copy(aH[:, par, x // 2, at:at + cw], hid[:, n, :]).then_inc(s["aH_done"], 1)

            def dn(f, w):
                for m in range(KD):
                    if m < KD - 1:
                        round_w(w + (m + 1), (m + 1) % 2, FT)
                    elif not isinstance(f, int) or f < NF - 3 + 1:
                        round_w(w + KD, 0, KD)
                    elif f < NF - 1:
                        round_w(w + KD, 0, FT)

            gu_par = [0]
            ffn_order(sc_, gu, dn)
            squares(2)

        @block.vector
        def _(dve):
            chain = [0]

            def link(op):
                chain[0] += 1
                op.then_inc(s["dve"], 1)
                dve.wait_ge(s["dve"], chain[0])

            dve.memset(mhalf, -0.5)
            dve.memset(epsc, EPS)
            dve.memset(avg[:, :], 1.0 / CONV_W)
            dve.memset(rbias[32:33, :], 1.0).then_inc(s["prep"], 1)
            dve.wait_ge(s["table_mm"], 1)
            dve.tensor_copy(fvec, bank[0][0:NH, 0:BAND]).then_inc(s["fvec_ev"], 1)
            dve.wait_ge(s["table_mm"], 2)
            dve.tensor_copy(ctab[:, :, :], bank[1][:, 0:CMPN * NH].rearrange("p (c h) -> p h c", h=NH)
                            ).then_inc(s["table_ev"], 1)
            dve.wait_ge(s["table_mm"], 3)
            dve.tensor_copy(stab[:, 0:128], bank[2][:, 0:128])
            for G in range(2):
                dve.tensor_tensor(stab[:, 128 + 32 * G:160 + 32 * G], bank[2][:, 128:160],
                                  cpk[:, C_MN + 32 * G:C_MN + 32 * G + 32], ALU.add)
            dve.tensor_tensor(stab[:, 192:320], bank[2][:, 160:288], cpk[:, C_MC:C_MC + 128], ALU.add
                              ).then_inc(s["table_ev"], 1)
            dve.wait_ge(s["state_turn"], 1)
            for c in range(2):
                for k in range(2):
                    dst = smp(glu[:, c, :], CB + T, GE, 0, CB)[:, 4 * k:4 * k + 4]
                    q = 120 * (2 * k + c)
                    op = dve.tensor_copy(dst, bank[6][:, q:q + 120].rearrange("p (b t) -> p b t", t=CB))
            op.then_inc(s["state_ev"], 1)
            for c in range(2):
                op = dve.tensor_copy(smp(uex[:, c, :], PB + T, UE, 0, PB), bank[7][:, 120 * c:120 * c + 120].rearrange(
                    "p (b t) -> p b t", t=PB))
            op.then_inc(s["state_ev"], 1)

            def norm(xs, outs, sq_, ms_, rs_, xn_, filled, evd, gain, base, free):
                for i in range(NT + 2):
                    n = tile_rows(i)
                    if i <= NT:
                        dve.wait_ge(s[sq_], base + i + 1)
                        dve.tensor_scalar(ms[0:n, i:i + 1], stat[0:n, i:i + 1], 1.0 / D, EPS, ALU.mult, ALU.add
                                          ).then_inc(s[ms_], 1)
                    if i >= 1 and filled:
                        p, n1 = i - 1, tile_rows(i - 1)
                        dve.wait_ge(s[filled], p + 1)
                        if callable(evd):
                            evd(p)
                        else:
                            dve.tensor_copy(featT[:, 4:8, P * p:P * p + n1],
                                            bank[2 * (p % 2) + 1].rearrange("p (k t) -> p k t", k=4)[:, :, 0:n1]
                                            ).then_inc(s[evd], 1)
                    if i <= NT:
                        dve.wait_ge(s[rs_], base + i + 1)
                        if i == 0:
                            dve.wait_ge(s[gain], 16)
                        free(i)
                        dve.scalar_tensor_tensor(out=outs[i % 2][0:n, :], in0=xs(i)[0:n, :], scalar=rstd[0:n, i:i + 1],
                                                 in1=gB[0:n, :], op0=ALU.mult, op1=ALU.mult).then_inc(s[xn_], 1)

            norm(lambda i: xring[:, i % 2, :], xn, "sq_done", "ms_done", "rstd_done", "xn_done", "turn_x", "evac_xd",
                 "gain_in", 0, lambda i: dve.wait_ge(s["turn_x"], i - 1) if i >= 2 else None)
            for c in range(2):
                dve.wait_ge(s["sig_done"], c + 1)
                dve.wait_ge(s["z_mm"], 2 * c + 2)
                for n, (at, w) in enumerate(chunks):
                    for lo, hi, dst in ext_cols(glu, c, at, w, CB, GE, CB):
                        a, b = bank[3 + n][:, lo:hi], sig[:, at + lo:at + hi]
                        if lo:
                            a, b = (v.rearrange("p (b t) -> p b t", t=NS) for v in (a, b))
                        op = dve.tensor_tensor(dst, a, b, ALU.mult)
                op.then_inc(s["glu_done"], 1)
            dve.wait_ge(s["glu_done"], 2)
            dve.wait_ge(s["chan_in"], 96)
            dve.wait_ge(s["pzero"], 1)
            dve.wait_ge(s["turn_x"], NT + 1)
            for k in range(CW):
                for c in range(2):
                    y, x, w = ybuf[:, c, 0:Y_L], glu[:, c, k:k + Y_L], convw[:, c, k:k + 1]
                    if k == 0:
                        op = dve.tensor_scalar(y, x, w, convb[:, c:c + 1], ALU.mult, ALU.add)
                    else:
                        dve.wait_ge(s["dve"], chain[0] - 1)
                        op = dve.scalar_tensor_tensor(out=y, in0=x, scalar=w, in1=y, op0=ALU.mult, op1=ALU.add)
                    chain[0] += 1
                    op.then_inc(s["dve"], 1)
            dve.wait_ge(s["dve"], chain[0])
            dve.engine_nop().then_inc(s["conv_done"], 1)
            dve.wait_ge(s["mean_mm"], 1)
            for n, (at, w) in enumerate(lnchunks):
                for c in range(2):
                    y, b, o = ybuf[:, c, at:at + w], bank[4 + n][:, 0:w], yc[:, c, at:at + w]
                    if at == T:
                        y = smp(ybuf[:, c, :], CB + T, GE, 0, NS)
                        b, o = (v.rearrange("p (b t) -> p b t", t=NS) for v in (b, o))
                    op = dve.tensor_tensor(o, y, b, ALU.subtract)
            op.then_inc(s["yc_done"], 1)
            dve.wait_ge(s["std_done"], 1)
            link(dve.reciprocal(ystd, ystd))
            for c in range(2):
                dve.tensor_tensor(yc[:, c, :], yc[:, c, :], ystd, ALU.mult).then_inc(s["norm_done"], 1)
            for c in range(2):
                dve.wait_ge(s["pairsum"], c + 1)
                for hp in range(2):
                    r = slice(HD * hp, HD * hp + HD)
                    S = pl[r, hp, :]
                    link(dve.tensor_tensor(S[:, PB:2 * PB], S[:, PB:2 * PB], cpk[r, C_FX + PB * c:C_FX + PB * c + PB], ALU.mult))
                    dve.scalar_tensor_tensor(out=dT[r, c, 0:T], in0=S[:, PB:PB + T], scalar=cpk[r, C_IW + c:C_IW + c + 1],
                                             in1=uex[r, c, PB:PB + T], op0=ALU.mult, op1=ALU.subtract)
                    op = dve.scalar_tensor_tensor(
                        out=dT[r, c, T:TT].rearrange("p (b t) -> p b t", t=NS), in0=smp(S, PB + T, UE, PB, NS),
                        scalar=cpk[r, C_IW + c:C_IW + c + 1], in1=smp(uex[r, c, :], PB + T, UE, PB, NS),
                        op0=ALU.mult, op1=ALU.subtract)
                op.then_inc(s["pool_d"], 1)
            dve.wait_ge(s["gates_done"], 1)
            dve.tensor_scalar(kvtok[:, 0, KVC:KVC + NH], kvtok[:, 0, KVC:KVC + NH], cpk[:, C_VA:C_VA + 1], None, ALU.mult
                              ).then_inc(s["valid_done"], 1)
            for kv, dst in ((0, kcT), (1, vcT)):
                dve.wait_ge(s["cmpw_used"], 4 * (kv + 1))
                if kv == 0:
                    dve.wait_ge(s["late_zero"], 2)
                link(dve.tensor_copy(posk[:, kv:kv + 1], bank[kv][:, KC_N - 1:KC_N]))
                dve.tensor_scalar(dst[:, :], bank[kv][:, 0:KC_N - 1], posk[:, kv:kv + 1], None, ALU.add
                                  ).then_inc(s["cmp_ev"], 1)
            dve.wait_ge(s["gate_mm"], 1)
            for G in range(2):
                link(dve.tensor_tensor(gjunk[:, 24 * G:24 * G + 24], bank[2 + G][:, 0:24], cpk[:, C_GM:C_GM + 24], ALU.mult))
                op = dve.tensor_reduce(sgate[:, 3 * G:3 * G + 3], gjunk[:, 24 * G:24 * G + 24].rearrange(
                    "p (a h) -> p a h", h=NH), AX, ALU.add)
            op.then_inc(s["gate_ev"], 1)
            dve.wait_ge(s["gate_ev"], 1)
            dve.wait_ge(s["btab_in"], 16)
            dve.wait_ge(s["tri_in"], 16)

            def biased_max(job, w, adds):
                sc = scores[job % 2]
                dve.wait_ge(s["score_mm"], job + 1)
                for at, tab in adds:
                    n = tab.free_size()
                    op = dve.tensor_tensor(sc[:, at:at + n], sc[:, at:at + n], tab, ALU.add)
                link(op)
                if job >= 2:
                    dve.wait_ge(s["exp_done"], job - 1)
                dve.tensor_reduce(nmax[:, job % 2:job % 2 + 1], sc[:, 0:w], AX, ALU.max, negate=True
                                  ).then_inc(s["score_in"], 1)

            def s_biased_max(j):
                G, br = SJOBS[j]
                if br == 0:
                    adds = [(0, stab[:, 192:320])]
                else:
                    adds = [(384, stab[:, 0:128]), (512, stab[:, 128 + 32 * G:160 + 32 * G])]
                    if br == 2:
                        adds.append((0, cpk[:, C_MW:C_MW + 4]))
                biased_max(j, s_width(j), adds)

            def finish(G):
                su, rc, o, dst = sums[G][:, 0:3], rec[G][:, 0:3], bank[6 + G], osmp[G]
                dve.wait_ge(s["exp_done"], 3 * G + 3)
                link(dve.reciprocal(rc, su))
                link(dve.tensor_tensor(rc, rc, sgate[:, 3 * G:3 * G + 3], ALU.mult))
                dve.wait_ge(s["probT_used"], PUNIT[("P", 3 * G + 2, 1)] + 1)
                link(dve.tensor_scalar(dst, o[:, 0:P], rc[:, 0:1], None, ALU.mult))
                link(dve.scalar_tensor_tensor(out=dst, in0=o[:, P:2 * P], scalar=rc[:, 1:2], in1=dst, op0=ALU.mult, op1=ALU.add))
                dve.scalar_tensor_tensor(out=dst, in0=o[:, 2 * P:3 * P], scalar=rc[:, 2:3], in1=dst, op0=ALU.mult,
                                         op1=ALU.add).then_inc(s["out_done"], 1)

            for j in range(-2, NSJ):
                if j + 2 < NSJ:
                    s_biased_max(j + 2)
                if j == 3:
                    finish(0)
            finish(1)

            def p_biased_max(n, r):
                i, g, br = GROUPS[n]
                w, h = g_width(n), GQ * g + r
                if br == 0:
                    m = min(w, CMPN)
                    adds = [(w - m, ctab[:, h, CMPN - m:])]
                else:
                    m = min(w, 256)
                    adds = [(w - m, btab[:, h, 256 - m:])]
                    if br == 2 and i >= 4:
                        adds.append((0, tri[:, :]))
                biased_max(NSJ + GQ * n + r, w, adds)

            def scale(n, r):
                i, g, br = GROUPS[n]
                rc = rec[n % 2]
                if r == 0:
                    dve.wait_ge(s["exp_done"], NSJ + GQ * (n + 1))
                    chain[0] += 1
                    dve.reciprocal(rc, sums[n % 2]).then_inc(s["rec_done"], 1)
                    dve.wait_ge(s["rec_done"], n + 1)
                    c = KVC + NH * br + GQ * g
                    link2(dve.tensor_tensor(rc, rc, kvtok[:, i, c:c + GQ], ALU.mult))
                w = g_width(n)
                p = prob[(GQ * n + r) % SLOTS][:, 0:w]
                dve.tensor_scalar(p, p, rc[:, r:r + 1], None, ALU.mult).then_inc(s["scaled"], 1)

            def link2(op):
                op.then_inc(s["dve"], 1)
                dve.wait_ge(s["dve"], chain[0])

            for scored, _ in steps():
                if scored:
                    p_biased_max(*scored)
                    n, r = scored
                if scored and n >= 1:
                    scale(n - 1, r)
            for r in range(GQ):
                scale(NG - 1, r)

            def rest_w(w, par, nk):
                dve.wait_ge(s["wH_done"], w + 1)
                dve.tensor_tensor(wL[:, par, 0:nk, :], wraw[:, par, 0:nk, :], wH[:, par, 0:nk, :].bitcast(F32), ALU.subtract
                                  ).then_inc(s["wL_done"], 1)

            def add_back(u0, m, par):
                cols = slice(P * m, P * m + P)
                for q in range(3):
                    dve.wait_ge(s["back_turn"], u0 + q + 1)
                    b = bank[6 + (u0 + q) % 2].rearrange("p (x n) -> p x n", n=P)
                    k = 3 if q < 2 else 2
                    x = xt[:, 3 * q:3 * q + k, cols]
                    op = dve.tensor_tensor(x, x, b[:, 0:k], ALU.add)
                    if q == 2:
                        op = dve.tensor_tensor(xt[0:TS, NT, cols], xt[0:TS, NT, cols], b[0:TS, 2], ALU.add)
                    op.then_inc(s["x_add"], 1)

            for k in range(KD):
                dve.wait_ge(s["mixH_done"], k + 1)
                dve.tensor_tensor(fL[:, k, :], featT[:, k, :], fH[:, k, :].bitcast(F32), ALU.subtract
                                  ).then_inc(s["mixL_done"], 1)
                if k == 0:
                    rest_w(0, 0, KD)
            dve.wait_ge(s["x2_in"], 16 * (NT + 1))
            for m in range(KD + 1):
                rest_w_at = m + 1
                if m < KD:
                    rest_w(rest_w_at, rest_w_at % 2, KD)
                if m >= 1:
                    add_back(3 * (m - 1), m - 1, 0)
            dve.wait_ge(s["x_add"], 3 * KD)

            def rest_norm(i):
                n = tile_rows(i)
                dve.wait_ge(s["evac3a"], i + 1)
                for hf in range(2):
                    o = (slice(None), slice(4 * hf, 4 * hf + 4), slice(P * i, P * i + n))
                    op = dve.tensor_tensor(fL[o], bank[2 * (i % 2) + hf].rearrange("p (k t) -> p k t", k=4)[:, :, 0:n],
                                           fH[o].bitcast(F32), ALU.subtract)
                op.then_inc(s["evac3d"], 1)

            norm(lambda i: xt[:, i, :], [xn2[:, 0, :], xn2[:, 1, :]], "sq3", "ms3", "rstd3", "xn3", "turn3", rest_norm,
                 "gain2_in", 0, lambda i: dve.wait_ge(s["turn3"], i - 1) if i >= 2 else None)

            def gu(f, w):
                par = gu_par[0] % 2
                gu_par[0] += 1
                for x in range(2 * FT):
                    F = f * FT + x // 2
                    nxt_dn = x == 2 * FT - 1 and not (isinstance(f, int) and f == 0)
                    rest_w(w + (x + 1), (x + 1) % 2, FT if nxt_dn else KD)
                    if x % 2 == 0:
                        continue
                    dve.wait_ge(s["unit_mm"], w + (x + 1))
                    for y in range(4):
                        if y < 3:
                            dve.wait_ge(s["silu_done"], F * 3 + (y + 1))
                            dve.tensor_tensor(hid[:, y, :], bank[3 + y][:, 0:NCH], hid[:, y, :], ALU.mult
                                              ).then_inc(s["hid_done"], 1)
                        if y >= 1:
                            n = y - 1
                            at, cw = chunks[n]
                            dve.wait_ge(s["aH_done"], F * 3 + (n + 1))
                            dve.tensor_tensor(aL[:, par, x // 2, at:at + cw], hid[:, n, :],
                                              aH[:, par, x // 2, at:at + cw].bitcast(F32), ALU.subtract).then_inc(s["aL_done"], 1)

            def dn(f, w):
                for m in range(KD):
                    if m < KD - 1:
                        rest_w(w + (m + 1), (m + 1) % 2, FT)
                    elif not isinstance(f, int) or f < NF - 3 + 1:
                        rest_w(w + KD, 0, KD)
                    elif f < NF - 1:
                        rest_w(w + KD, 0, FT)
                    dve.wait_ge(s["unit_mm"], w + (m + 1))
                    dve.wait_ge(s["y_add"], (f * KD + m) * 3 + 1)
                    for n, (at, cw) in enumerate(chunks):
                        y = yT[:, m, at:at + cw]
                        dve.tensor_tensor(y, y, bank[3 * (m % 2) + n][:, 0:cw], ALU.add).then_inc(s["y_add"], 1)

            gu_par = [0]
            ffn_order(dve, gu, dn)
            for m in range(KD):
                add_back(3 * (KD + m), m, 0)
            dve.wait_ge(s["x_add"], 6 * KD)
            norm(lambda i: xt[:, i, :], yo, "sq3", "ms3", "rstd3", "y_done", None, None, "gain3_in", NT + 1,
                 lambda i: dve.wait_ge(s[f"y_out{i % 2}"], 16 * (i // 2)) if i >= 2 else None)

        @block.gpsimd
        def _(pool):
            nst = [0]

            def store(dst, src_):
                nst[0] += 1
                pool.dma_start(dst, src_).then_inc(s["stores"], 16)

            for c in range(2):
                pool.memset(glu[:, c, 0:CB], 0.0)
                pool.memset(uex[:, c, 0:PB], 0.0)
            pool.memset(poolbd[:, :, :], 0.0).then_inc(s["pzero"], 1)
            pool.memset(tsel, 0.0).then_inc(s["pool"], 1)
            pool.wait_ge(s["table_in"], 96)
            pool.wait_ge(s["pool"], 1)
            ts = tsel.rearrange("p (b h t) -> p b h t", b=4, h=NH)
            for t in range(NS):
                r = slice(32 * t, 32 * t + 32)
                for b in range(4):
                    op = pool.tensor_copy(ts[r, b, :, t], rbias4[r, :])
            op.then_inc(s["tsel_done"], 1)
            pool.wait_ge(s["fvec_ev"], 1)
            pool.dma_start(scratch.ap(), fvec[:, None, :].to_broadcast([NH, P, BAND])).then_inc(s["fvec_out"], 16)

            def rstds(ms_, rs_, base):
                pool.wait_ge(s["prep"], 1)
                for i in range(NT + 1):
                    n = tile_rows(i)
                    pool.wait_ge(s[ms_], base + i + 1)
                    pool.tensor_tensor(rstd[0:n, i:i + 1], ms[0:n, i:i + 1], mhalf[0:n, :], ALU.pow).then_inc(s[rs_], 1)

            rstds("ms_done", "rstd_done", 0)
            store(out["new_win_sample"][:, 0:WINDOW - NS], A["cache_win_kv"][0].rearrange("b t a g d -> b t (a g d)")[:, NS:])
            store(out["new_conv_sample"][:, 0:CB - NS], A["state_conv"][0][:, NS:])
            store(out["new_pool_sample"][:, 0:PB - NS], A["state_pool"][0][:, NS:])
            pool.wait_ge(s["zc_done"], 2)
            pool.wait_ge(s["state_ev"], 2)
            pool.wait_ge(s["glu_done"], 2)
            step = [1]
            for c in range(2):
                for k, src_ in ((c, smp(glu[:, c, :], CB + T, GE, CB, NS)), (2 + c, smp(uex[:, c, :], PB + T, UE, PB, NS))):
                    op = pool.tensor_copy(newcols[:, k, :].rearrange("p (b t) -> p b t", t=NS), src_)
            op.then_inc(s["newcols_done"], 1)

            def plink(op):
                step[0] += 1
                op.then_inc(s["pool"], 1)
                pool.wait_ge(s["pool"], step[0])

            a, b, hi = pl[:, 0, :], pl[:, 1, :], slice(HD, P)
            for c in range(2):
                if c:
                    pool.wait_ge(s["pool_d"], 1)
                u = uex[:, c, :]
                plink(pool.tensor_tensor(a[:, 1:], u[:, 1:], u[:, :-1], ALU.add))
                if c == 0:
                    pool.tensor_tensor(b[hi, 3:], a[hi, 3:], a[hi, 1:-2], ALU.add).then_inc(s["pairsum"], 1)
                    pool.wait_ge(s["last_ev"], 1)
                    pool.dma_start(out["new_conv_prompt"], lastT[0:CB, 0, :]).then_inc(s["last_out"], 16)
                    pool.dma_start(out["new_pool_prompt"], lastT[0:PB, 1, :]).then_inc(s["last_out"], 16)
                    for b_ in range(NB):
                        r = slice(NS * b_, NS * b_ + NS)
                        pool.dma_start(out["new_conv_sample"][b_, CB - NS:], lastT[r, 2, :]).then_inc(s["last_out"], 16)
                        pool.dma_start(out["new_pool_sample"][b_, PB - NS:], lastT[r, 3, :]).then_inc(s["last_out"], 16)
                else:
                    plink(pool.tensor_tensor(b[:, 3:], a[:, 3:], a[:, 1:-2], ALU.add))
                    plink(pool.tensor_tensor(a[:, 7:], b[:, 7:], b[:, 3:-4], ALU.add))
                    pool.tensor_tensor(b[hi, 15:], a[hi, 15:], a[hi, 7:-8], ALU.add).then_inc(s["pairsum"], 1)
            pool.wait_ge(s["pairsum"], 2)
            pool.memset(qbd[:, :, :], 0.0).then_inc(s["late_zero"], 1)
            pool.wait_ge(s["kv_mm"], NT + 1)
            pool.wait_ge(s["pool_mm"], 2)
            pool.memset(cmpw[:, :, :, :], 0.0).then_inc(s["late_zero"], 1)
            pool.wait_ge(s["late_zero"], 2)
            for g in range(KVH):
                gp = slice(HD * g, HD * g + HD)
                for G in range(2):
                    for b_ in range(4):
                        dst = qbd[gp, G, 32 * b_ + 16 * g:32 * b_ + 16 * g + 16].rearrange("p (r t) -> p r t", t=NS)
                        at = T + 16 * G + NS * b_
                        op = pool.tensor_copy(dst, qT[gp, :, at:at + NS])
            op.then_inc(s["qbd_done"], 1)
            pool.wait_ge(s["kv_ev"], NT + 1)
            for br, name in ((0, "cmp"), (1, "slc")):
                store(out[f"new_{name}_prompt"].rearrange("(i p) n -> p i n", p=P), kvtok[:, 0:NT, 256 * br:256 * br + 256])
                store(out[f"new_{name}_sample"], kvtok[0:TS, NT, 256 * br:256 * br + 256])
            store(out["new_win_prompt"].rearrange("(i p) n -> p i n", p=P), kvtok[:, NT - WINDOW // P:NT, 512:768])
            for b_ in range(NB):
                store(out["new_win_sample"][b_, WINDOW - NS:], kvtok[NS * b_:NS * b_ + NS, NT, 512:768])
            assert nst[0] == STORES
            rstds("ms3", "rstd3", 0)
            pool.wait_ge(s["mixL_done"], KD)
            pool.wait_ge(s["sq3"], NT + 1)
            pool.memset(yT[:, :, :], 0.0).then_inc(s["y_add"], 1)
            rstds("ms3", "rstd3", NT + 1)


STORES = 3 + 4 + 1 + NB
LASTS = 2 + 2 * NB
NPHYS = 40

_INS = ["x_prompt", "x_sample", "cache_cmp_kv", "cache_slc_kv", "cache_win_kv", "state_conv", "state_pool",
        "page_table", "rel_bias", "norm1", "w_in", "conv_dw", "conv_b", "conv_ln_g", "conv_ln_b", "pool_w",
        "pool_scale", "cmp_pe_k", "cmp_wk", "cmp_pe_v", "cmp_wv", "w_out", "norm2", "w_gu", "w_down", "final_norm"]
_KVR = KVH * HD * 2
_OUTS = [("y_prompt", (1, T, D), None), ("y_sample", (NB, NS, D), None),
         ("new_cmp_prompt", (T, _KVR), (1, 1, T, 2, KVH, HD)), ("new_slc_prompt", (T, _KVR), (1, 1, T, 2, KVH, HD)),
         ("new_win_prompt", (WINDOW, _KVR), (1, 1, WINDOW, 2, KVH, HD)),
         ("new_conv_prompt", (CB, CONV_W), (1, 1, CB, CONV_W)), ("new_pool_prompt", (PB, POOL_W), (1, 1, PB, POOL_W)),
         ("new_cmp_sample", (TS, _KVR), (1, NB, NS, 2, KVH, HD)), ("new_slc_sample", (TS, _KVR), (1, NB, NS, 2, KVH, HD)),
         ("new_win_sample", (NB, WINDOW, _KVR), (1, NB, WINDOW, 2, KVH, HD)),
         ("new_conv_sample", (NB, CB, CONV_W), (1, NB, CB, CONV_W)),
         ("new_pool_sample", (NB, PB, POOL_W), (1, NB, PB, POOL_W))]


def kernel(**inputs):
    import concourse.bacc as bacc
    from concourse.bass_utils import run_bass_kernel_spmd

    nc = bacc.Bacc("TRN2", target_bir_lowering=False, num_devices=1)
    arrays = {n: np.ascontiguousarray(inputs[n]) for n in _INS}
    arrays.update(constants())
    feed, A = {}, {}
    for n, a in arrays.items():
        feed[f"in_{n}"] = a
        A[n] = nc.dram_tensor(f"in_{n}", a.shape, mybir.dt.from_np(a.dtype), kind="ExternalInput").ap()
    out = {n: nc.dram_tensor(f"out_{n}", shape, F32, kind="ExternalOutput").ap() for n, shape, _ in _OUTS}
    build(nc, A, out)
    r = run_bass_kernel_spmd(nc, [feed], core_ids=[0]).results[0]
    return tuple(r[f"out_{n}"].reshape(full or shape) for n, shape, full in _OUTS)
```

```python
import math
from contextlib import ExitStack

import numpy as np

import concourse.bass as bass
from concourse import mybir

F32 = mybir.dt.float32
F32R = mybir.dt.float32r
I32 = mybir.dt.int32
ALU = mybir.AluOpType
ACT = mybir.ActivationFunctionType
AX = mybir.AxisListType.X

P = 128
D = 1024
T = 1024
NB, NS = 8, 4
TS = NB * NS
TT = T + TS
NT = T // P
KD = D // P
PAST, PAGE = 512, 128
NPG = PAST // PAGE
CONV_W, POOL_W, NH, HD, KVH = 256, 256, 8, 64, 2
GQ = NH // KVH
CW, CB = 31, 30
PB = 15
WINS = (2, 4, 8, 16)
STRIDE, CBLK, WINDOW = 16, 32, 512
NCMP = T // STRIDE - 1
BUCKETS, MAXD = 32, 128
DFF = 2816
KF = DFF // P
EPS, NEG = 1e-6, -1e30
OFF_POOL, OFF_Q = 2 * CONV_W, 2 * CONV_W + POOL_W
OFF_KV = OFF_Q + NH * HD
KVC = 6 * KVH * HD
KVG = KVC + 3 * NH
IN_W = OFF_KV + KVG
NCH = TT // 3
GE, UE = CB + NS, PB + NS
GLU_L = CB + T + NB * GE
U_L = PB + T + NB * UE
Y_L = GLU_L - CB
FT = 2
NF = KF // FT
NLOOP = (NF - 3) // 2
WB = KD
WGU, WDN = 2 * FT, KD
DLO, DHI = -160, 256
ND = DHI - DLO + 1
BAND = 3 * P
C_ID, C_OH, C_MN, C_MW, C_MC = 0, 128, 416, 480, 484
C_GM, C_VA, C_IW, C_FX, C_SEL, C_END = 612, 636, 637, 639, 669, 925
CMPN = 15
KC_L = NB * PAST + TT
KC_N = KC_L // STRIDE - 1


def bucket(n):
    n = np.asarray(n)
    e = BUCKETS // 2
    big = e + (np.log(np.maximum(n, 1).astype(np.float32) / e) / math.log(MAXD / e) * (BUCKETS - e)).astype(np.int32)
    return np.where(n < e, n, np.minimum(big, BUCKETS - 1))


def onehot(d):
    m = np.zeros((BUCKETS + 1, len(d)), np.float32)
    for j, x in enumerate(d):
        if x >= 0:
            m[bucket(x), j] += 1
            m[BUCKETS - 1, j] -= 1
        else:
            m[BUCKETS, j] = NEG
    return m


def constants():
    dist = np.concatenate([onehot(np.arange(DLO, DHI + 1)), onehot(2 * P - 1 - np.arange(BAND))], axis=1)
    c = np.zeros((P, C_END), np.float32)
    c[:, C_ID:C_ID + P] = np.eye(P)
    for t in range(NS):
        r = slice(32 * t, 32 * t + 32)
        c[r, C_OH:C_OH + 128] = onehot(PAST + t - (384 + np.arange(128)))[:32]
        c[r, C_OH + 128:C_OH + 160] = onehot(t - np.tile(np.arange(NS), NB))[:32]
        n = np.tile(np.arange(32), 4)
        o = onehot(PAST + t - (STRIDE * n + CBLK - 1))[:32]
        c[r, C_OH + 160:C_OH + 288] = o
    for row in range(P):
        b, h, t = row // 32, row // 4 % 8, row % 4
        for G in range(2):
            for col in range(32):
                if col // 4 != 4 * G + b or col % 4 > t:
                    c[row, C_MN + 32 * G + col] = NEG
            c[4 * 4 * G + 4 * b + t, C_SEL + 128 * G + row] = 1
        c[row, C_MW:C_MW + 4] = np.where(np.arange(4) <= t, NEG, 0)
        col = np.arange(128)
        c[row, C_MC:C_MC + 128] = np.where((col // 32 != b) | (col % 32 == 31), NEG, 0)
        for br in range(3):
            c[row, C_GM + 8 * br + h] = 1
    c[:, C_VA] = np.arange(P) >= CBLK - 1
    for k in range(2):
        w = np.where(np.arange(P) < 64, WINS[2 * k], WINS[2 * k + 1])
        c[:, C_IW + k] = 1.0 / w
        c[:, C_FX + 15 * k:C_FX + 15 * k + 15] = w[:, None] / np.minimum(w[:, None], np.arange(15)[None] + 1)
    tri = np.where(np.arange(P)[:, None] >= np.arange(P)[None, :], NEG, 0).astype(np.float32)
    return {"c_dist": dist, "c_pack": c, "c_tri": tri}


def tile_rows(i):
    return P if i < NT else TS


SJOBS = [(G, br) for G in range(2) for br in range(3)]
NSJ = len(SJOBS)


def s_width(j):
    return P if SJOBS[j][1] == 0 else PAST + TS


def s_groups(j):
    w = s_width(j)
    cols = [(c, min(P, w - c)) for c in range(0, w, P)]
    return [cols[k:k + 4] for k in range(0, len(cols), 4)]


ORDER = [(0, 1), (0, 0), (0, 2), (1, 1), (1, 0), (1, 2)]
GROUPS = [(i, g, br) for i in range(NT) for g, br in ORDER]
NG = len(GROUPS)
LAG = 3
PSETS = 6


def g_width(n):
    i, _, br = GROUPS[n]
    return 8 * i + 7 if br == 0 else P * (i + 1) if br == 1 else P * min(i + 1, 5)


def g_tiles(n):
    return [(c, min(P, g_width(n) - c)) for c in range(0, g_width(n), P)]


def steps():
    for n in range(NG + LAG):
        old = n - LAG
        tiles = g_tiles(old) if old >= 0 else []
        for r in range(GQ):
            yield (n, r) if n < NG else None, [(old, x) for x in range(len(tiles)) if x * GQ // len(tiles) == r]


def score_places():
    places, last, at = [], [0] * 4, 0
    for n in range(NG):
        wide = g_width(n) > 512
        for r in range(GQ):
            at += at % 2 if wide else 0
            mine = [at % 4, at % 4 + 1] if wide else [at % 4]
            places.append((at % 4, max(last[b] for b in mine)))
            at += len(mine)
            for b in mine:
                last[b] = GQ * n + r + 1
    return places


PLACES = score_places()
ZTILES = [CONV_W, 0, CONV_W + P, P, OFF_POOL, OFF_POOL + P]
NZ = len(ZTILES) + GQ


EARLY_CP = 3


def turn_units():
    keys = [("cp", b, kv) for b in range(EARLY_CP) for kv in range(2)]
    keys += [("knew", 0), ("knew", 1)] + [("kT", ty, hf) for ty in range(4) for hf in range(2)]
    keys += [("pe", 0), ("pe", 1)] + [("cp", b, kv) for b in range(EARLY_CP, NB) for kv in range(2)]
    keys += [("vc", x) for x in range(3)]
    for j in range(-2, NSJ):
        if j + 2 < NSJ and SJOBS[j + 2][1] > 0:
            keys += [("kp", j + 2, b) for b in range(4)]
        if j >= 0:
            keys += [("P", j, k) for k in range(len(s_groups(j)))]
            if j == 3:
                keys.append(("o", 0))
    keys.append(("o", 1))
    for _, tiles in steps():
        keys += [("t",) + x for x in tiles]
    return {k: n for n, k in enumerate(keys)}


UNIT = turn_units()
PUNIT = {k: n for n, k in enumerate([k for k in UNIT if k[0] in "Pt"])}
KUNIT = {k: n for n, k in enumerate([k for k in UNIT if k[0] == "kp"])}
NPT = 3


def build(nc, A, out):
    ctx = ExitStack()
    with ctx:
        def sem(name):
            return ctx.enter_context(nc.semaphore(name))

        def sb(name, shape, at=ctx, dt=F32):
            return at.enter_context(nc.sbuf_tensor(name, shape, dt))

        psA = ctx.enter_context(nc.psum_tensor("psA", [P, 1024], F32))
        psB = ctx.enter_context(nc.psum_tensor("psB", [P, 1024], F32))
        psC = ctx.enter_context(nc.psum_tensor("psC", [P, 1024], F32))
        psD = ctx.enter_context(nc.psum_tensor("psD", [P, 1024], F32))
        bank = [t[:, 512 * k:512 * k + 512] for t in (psA, psB, psC, psD) for k in range(2)]
        scores = [psA, psB]

        cpk = sb("cpk", [P, C_END])
        avg = sb("avg", [P, P])
        featT = sb("featT", [P, KD, TT])
        gB = sb("gB", [P, D])
        small = sb("small", [P, 64])
        nmax = sb("nmax", [P, 4])
        mhalf, epsc = small[:, 0:1], small[:, 1:2]
        stat, ms, rstd = small[:, 2:11], small[:, 11:20], small[:, 20:29]
        convb, lng, lnb, pscale = (small[:, 29 + 2 * k:31 + 2 * k] for k in range(4))
        posk = small[:, 37:39]
        sums = [small[:, 41:45], small[:, 45:49]]
        rec = [small[:, 49:53], small[:, 60:64]]
        sgate = small[:, 53:59]
        ident = cpk[:, C_ID:C_ID + P]

        mid = ExitStack()
        kvtok = sb("kvtok", [P, NT + 1, KVG], mid)
        qT = sb("qT", [P, GQ, TT], mid)
        keysT = sb("keysT", [P, 2, T], mid)
        knewT = sb("knewT", [P, 2, TS], mid)
        btab = sb("btab", [P, NH, 256], mid)
        ctab = sb("ctab", [P, NH, CMPN], mid)
        stab = sb("stab", [P, 320], mid)
        tri = sb("tri", [P, P], mid)
        convw = sb("convw", [P, 2, CW], mid)
        posr = sb("posr", [32, 2, P], mid)
        qbd = sb("qbd", [P, 2, P], mid)

        early = ExitStack()
        ring = sb("ring", [P, 5 * TT], early)
        wring = ring[:, 0:3 * D].rearrange("p (s k n) -> p s k n", s=3, k=KD)
        xring = ring[:, 3 * D:5 * D].rearrange("p (s n) -> p s n", s=2)
        ysq = ring[:, 0:2 * TT].rearrange("p (c t) -> p c t", c=2)
        ystd = ring[:, 2 * TT:3 * TT]
        yc = ring[:, 3 * TT:5 * TT].rearrange("p (c t) -> p c t", c=2)
        kvw = sb("kvw", [P, KD, KVG], early)
        dT = sb("dT", [P, 2, TT], early)
        poolbd = sb("poolbd", [P, 2, P], early)
        ybuf = sb("ybuf", [P, 2, GLU_L], early)
        glu = sb("glu", [P, 2, GLU_L], early)
        uex = sb("uex", [P, 2, U_L], early)
        pl = sb("pl", [P, 2, U_L], early)
        stin = sb("stin", [P, 4, 256], early)
        newcols = sb("newcols", [P, 4, TS], early)
        kflat = kvw[:, :, :].rearrange("p k n -> p (k n)")

        def x_tile(i):
            return xring[:, i % NT, :] if i < 2 or i == NT else kflat[:, D * (i - 2):D * (i - 1)]

        yflat = ybuf[:, :, :].rearrange("p c n -> p (c n)")
        xn = [yflat[:, 0:D], yflat[:, D:2 * D]]
        sig = pl[:, 0, 0:TT]
        sqjunk = pl[:, 1, 0:D]
        dflat = dT[:, :, :].rearrange("p c t -> p (c t)")
        rbias, rbias4 = dflat[0:33, 0:NH], dflat[:, 16:16 + NH]
        fvec = dflat[0:NH, 64:64 + BAND]
        tsel = dflat[:, 448:576]
        distt = dflat[0:33, 576:576 + ND + BAND]
        lastT = stin[0:32, :, :]

        early.close()
        late = ExitStack()
        split = ExitStack()
        kH = sb("kH", [P, 2, KVH, T], split, F32R)
        kL = sb("kL", [P, 2, T], split, F32R)
        qS = sb("qS", [P, 2, KVH, GQ, P], split, F32R)
        split.close()
        pages = sb("pages", [P, 8, NPG, 256], late)
        probTb = sb("probTb", [P, NPT, 512], late)
        kcT = sb("kcT", [P, KC_N - 1], late)
        vcT = sb("vcT", [P, KC_N - 1], late)
        vctok = sb("vctok", [P, 3, P], late)
        probT = [probTb[:, k, :] for k in range(NPT)]
        rawkv = ExitStack()
        cmpw = sb("cmpw", [P, 3, 8, P], rawkv)
        behind = (5 * TT + KD * KVG + 2 * TT + 2 * P) - (8 * NPG * 256 + NPT * 512 + 2 * (KC_N - 1) + 3 * P + 24 * P)
        sb("gap", [P, behind], rawkv)
        ckT = sb("ckT", [P, KC_L], rawkv)
        cvT = sb("cvT", [P, KC_L], rawkv)
        rawkv.close()
        late2 = ExitStack()
        WP = (64, T, 5 * P)
        wide = sb("wide", [P, 2, GQ, WP[1]], late2)
        narrow = sb("narrow", [P, 2 * GQ * (WP[2] + WP[0])], late2)
        sprob = [narrow[:, WP[2] * k:WP[2] * k + WP[2]] for k in range(2)]
        kpT = [narrow[:, 2 * WP[2] + 512 * k:2 * WP[2] + 512 * k + 512] for k in range(2)]
        osmp = [narrow[:, 2 * WP[2] + 1024 + P * k:2 * WP[2] + 1024 + P * k + P] for k in range(2)]
        gjunk = narrow[:, 2 * WP[2] + 1280:2 * WP[2] + 1328]

        def prob(n, r):
            _, k, br = GROUPS[n]
            if br == 1:
                return wide[:, k, r, :]
            at = (0 if br == 2 else 2 * GQ * WP[2]) + (GQ * k + r) * WP[br]
            return narrow[:, at:at + WP[br]]

        def p_scores(n, r):
            b, w = PLACES[GQ * n + r][0], g_width(n)
            at = 512 * (b % 2) if w <= 512 else 512 - w // 2
            return scores[b // 2][:, at:at + w]

        def page_slot(pj, b):
            return pages[:, 4 * pj + b] if pj < 2 else \
                wide[:, pj - 2, b, :].rearrange("p (n c) -> p n c", n=NPG)

        late2.close()
        late.close()
        mid.close()

        fH = sb("fH", [P, KD, TT], dt=F32R)
        fL = sb("fL", [P, KD, TT], dt=F32R)
        wraw = sb("wraw", [P, 2, KD, P])
        wH = sb("wH", [P, 2, KD, P], dt=F32R)
        wL = sb("wL", [P, 2, KD, P], dt=F32R)
        xt = sb("xt", [P, NT + 1, D])
        hid = sb("hid", [P, 3, NCH])
        back0 = ExitStack()
        backT = sb("backT", [P, 2, TT], back0)
        xn2 = sb("xn2", [P, 2, D], back0)
        back0.close()
        aH = sb("aH", [P, 2, FT, TT], dt=F32R)
        aL = sb("aL", [P, 2, FT, TT], dt=F32R)
        yT = featT
        yflat2 = yT[:, :, :].rearrange("p k t -> p (k t)")
        yo = [yflat2[:, D * i:D * i + D] for i in range(NT)] + [hid[:, :, :].rearrange("p a b -> p (a b)")[:, 0:D]]
        aH_sq = yT[:, 0, 0:D]
        sqb = wraw[:, 1].rearrange("p k n -> p (k n)")

        scratch = nc.dram_tensor("bias_scratch", [NH, P, BAND], F32, kind="Internal")

        names = (
            "const_in table_in gain_in x_in0 x_in1 x_in2 x_in3 x_in4 x_in5 x_in6 x_in7 x_in8 state_in w_in0 w_in1 w_in2 kvw_in chan_in poolw_in "
            "tri_in table_mm table_ev fvec_ev fvec_out btab_in tsel_done prep "
            "sq_done ms_done rstd_done xn_done turn_x evac_xa evac_xd state_turn state_ev "
            "z_mm sig_done glu_done zc_done kv_mm kv_ev gates_done valid_done last_out "
            "dve pool pairsum pool_d conv_done mean_mm yc_done sq2_done var_mm std_done norm_done "
            "mix_done pool_mm newcols_done last_turn last_ev stores pzero "
            "late_zero turn_fill turn_drain page_in0 page_in1 page_in2 page_in3 cmpw_in0 cmpw_in1 cmpw_in2 cmpw_used cmp_ev posr_in "
            "gate_mm gate_ev qbd_done score_mm score_in exp_done probT_used keys_used out_done rec_done scaled o_ev tile_split "
            "x2_in mixH_done mixL_done raw_in0 raw_in1 wH_done wL_done unit_mm back_ev back_turn x_add "
            "sq3 ms3 rstd3 xn3 turn3 evac3a evac3d silu_done hid_done aH_done aL_done y_add gain2_in gain3_in "
            "y_done y_out").split()
        s = {n: sem(n) for n in names}
        cpage = [sem(f"cmp_page{b}") for b in range(NB)]
        block = ctx.enter_context(nc.Block())

        chunks = [(NCH * n, NCH) for n in range(3)]
        lnchunks = [(0, 512), (512, 512), (T, TS)]

        POOL_BANKS = ((0, 1, 2), (3, 6, 7))

        def smp(t, L, ext, lo, n):
            return t[:, L:].rearrange("p (b g) -> p b g", g=ext)[:, :, lo:lo + n]

        def ext_cols(t, c, at, w, start, ext, lo):
            parts = []
            if at < T:
                n = min(w, T - at)
                parts.append((0, n, t[:, c, start + at:start + at + n]))
            if at + w > T:
                parts.append((T - at, w, smp(t[:, c, :], start + T, ext, lo, NS)))
            return parts

        def half(w, par):
            return (w - par) // 2 if isinstance(w, int) else (w - par) // 2

        def ffn_order(eng, gu, dn):
            gu(0, WB)
            gu(1, WB + WGU)
            at = WB + 2 * WGU
            with eng.Fori(0, NLOOP) as t:
                for x in range(2):
                    w = t * (2 * (WGU + WDN)) + (at + (WGU + WDN) * x)
                    dn(t * 2 + x, w)
                    gu(t * 2 + (x + 2), w + WDN)
            f = 2 * NLOOP
            at += f * (WGU + WDN)
            dn(f, at)
            gu(f + 2, at + WDN)
            dn(f + 1, at + WDN + WGU)
            dn(f + 2, at + 2 * WDN + WGU)

        @block.sync
        def _(sp):
            def load_x(dst, i):
                n = tile_rows(i)
                src = A["x_prompt"][0, P * i:P * i + P, :] if i < NT else A["x_sample"].rearrange("b t d -> (b t) d")
                return sp.dma_start(dst[0:n, :], src)

            w_in = A["w_in"][0].rearrange("(k p) n -> p k n", p=P)

            def load_z(m):
                slot, q = wring[:, m % 3], m - len(ZTILES)
                if m >= 3:
                    sp.wait_ge(s["z_mm"], m - 2)
                if q < 0:
                    sp.dma_start(slot, w_in[:, :, ZTILES[m]:ZTILES[m] + P]).then_inc(s[f"w_in{m % 3}"], 32)
                else:
                    for g in range(KVH):
                        c = OFF_Q + HD * (GQ * g + q)
                        sp.dma_start(slot[:, :, HD * g:HD * g + HD], w_in[:, :, c:c + HD]).then_inc(s[f"w_in{m % 3}"], 16)

            load_x(x_tile(0), 0).then_inc(s["x_in0"], 16)
            sp.dma_start(cpk[:, :], A["c_pack"]).then_inc(s["const_in"], 16)
            load_x(x_tile(1), 1).then_inc(s["x_in1"], 16)
            sp.dma_start(distt, A["c_dist"]).then_inc(s["table_in"], 16)
            sp.dma_start(rbias[0:32, :], A["rel_bias"]).then_inc(s["table_in"], 16)
            for t in range(NS):
                sp.dma_start(rbias4[32 * t:32 * t + 32, :], A["rel_bias"]).then_inc(s["table_in"], 16)
            sp.dma_start(gB[:, :], A["norm1"].to_broadcast([P, D])).then_inc(s["gain_in"], 16)
            load_x(x_tile(2), 2).then_inc(s["x_in2"], 16)
            for k in range(2):
                sp.dma_start(stin[0:120, k, :], A["state_conv"][0, 4 * k:4 * k + 4].rearrange("b t c -> (b t) c")
                             ).then_inc(s["state_in"], 16)
            sp.dma_start(stin[0:120, 2, :], A["state_pool"][0].rearrange("b t c -> (b t) c")).then_inc(s["state_in"], 16)
            load_x(x_tile(3), 3).then_inc(s["x_in3"], 16)
            load_x(x_tile(4), 4).then_inc(s["x_in4"], 16)
            load_z(0)
            for i in range(5, NT):
                load_x(x_tile(i), i).then_inc(s[f"x_in{i}"], 16)
            sp.wait_ge(s["xn_done"], 1)
            load_x(x_tile(NT), NT).then_inc(s[f"x_in{NT}"], 16)
            load_z(1)
            load_z(2)
            with nc.allow_non_contiguous_dma(reason="per-channel vectors"):
                for t, name in ((convb, "conv_b"), (lng, "conv_ln_g"), (lnb, "conv_ln_b"), (pscale, "pool_scale")):
                    sp.dma_start(t, A[name][0].rearrange("(c p) -> p c", p=P)).then_inc(s["chan_in"], 16)
                for c in range(2):
                    sp.dma_start(convw[:, c, :], A["conv_dw"][0].rearrange("k (c p) -> c p k", p=P)[c]
                                 ).then_inc(s["chan_in"], 16)
            sp.wait_ge(s["xn_done"], NT)
            sp.dma_start(kvw[:, :, :], w_in[:, :, OFF_KV:]).then_inc(s["kvw_in"], 16)
            sp.wait_ge(s["pzero"], 1)
            for g in range(4):
                r = slice(HD * (g % 2), HD * (g % 2) + HD)
                sp.dma_start(poolbd[r, g // 2, r], A["pool_w"][0, g]).then_inc(s["poolw_in"], 16)
            sp.dma_start(tri[:, :], A["c_tri"]).then_inc(s["tri_in"], 16)
            sp.wait_ge(s["fvec_out"], 16)
            band = bass.AP(tensor=scratch, offset=P - 1, ap=[[BAND - 1, P], [P * BAND, NH], [1, 2 * P]])
            sp.dma_start(btab[:, :, :], band).then_inc(s["btab_in"], 16)
            sp.dma_start(posr[:, 0, 0:HD], A["cmp_pe_k"][0]).then_inc(s["posr_in"], 16)
            sp.dma_start(posr[:, 0, HD:P], A["cmp_pe_k"][0]).then_inc(s["posr_in"], 16)
            sp.dma_start(posr[:, 1, 0:HD], A["cmp_pe_v"][0]).then_inc(s["posr_in"], 16)
            sp.dma_start(posr[:, 1, HD:P], A["cmp_pe_v"][0]).then_inc(s["posr_in"], 16)
            page = []
            for m in range(3, NZ):
                load_z(m)
                for b in range(len(page), min(NB, 2 * (m - 2))):
                    page.append([sp.value_load(A["page_table"][b:b + 1, n:n + 1], min_val=0, max_val=NPHYS - 1)
                                 for n in range(NPG)])

            for b in range(NB):
                if b == 0:
                    sp.wait_ge(s["norm_done"], 2)
                elif b == 3:
                    sp.wait_ge(s["mix_done"], 2)
                    sp.wait_ge(s["kv_mm"], NT + 1)
                for n in range(NPG):
                    sp.dma_start(pages[:, b, n, :], A["cache_cmp_kv"][0].rearrange("f p a g d -> f p (a g d)")[
                        bass.ds(page[b][n], 1), :, :].rearrange("f p n -> (f p) n")).then_inc(cpage[b], 16)
            sp.wait_ge(s["late_zero"], 2)

            def load_cmpw(q):
                kv, l0 = q // 4, 8 * (q % 4)
                if q >= 3:
                    sp.wait_ge(s["cmpw_used"], q - 2)
                w = A["cmp_wv" if kv else "cmp_wk"][0, l0:l0 + 8].rearrange("l d e -> d l e")
                for g in range(KVH):
                    r = slice(HD * g, HD * g + HD)
                    sp.dma_start(cmpw[r, q % 3, :, r], w).then_inc(s[f"cmpw_in{q % 3}"], 16)

            def load_pages(pj):
                G, br = pj // 2, 1 + pj % 2
                if pj == 2:
                    sp.wait_ge(s["cmpw_used"], 8)
                for b in range(4):
                    slot = page_slot(pj, b)
                    if pj < 2:
                        sp.wait_ge(s["turn_fill"], UNIT[("cp", 4 * pj + b, 1)] + 1)
                    if br == 1:
                        for n in range(NPG):
                            sp.dma_start(slot[:, n, :], A["cache_slc_kv"][0].rearrange("f p a g d -> f p (a g d)")[
                                bass.ds(page[4 * G + b][n], 1), :, :].rearrange("f p n -> (f p) n")).then_inc(s[f"page_in{pj}"], 16)
                    else:
                        sp.dma_start(slot[:, :, :], A["cache_win_kv"][0, 4 * G + b].rearrange(
                            "(n p) a g d -> p n (a g d)", p=PAGE)).then_inc(s[f"page_in{pj}"], 16)

            for q in range(3):
                load_cmpw(q)
            load_pages(0)
            for q in range(3, 8):
                load_cmpw(q)
            for pj in range(1, 4):
                load_pages(pj)

            sp.wait_ge(s["score_mm"], NSJ + GQ * NG)

            def raw(w, par):
                if not (isinstance(w, int) and w < 2):
                    sp.wait_ge(s["wL_done"], w - 1)
                return wraw[:, par]

            for m in range(KD):
                if m == 2:
                    sp.wait_ge(s["o_ev"], NT)
                    for i in range(NT + 1):
                        load_x(xt[:, i, :], i).then_inc(s["x2_in"], 16)
                    sp.dma_start(gB[:, :], A["norm2"].to_broadcast([P, D])).then_inc(s["gain2_in"], 16)
                slot = raw(m, m % 2)
                cols = slice(P * m, P * m + P)
                sp.dma_start(slot[:, 0:4, :], A["w_out"][0, 0:512, cols].rearrange("(k p) n -> p k n", p=P)
                             ).then_inc(s[f"raw_in{m % 2}"], 16)
                for g in range(KVH):
                    rows = 512 + GQ * HD * g
                    sp.dma_start(slot[HD * g:HD * g + HD, 4:8, :], A["w_out"][0, rows:rows + GQ * HD, cols].rearrange(
                        "(r d) n -> d r n", d=HD)).then_inc(s[f"raw_in{m % 2}"], 16)
            w_gu = A["w_gu"][0].rearrange("(k p) n -> p k n", p=P)
            w_dn = A["w_down"][0].rearrange("(k p) n -> p k n", p=P)

            def load_gu(f, w):
                for x in range(2 * FT):
                    c = (x % 2) * DFF + P * (x // 2)
                    sp.dma_start(raw(w + x, x % 2), w_gu[:, :, bass.ds(f * (FT * P) + c, P)]).then_inc(s[f"raw_in{x % 2}"], 48)

            def load_dn(f, w):
                for m in range(KD):
                    sp.dma_start(raw(w + m, m % 2)[:, 0:FT, :], w_dn[:, bass.ds(f * FT, FT), P * m:P * m + P]
                                 ).then_inc(s[f"raw_in{m % 2}"], 48)

            ffn_order(sp, load_gu, load_dn)
            sp.wait_ge(s["xn3"], NT + 1)
            sp.dma_start(gB[:, :], A["final_norm"][None, :].to_broadcast([P, D])).then_inc(s["gain3_in"], 16)
            for i in range(NT + 1):
                sp.wait_ge(s["y_done"], i + 1)
                n = tile_rows(i)
                dst = out["y_prompt"][0, P * i:P * i + P, :] if i < NT else out["y_sample"].rearrange("b t d -> (b t) d")
                sp.dma_start(dst, yo[i][0:n, :]).then_inc(s["y_out"], 16)
            sp.wait_ge(s["y_out"], 16 * (NT + 1))
            sp.wait_ge(s["stores"], 16 * STORES)
            sp.wait_ge(s["last_out"], 16 * LASTS)

        @block.tensor
        def _(pe):
            def turn_tile(dst, src, n):
                return pe.transpose(dst, src, ident[0:n, 0:n])

            pe.wait_ge(s["const_in"], 16)

            def turn_norm(xs, done, filled, eva, evd, between):
                for i in range(NT + 1):
                    n = tile_rows(i)
                    pe.wait_ge(s[done], i + 1)
                    if i >= 2:
                        pe.wait_ge(s[eva], i - 1)
                        pe.wait_ge(s[evd], i - 1)
                    for k in range(KD):
                        b = bank[4 + 2 * (i % 2) + k // 4]
                        mm = turn_tile(b[:, P * (k % 4):P * (k % 4) + n], xs[i % 2][0:n, P * k:P * k + P], n)
                    mm.then_inc(s[filled], 1)
                    between(i)

            def tables():
                pe.wait_ge(s["table_in"], 16 * 6)
                pe.wait_ge(s["prep"], 1)
                pe.matmul(bank[0][0:NH, 0:BAND], rbias, distt[:, ND:ND + BAND], start=True, stop=True).then_inc(s["table_mm"], 1)
                for c in range(CMPN):
                    at = -(CBLK - 1) - STRIDE * (c - 8) - DLO
                    mm = pe.matmul(bank[1][:, NH * c:NH * c + NH], distt[:, at:at + P], rbias, start=True, stop=True)
                mm.then_inc(s["table_mm"], 1)
                pe.wait_ge(s["tsel_done"], 1)
                pe.matmul(bank[2][:, 0:288], tsel, cpk[:, C_OH:C_OH + 288], start=True, stop=True).then_inc(s["table_mm"], 1)
                pe.wait_ge(s["state_in"], 48)
                for k in range(2):
                    for c in range(2):
                        q = 2 * k + c
                        turn_tile(bank[3][:, 120 * q:120 * q + 120], stin[0:120, k, P * c:P * c + P], 120)
                for c in range(2):
                    mm = turn_tile(bank[1][:, 128 + 120 * c:248 + 120 * c], stin[0:120, 2, P * c:P * c + P], 120)
                mm.then_inc(s["state_turn"], 1)

            def z_chunk(m, n):
                at, w = chunks[n]
                for k in range(KD):
                    mm = pe.matmul(bank[3 * (m % 2) + n][:, 0:w], wring[:, m % 3, k, :], featT[:, k, at:at + w],
                                   start=(k == 0), stop=(k == KD - 1))
                if n == 2:
                    mm.then_inc(s["z_mm"], 1)

            def z_between(i):
                if i == 1:
                    tables()
                for n, after in ((0, 4), (1, 7), (2, 8)):
                    if i == after:
                        if n == 0:
                            pe.wait_ge(s["table_ev"], 2)
                            pe.wait_ge(s["fvec_ev"], 1)
                            pe.wait_ge(s["state_ev"], 2)
                            pe.wait_ge(s["w_in0"], 32)
                        pe.wait_ge(s["evac_xa"], 3 * n + 3)
                        pe.wait_ge(s["evac_xd"], 3 * n + 3)
                        z_chunk(0, n)

            turn_norm(xn, "xn_done", "turn_x", "evac_xa", "evac_xd", z_between)
            for m in range(1, NZ):
                pe.wait_ge(s[f"w_in{m % 3}"], 32 * (m // 3 + 1))
                if m >= 2:
                    p = m - 2
                    if p < 4:
                        pe.wait_ge(s["glu_done" if p % 2 else "sig_done"], p // 2 + 1)
                    else:
                        pe.wait_ge(s["zc_done"], p - 3)
                for n in range(3):
                    z_chunk(m, n)
                if m == 7:
                    pe.wait_ge(s["state_ev"], 2)
                    pe.wait_ge(s["newcols_done"], 1)
                    for c in range(2):
                        turn_tile(bank[6][0:30, P * c:P * c + P], glu[:, c, T:CB + T], P)
                        turn_tile(bank[6][0:15, 256 + P * c:256 + P * c + P], uex[:, c, T:PB + T], P)
                    for c in range(2):
                        turn_tile(bank[7][0:TS, P * c:P * c + P], newcols[:, c, :], P)
                        mm = turn_tile(bank[7][0:TS, 256 + P * c:256 + P * c + P], newcols[:, 2 + c, :], P)
                    mm.then_inc(s["last_turn"], 1)
            nturn = [0]

            def turn(key, parts, first=None):
                u = UNIT[key]
                assert u == nturn[0]
                nturn[0] += 1
                if u >= 2:
                    pe.wait_ge(s["turn_drain"], u - 1)
                for at, n, srcap in parts:
                    m = srcap.free_size()
                    mm = turn_tile(bank[4 + u % 2][0:m, at:at + n], srcap, n)
                mm.then_inc(s["turn_fill"], 1)

            pe.wait_ge(s["kvw_in"], 16)
            pe.wait_ge(s["zc_done"], NZ - 4)
            hk = KVG // 2

            def channel_mean(src, done):
                for n, (at, w) in enumerate(lnchunks):
                    for c in range(2):
                        mm = pe.matmul(bank[4 + n][:, 0:w], avg[:, :], src(c, at, w), start=(c == 0), stop=(c == 1))
                mm.then_inc(s[done], 1)

            def turn_pages(b):
                pe.wait_ge(cpage[b], 16 * NPG)
                for kv in range(2):
                    turn(("cp", b, kv), [(P * x, P, pages[:, b, x, P * kv:P * kv + P]) for x in range(NPG)])

            for i in range(NT + 1):
                n = tile_rows(i)
                if i >= 2:
                    pe.wait_ge(s["kv_ev"], i - 1)
                for hf in range(2):
                    for k in range(KD):
                        mm = pe.matmul(bank[2 * (i % 2) + hf][0:n, 0:hk], featT[:, k, P * i:P * i + n],
                                       kvw[:, k, hk * hf:hk * hf + hk], start=(k == 0), stop=(k == KD - 1))
                mm.then_inc(s["kv_mm"], 1)
                if i == 1:
                    pe.wait_ge(s["last_ev"], 1)
                    pe.wait_ge(s["conv_done"], 1)
                    channel_mean(lambda c, at, w: ybuf[:, c, at:at + w] if at < T else
                                 smp(ybuf[:, c, :], CB + T, GE, 0, NS), "mean_mm")
                elif i == 2:
                    pe.wait_ge(s["sq2_done"], 1)
                    channel_mean(lambda c, at, w: ysq[:, c, at:at + w], "var_mm")
                elif i == NT - EARLY_CP:
                    pe.wait_ge(s["std_done"], 1)
                if NT - EARLY_CP <= i < NT:
                    turn_pages(i - (NT - EARLY_CP))
            pe.wait_ge(s["poolw_in"], 64)
            pe.wait_ge(s["pool_d"], 2)
            pe.wait_ge(s["kv_ev"], NT + 1)
            for c in range(2):
                for n, (at, w) in enumerate(chunks):
                    mm = pe.matmul(bank[POOL_BANKS[c][n]][:, 0:w], poolbd[:, c, :], dT[:, c, at:at + w], start=True, stop=True)
                mm.then_inc(s["pool_mm"], 1)
            for w in range(2):
                turn(("knew", w), [(0, TS, kvtok[0:TS, NT, 256 * (w + 1):256 * (w + 1) + P])])
            for ty in range(4):
                col = (0, 128, 256, 512)[ty]
                for hf in range(2):
                    turn(("kT", ty, hf), [(P * x, P, kvtok[:, 4 * hf + x, col:col + P]) for x in range(4)])
            pe.wait_ge(s["posr_in"], 64)
            for kv in range(2):
                turn(("pe", kv), [(0, 32, posr[:, kv, :])])
            for b in range(EARLY_CP, NB):
                turn_pages(b)
            pe.wait_ge(s["turn_drain"], nturn[0])
            for kv in range(2):
                srcT = cvT if kv else ckT
                for l in range(CBLK):
                    q = 4 * kv + l // 8
                    if l % 8 == 0:
                        pe.wait_ge(s[f"cmpw_in{q % 3}"], 32 * (q // 3 + 1))
                    mm = pe.matmul(bank[kv][:, 0:KC_N], cmpw[:, q % 3, l % 8, :],
                                   srcT[:, l:l + STRIDE * (KC_N - 1) + 1:STRIDE], start=(l == 0), stop=(l == CBLK - 1))
                    if l % 8 == 7:
                        mm.then_inc(s["cmpw_used"], 1)
            for G in range(2):
                mm = pe.matmul(bank[2 + G][:, 0:24], cpk[0:TS, C_SEL + P * G:C_SEL + P * G + P], kvtok[0:TS, NT, KVC:KVG],
                               start=True, stop=True)
            mm.then_inc(s["gate_mm"], 1)
            pe.wait_ge(s["cmp_ev"], 2)
            turn(("vc", 0), [(0, P, vcT[:, NB * 32:NB * 32 + NCMP])])
            for G in range(2):
                turn(("vc", 1 + G), [(0, P, vcT[:, P * G:P * G + P])])
            pe.wait_ge(s["turn_drain"], nturn[0])
            pe.wait_ge(s["gate_ev"], 1)
            pe.wait_ge(s["qbd_done"], 1)

            def score(j):
                i, br = SJOBS[j]
                sc = scores[j % 2]
                if j >= 2:
                    pe.wait_ge(s["exp_done"], j - 1)
                if br == 0:
                    mm = pe.matmul(sc[:, 0:P], qbd[:, i, :], kcT[:, P * i:P * i + P], start=True, stop=True)
                else:
                    pj = 2 * i + br - 1
                    pe.wait_ge(s[f"page_in{pj}"], 256 if br == 1 else 64)
                    for b in range(5):
                        if b < 4:
                            turn(("kp", j, b), [(P * x, P, page_slot(pj, b)[:, x, 0:P]) for x in range(NPG)])
                        if b >= 1:
                            kb = KUNIT[("kp", j, b - 1)]
                            pe.wait_ge(s["turn_drain"], UNIT[("kp", j, b - 1)] + 1)
                            r = slice(32 * (b - 1), 32 * b)
                            pe.matmul(sc[r, 0:PAST], qbd[:, i, r], kpT[kb % 2], start=True, stop=True
                                      ).then_inc(s["keys_used"], 1)
                            mm = pe.matmul(sc[r, PAST:PAST + TS], qbd[:, i, r], knewT[:, br - 1, :], start=True, stop=True)
                mm.then_inc(s["score_mm"], 1)

            def values(j, k):
                i, br = SJOBS[j]
                pu = PUNIT[("P", j, k)]
                pt = probT[pu % NPT]
                o = bank[6 + i]
                pe.wait_ge(s["turn_drain"], UNIT[("P", j, k)] + 1)
                if br == 0:
                    mm = pe.matmul(o[:, 0:P], pt[:, 0:P], vctok[:, 1 + i, :], start=True, stop=True)
                else:
                    for b in range(4):
                        r = slice(32 * b, 32 * b + 32)
                        ob = o[r, P * br:P * br + P]
                        if k == 0:
                            slot = page_slot(2 * i + br - 1, b)
                            for x in range(NPG):
                                mm = pe.matmul(ob, pt[:, P * x + 32 * b:P * x + 32 * b + 32], slot[:, x, P:2 * P],
                                               start=(x == 0), stop=False)
                        else:
                            c = 256 * br + P
                            mm = pe.matmul(ob, pt[0:TS, 32 * b:32 * b + 32], kvtok[0:TS, NT, c:c + P],
                                           start=False, stop=True)
                mm.then_inc(s["probT_used"], 1)

            def turn_out(o):
                pe.wait_ge(s["out_done"], 1 + o)
                turn(("o", o), [(0, P, osmp[o])])

            pend = []
            for j in range(-2, NSJ):
                if j + 2 < NSJ:
                    score(j + 2)
                if j < 0:
                    continue
                pe.wait_ge(s["exp_done"], j + 1)
                for k, grp in enumerate(s_groups(j)):
                    turn(("P", j, k), [(P * x, P, sprob[j % 2][:, c:c + n]) for x, (c, n) in enumerate(grp)])
                    if pend:
                        values(*pend.pop())
                    pend.append((j, k))
                if j == 3:
                    turn_out(0)
            values(*pend.pop())
            turn_out(1)

            def p_score(n, r):
                i, g, br = GROUPS[n]
                pe.wait_ge(s["exp_done"], NSJ + PLACES[GQ * n + r][1])
                sc, w, gp = p_scores(n, r), g_width(n), slice(HD * g, HD * g + HD)
                if br == 0:
                    mm = pe.matmul(sc[:, 0:w], qT[gp, r, P * i:P * i + P], kcT[gp, NB * 32:NB * 32 + w], start=True, stop=True)
                else:
                    if n % 6 == 0 and r == 0:
                        pe.wait_ge(s["tile_split"], i + 1)
                    k0 = 0 if br == 1 else P * (i + 1) - w
                    half_w = w if w <= 512 else w // 2
                    for c in range(0, w, half_w):
                        cols = slice(k0 + c, k0 + c + half_w)
                        pe.matmul(sc[:, c:c + half_w], qS[:, i % 2, g, r, :], kH[:, br - 1, g, cols], start=True, stop=False)
                        mm = pe.matmul(sc[:, c:c + half_w], qS[gp, i % 2, g, r, :], kL[gp, br - 1, cols],
                                       start=False, stop=True)
                mm.then_inc(s["score_mm"], 1)

            def p_values(n, x):
                i, g, br = GROUPS[n]
                c, m = g_tiles(n)[x]
                pe.wait_ge(s["turn_drain"], UNIT[("t", n, x)] + 1)
                mine = [k for k, (h, _) in enumerate(ORDER) if h == g]
                if x == 0 and n % 6 == 0 and i >= 2:
                    pe.wait_ge(s["o_ev"], i - 1)
                if br == 0:
                    v = vctok[0:m, 0, HD * g:HD * g + HD]
                else:
                    kt = c // P if br == 1 else i + 1 - g_width(n) // P + c // P
                    vc = 256 * br + P + HD * g
                    v = kvtok[:, kt, vc:vc + HD]
                mm = pe.matmul(bank[6 + i % 2][HD * g:HD * g + HD, :], v, probT[PUNIT[("t", n, x)] % NPT][0:m, :],
                               start=(x == 0 and mine[0] == n % 6), stop=(x == len(g_tiles(n)) - 1 and mine[-1] == n % 6))
                mm.then_inc(s["probT_used"], 1)

            for scored, tiles in steps():
                if scored:
                    p_score(*scored)
                for n, x in tiles:
                    if x == 0:
                        pe.wait_ge(s["scaled"], GQ * (n + 1))
                    c, m = g_tiles(n)[x]
                    turn(("t", n, x), [(P * r, P, prob(n, r)[:, c:c + m]) for r in range(GQ)])
                    if pend:
                        p_values(*pend.pop())
                    pend.append((n, x))
            p_values(*pend.pop())

            def unit_chunk(par, nk, mH, mL, n, ready):
                at, cw = chunks[n]
                for k in range(nk):
                    ready(n, k)
                    for wt, mv in ((wH, mH), (wH, mL), (wL, mH)):
                        mm = pe.matmul(bank[3 * par + n][:, 0:cw], wt[:, par, k, :], mv[:, k, at:at + cw],
                                       start=(k == 0 and mv is mH and wt is wH), stop=(k == nk - 1 and wt is wL))
                if n == 2:
                    mm.then_inc(s["unit_mm"], 1)

            def unit(w, par, nk, mH, mL, free, ready=lambda n, k: None):
                pe.wait_ge(s["wL_done"], w + 1)
                for n in range(3):
                    free(n)
                    unit_chunk(par, nk, mH, mL, n, ready)

            def turn_back(u0, srcT, m):
                for q in range(3):
                    u = u0 + q
                    if u >= 2:
                        pe.wait_ge(s["x_add"], u - 1)
                    for x in range(3):
                        i = 3 * q + x
                        n = tile_rows(i)
                        mm = turn_tile(bank[6 + q0[0] % 2][0:n, P * x:P * x + P], srcT[:, P * i:P * i + n], P)
                    q0[0] += 1
                    mm.then_inc(s["back_turn"], 1)

            q0 = [0]
            pe.wait_ge(s["exp_done"], NSJ + GQ * NG)
            for m in range(KD + 1):
                if m < KD:
                    unit(m, m % 2, KD, fH, fL, lambda n: pe.wait_ge(s["back_ev"], m - 1) if m >= 2 and n == 0 else None,
                         lambda n, k: pe.wait_ge(s["mixL_done"], k + 1) if m == n == 0 else None)
                if m >= 1:
                    pe.wait_ge(s["back_ev"], m)
                    turn_back(3 * (m - 1), backT[:, (m - 1) % 2, :], m - 1)
            def gate_between(i):
                for n, after in ((0, 4), (1, 7), (2, 8)):
                    if i == after:
                        pe.wait_ge(s["wL_done"], WB + 1)
                        pe.wait_ge(s["evac3d"], 3 * n + 3)
                        unit_chunk(0, KD, fH, fL, n, lambda n, k: None)

            turn_norm([xn2[:, 0, :], xn2[:, 1, :]], "xn3", "turn3", "evac3a", "evac3d", gate_between)

            def gu(f, w):
                for x in range(2 * FT):
                    if isinstance(f, int) and f == x == 0:
                        continue
                    F = f * FT + x // 2
                    if x % 2 == 0:
                        free = lambda n: pe.wait_ge(s["silu_done"], F * 3 + (n - 2)) if x == 2 else before(f, 6, n)
                    else:
                        free = lambda n: pe.wait_ge(s["hid_done"], F * 3 + (n - 2)) if x == 3 else before(f, 7, n)
                    unit(w + x, x % 2, KD, fH, fL, free)

            def before(f, m, n):
                if isinstance(f, int) and f == 0:
                    return
                if isinstance(f, int) and f == 1:
                    pe.wait_ge(s["silu_done" if m == 6 else "hid_done"], 3 * (FT - 1) + n + 1)
                else:
                    pe.wait_ge(s["y_add"], ((f - 2) * KD + m) * 3 + (n + 2))

            def dn(f, w):
                last = not isinstance(f, int) or f < NF - 1
                pe.wait_ge(s["aL_done"], (f + 1) * (3 * FT))
                par = dn_par[0] % 2
                dn_par[0] += 1
                for m in range(KD):
                    if m >= 2 or not last:
                        D_ = f * KD + (m - 2)
                        free = lambda n: pe.wait_ge(s["y_add"], D_ * 3 + (n + 2))
                    else:
                        F = f * FT + (2 * FT - 1)
                        free = lambda n: pe.wait_ge(s["silu_done" if m == 0 else "hid_done"], F * 3 + (n + 1))
                    unit(w + m, m % 2, FT, aH[:, par], aL[:, par], free)
                    if isinstance(f, int) and f == NF - 1 and m >= 2:
                        turn_y(m - 2)

            def turn_y(m):
                pe.wait_ge(s["y_add"], 3 * (KD * (NF - 1) + m + 1) + 1)
                turn_back(3 * (KD + m), yT[:, m, :], m)

            dn_par = [0]
            ffn_order(pe, gu, dn)
            turn_y(KD - 2)
            turn_y(KD - 1)

        @block.scalar
        def _(sc_):
            for i in range(NT + 1):
                n = tile_rows(i)
                sc_.wait_ge(s[f"x_in{i}"], 16)
                if i >= 1:
                    sc_.wait_ge(s["sq_done"], i)
                sc_.activation(sqjunk[0:n, :], x_tile(i)[0:n, :], ACT.Square, accum_out=stat[0:n, i:i + 1]
                               ).then_inc(s["sq_done"], 1)
                if i >= 1:
                    p = i - 1
                    sc_.wait_ge(s["turn_x"], p + 1)
                    sc_.copy(featT[:, 0:4, P * p:P * p + P], bank[4 + 2 * (p % 2)].rearrange("p (k t) -> p k t", k=4)
                             ).then_inc(s["evac_xa"], 1)
            sc_.wait_ge(s["turn_x"], NT + 1)
            sc_.copy(featT[:, 0:4, T:TT], bank[4 + 2 * (NT % 2)].rearrange("p (k t) -> p k t", k=4)[:, :, 0:TS]
                     ).then_inc(s["evac_xa"], 1)
            for m in range(NZ):
                if m in (1, 3):
                    continue
                sc_.wait_ge(s["z_mm"], m + 1)
                if m == 2:
                    sc_.wait_ge(s["glu_done"], 1)
                for n, (at, w) in enumerate(chunks):
                    b = bank[3 * (m % 2) + n]
                    if m in (0, 2):
                        op = sc_.activation(sig[:, at:at + w], b[:, 0:w], ACT.Sigmoid)
                    elif m < len(ZTILES):
                        for lo, hi, dst in ext_cols(uex, m - 4, at, w, PB, UE, PB):
                            srcap = b[:, lo:hi]
                            if lo:
                                srcap = srcap.rearrange("p (b t) -> p b t", t=NS)
                            op = sc_.copy(dst, srcap)
                    else:
                        op = sc_.mul(qT[:, m - len(ZTILES), at:at + w], b[:, 0:w], HD ** -0.5)
                op.then_inc(s["sig_done" if m in (0, 2) else "zc_done"], 1)
                if m == 8:
                    sc_.wait_ge(s["last_turn"], 1)
                    sc_.wait_ge(s["state_turn"], 1)
                    sc_.copy(lastT[0:30, 0, :], bank[6][0:30, 0:256])
                    sc_.copy(lastT[0:15, 1, :], bank[6][0:15, 256:512])
                    sc_.copy(lastT[:, 2:4, :], bank[7][0:TS, :].rearrange("p (k n) -> p k n", k=2)).then_inc(s["last_ev"], 1)
            hk = KVG // 2
            nturn = [0]

            def drain(key, copies):
                u = UNIT[key]
                assert u == nturn[0]
                nturn[0] += 1
                sc_.wait_ge(s["turn_fill"], u + 1)
                for dst, srcfn in copies:
                    op = sc_.copy(dst, srcfn(bank[4 + u % 2]))
                op.then_inc(s["turn_drain"], 1)

            def drain_pages(b_):
                for kv in range(2):
                    drain(("cp", b_, kv), [((cvT if kv else ckT)[:, PAST * b_:PAST * b_ + PAST], lambda b: b)])

            for i in range(NT + 1):
                n = tile_rows(i)
                sc_.wait_ge(s["kv_mm"], i + 1)
                for hf in range(2):
                    op = sc_.copy(kvtok[0:n, i, hk * hf:hk * hf + hk], bank[2 * (i % 2) + hf][0:n, 0:hk])
                op.then_inc(s["kv_ev"], 1)
                if i == 1:
                    sc_.wait_ge(s["yc_done"], 1)
                    for c in range(2):
                        op = sc_.activation(ysq[:, c, :], yc[:, c, :], ACT.Square)
                    op.then_inc(s["sq2_done"], 1)
                elif i == 2:
                    sc_.wait_ge(s["var_mm"], 1)
                    sc_.wait_ge(s["prep"], 1)
                    for k, (at, w) in enumerate(lnchunks):
                        op = sc_.activation(ystd[:, at:at + w], bank[4 + k][:, 0:w], ACT.Sqrt, bias=epsc)
                    op.then_inc(s["std_done"], 1)
                elif i == NT - EARLY_CP:
                    sc_.wait_ge(s["yc_done"], 1)
                    sc_.wait_ge(s["newcols_done"], 1)
                    sc_.wait_ge(s["pool_d"], 2)
                    sc_.wait_ge(s["last_out"], 16 * LASTS)
                if NT - EARLY_CP <= i < NT:
                    drain_pages(i - (NT - EARLY_CP))
            sc_.wait_ge(s["kv_ev"], NT + 1)
            sc_.wait_ge(s["norm_done"], 2)
            sc_.wait_ge(s["chan_in"], 96)
            for c in range(2):
                sc_.activation(featT[:, c, :], yc[:, c, :], ACT.Silu, bias=lnb[:, c:c + 1], scale=lng[:, c:c + 1]
                               ).then_inc(s["mix_done"], 1)
            for c in range(2):
                sc_.wait_ge(s["pool_mm"], c + 1)
                for n, (at, w) in enumerate(chunks):
                    op = sc_.activation(featT[:, 2 + c, at:at + w], bank[POOL_BANKS[c][n]][:, 0:w], ACT.Copy,
                                        scale=pscale[:, c:c + 1])
                op.then_inc(s["mix_done"], 1)
            sc_.activation(kvtok[:, 0:NT, KVC:KVG], kvtok[:, 0:NT, KVC:KVG], ACT.Sigmoid).then_inc(s["gates_done"], 1)
            sc_.activation(kvtok[0:TS, NT, KVC:KVG], kvtok[0:TS, NT, KVC:KVG], ACT.Sigmoid).then_inc(s["gates_done"], 1)

            for w in range(2):
                drain(("knew", w), [(knewT[:, w, :], lambda b: b[:, 0:TS])])
            for ty in range(4):
                for hf in range(2):
                    dst = (ckT[:, NB * PAST:], cvT[:, NB * PAST:], keysT[:, 0], keysT[:, 1])[ty]
                    drain(("kT", ty, hf), [(dst[:, 512 * hf:512 * hf + 512], lambda b: b)])
            for kv in range(2):
                drain(("pe", kv), [((cvT if kv else ckT)[:, KC_L - 32:KC_L], lambda b: b[:, 0:32])])
            for b_ in range(EARLY_CP, NB):
                drain_pages(b_)
            drain(("vc", 0), [(vctok[0:NCMP, 0, :], lambda b: b[0:NCMP, 0:P])])
            for G in range(2):
                drain(("vc", 1 + G), [(vctok[:, 1 + G, :], lambda b: b[:, 0:P])])

            def drain_keys(j):
                for b_ in range(4):
                    kb = KUNIT[("kp", j, b_)]
                    if kb >= 2:
                        sc_.wait_ge(s["keys_used"], kb - 1)
                    drain(("kp", j, b_), [(kpT[kb % 2], lambda b: b)])

            def drain_prob(j, k):
                pu = PUNIT[("P", j, k)]
                if pu >= NPT:
                    sc_.wait_ge(s["probT_used"], pu - NPT + 1)
                grp = s_groups(j)[k]
                n, w = grp[0][1], P * len(grp)
                drain(("P", j, k), [(probT[pu % NPT][0:n, 0:w], lambda b: b[0:n, 0:w])])

            def expo(j):
                G, br = SJOBS[j]
                sc_.wait_ge(s["score_in"], j + 1)
                if j >= 2:
                    sc_.wait_ge(s["turn_fill"], UNIT[("P", j - 2, len(s_groups(j - 2)) - 1)] + 1)
                sc_.activation(sprob[j % 2][:, 0:s_width(j)], scores[j % 2][:, 0:s_width(j)], ACT.Exp,
                               bias=nmax[:, j % 4:j % 4 + 1], accum_out=sums[G][:, br:br + 1]).then_inc(s["exp_done"], 1)

            def drain_out(o):
                copies = []
                for g in range(KVH):
                    gp = slice(HD * g, HD * g + HD)
                    dst = featT[gp, 4:8, T + 16 * o:T + 16 * o + 16].rearrange("p r (b t) -> p b r t", t=NS)
                    copies.append((dst, lambda b, gp=gp, g=g: b[gp, 0:P].rearrange(
                        "p (b g r t) -> p b g r t", b=4, g=KVH, r=GQ)[:, :, g]))
                drain(("o", o), copies)

            for j in range(-2, NSJ):
                if j + 2 < NSJ and SJOBS[j + 2][1] > 0:
                    drain_keys(j + 2)
                if j < 0:
                    if j == -1:
                        expo(0)
                    continue
                for k in range(len(s_groups(j))):
                    drain_prob(j, k)
                    if k == 0 and j + 1 < NSJ:
                        expo(j + 1)
                if j == 3:
                    drain_out(0)
            drain_out(1)

            def p_exp(n, r):
                job = NSJ + GQ * n + r
                w = g_width(n)
                sc_.wait_ge(s["score_in"], job + 1)
                if n >= PSETS:
                    old = n - PSETS
                    sc_.wait_ge(s["turn_fill"], UNIT[("t", old, len(g_tiles(old)) - 1)] + 1)
                if r == 0 and n >= 2:
                    sc_.wait_ge(s["rec_done"], n - 1)
                elif r == 0:
                    sc_.wait_ge(s["out_done"], 2)
                sc_.activation(prob(n, r)[:, 0:w], p_scores(n, r)[:, 0:w], ACT.Exp,
                               bias=nmax[:, job % 4:job % 4 + 1], accum_out=sums[n % 2][:, r:r + 1]).then_inc(s["exp_done"], 1)

            def out_tile(i):
                last = [k for k in PUNIT if k[0] == "t" and GROUPS[k[1]][0] == i][-1]
                sc_.wait_ge(s["probT_used"], PUNIT[last] + 1)
                sc_.copy(featT[:, 4:8, P * i:P * i + P], bank[6 + i % 2].rearrange("p (r t) -> p r t", r=GQ)
                         ).then_inc(s["o_ev"], 1)

            def round_w(w, par, nk):
                sc_.wait_ge(s[f"raw_in{par}"], half(w, par) * 48 + 48)
                if not (isinstance(w, int) and w < 2):
                    sc_.wait_ge(s["unit_mm"], w - 1)
                sc_.copy(wH[:, par, 0:nk, :], wraw[:, par, 0:nk, :]).then_inc(s["wH_done"], 1)

            late_exp, done_tile = None, 0
            for scored, tiles in steps():
                if late_exp:
                    p_exp(*late_exp)
                late_exp = scored
                for n, x in tiles:
                    i = GROUPS[n][0]
                    if (n, x) == (NG - 2, 0):
                        for w in range(2):
                            round_w(w, w, KD)
                    if i > done_tile and (x >= 1 or n != 6 * i):
                        out_tile(done_tile)
                        done_tile += 1
                    pu = PUNIT[("t", n, x)]
                    m = g_tiles(n)[x][1]
                    sc_.wait_ge(s["probT_used"], pu - NPT + 1)
                    drain(("t", n, x), [(probT[pu % NPT][0:m, :], lambda b: b[0:m, :])])
            out_tile(NT - 1)

            def square(base, i):
                n = tile_rows(i)
                at = (NT + 1) * (base - 1) + i
                if at:
                    sc_.wait_ge(s["sq3"], at)
                sc_.activation(sqb2[base - 1][0:n, :], xt[0:n, i, :], ACT.Square, accum_out=stat[0:n, i:i + 1]
                               ).then_inc(s["sq3"], 1)

            sqb2 = [aH_sq, sqb]
            sc_.wait_ge(s["stores"], 16 * STORES)
            for k in range(KD):
                if k == 4:
                    sc_.wait_ge(s["o_ev"], NT)
                sc_.copy(fH[:, k, :], featT[:, k, :]).then_inc(s["mixH_done"], 1)
            for m in range(KD):
                if m >= 1:
                    round_w(m + 1, (m + 1) % 2, KD)
                sc_.wait_ge(s["unit_mm"], m + 1)
                if m >= 2:
                    sc_.wait_ge(s["back_turn"], 3 * (m - 1))
                for n, (at, w) in enumerate(chunks):
                    op = sc_.copy(backT[:, m % 2, at:at + w], bank[3 * (m % 2) + n][:, 0:w])
                op.then_inc(s["back_ev"], 1)
            sc_.wait_ge(s["x_add"], 3 * KD)
            square(1, 0)
            square(1, 1)
            for i in range(NT + 1):
                n = tile_rows(i)
                if i + 2 <= NT:
                    square(1, i + 2)
                sc_.wait_ge(s["turn3"], i + 1)
                for hf in range(2):
                    op = sc_.copy(fH[:, 4 * hf:4 * hf + 4, P * i:P * i + n],
                                  bank[4 + 2 * (i % 2) + hf].rearrange("p (k t) -> p k t", k=4)[:, :, 0:n])
                op.then_inc(s["evac3a"], 1)

            def gu(f, w):
                par = gu_par[0] % 2
                gu_par[0] += 1
                for x in range(2 * FT):
                    F = f * FT + x // 2
                    nxt_dn = x == 2 * FT - 1 and not (isinstance(f, int) and f == 0)
                    round_w(w + (x + 1), (x + 1) % 2, FT if nxt_dn else KD)
                    sc_.wait_ge(s["unit_mm"], w + (x + 1))
                    for n in range(3):
                        if x % 2 == 0:
                            if not (isinstance(f, int) and f == 0 and x == 0):
                                sc_.wait_ge(s["aL_done"], F * 3 + (n - 2))
                            sc_.activation(hid[:, n, :], bank[n][:, 0:NCH], ACT.Silu).then_inc(s["silu_done"], 1)
                        else:
                            sc_.wait_ge(s["hid_done"], F * 3 + (n + 1))
                            at, cw = chunks[n]
                            sc_.copy(aH[:, par, x // 2, at:at + cw], hid[:, n, :]).then_inc(s["aH_done"], 1)

            def dn(f, w):
                for m in range(KD):
                    if m < KD - 1:
                        round_w(w + (m + 1), (m + 1) % 2, FT)
                    elif not isinstance(f, int) or f < NF - 3 + 1:
                        round_w(w + KD, 0, KD)
                    elif f < NF - 1:
                        round_w(w + KD, 0, FT)

            gu_par = [0]
            ffn_order(sc_, gu, dn)
            sc_.wait_ge(s["x_add"], 6 * KD)
            for i in range(NT + 1):
                square(2, i)

        @block.vector
        def _(dve):
            chain = [0]

            def link(op):
                chain[0] += 1
                op.then_inc(s["dve"], 1)
                dve.wait_ge(s["dve"], chain[0])

            dve.memset(mhalf, -0.5)
            dve.memset(epsc, EPS)
            dve.memset(avg[:, :], 1.0 / CONV_W)
            dve.memset(rbias[32:33, :], 1.0).then_inc(s["prep"], 1)
            def tables():
                dve.wait_ge(s["table_mm"], 1)
                dve.tensor_copy(fvec, bank[0][0:NH, 0:BAND]).then_inc(s["fvec_ev"], 1)
                dve.wait_ge(s["table_mm"], 2)
                dve.wait_ge(s["state_turn"], 1)
                dve.tensor_copy(ctab[:, :, :], bank[1][:, 0:CMPN * NH].rearrange("p (c h) -> p h c", h=NH)
                                ).then_inc(s["table_ev"], 1)
                dve.wait_ge(s["table_mm"], 3)
                dve.tensor_copy(stab[:, 0:128], bank[2][:, 0:128])
                for G in range(2):
                    dve.tensor_tensor(stab[:, 128 + 32 * G:160 + 32 * G], bank[2][:, 128:160],
                                      cpk[:, C_MN + 32 * G:C_MN + 32 * G + 32], ALU.add)
                dve.tensor_tensor(stab[:, 192:320], bank[2][:, 160:288], cpk[:, C_MC:C_MC + 128], ALU.add
                                  ).then_inc(s["table_ev"], 1)
                dve.wait_ge(s["state_turn"], 1)
                for c in range(2):
                    for k in range(2):
                        dst = smp(glu[:, c, :], CB + T, GE, 0, CB)[:, 4 * k:4 * k + 4]
                        q = 120 * (2 * k + c)
                        op = dve.tensor_copy(dst, bank[3][:, q:q + 120].rearrange("p (b t) -> p b t", t=CB))
                op.then_inc(s["state_ev"], 1)
                for c in range(2):
                    op = dve.tensor_copy(smp(uex[:, c, :], PB + T, UE, 0, PB), bank[1][:, 128 + 120 * c:248 + 120 * c].rearrange(
                        "p (b t) -> p b t", t=PB))
                op.then_inc(s["state_ev"], 1)

            def norm(xs, outs, sq_, ms_, rs_, xn_, filled, evd, gain, base, free, between=lambda i: None, ahead=0):
                for i in range(-ahead, NT + 3):
                    a = i + ahead
                    if a <= NT:
                        dve.wait_ge(s[sq_], base + a + 1)
                        n = tile_rows(a)
                        dve.tensor_scalar(ms[0:n, a:a + 1], stat[0:n, a:a + 1], 1.0 / D, EPS, ALU.mult, ALU.add
                                          ).then_inc(s[ms_], 1)
                    if i < 0:
                        continue
                    n = tile_rows(i)
                    if i >= 2 and filled:
                        p, n1 = i - 2, tile_rows(i - 2)
                        dve.wait_ge(s[filled], p + 1)
                        if callable(evd):
                            evd(p)
                        else:
                            dve.tensor_copy(featT[:, 4:8, P * p:P * p + n1],
                                            bank[5 + 2 * (p % 2)].rearrange("p (k t) -> p k t", k=4)[:, :, 0:n1]
                                            ).then_inc(s[evd], 1)
                    if i <= NT:
                        dve.wait_ge(s[rs_], base + i + 1)
                        if i == 0:
                            dve.wait_ge(s[gain], 16)
                        free(i)
                        dve.scalar_tensor_tensor(out=outs[i % len(outs)][0:n, :], in0=xs(i)[0:n, :], scalar=rstd[0:n, i:i + 1],
                                                 in1=gB[0:n, :], op0=ALU.mult, op1=ALU.mult).then_inc(s[xn_], 1)
                    between(i)

            norm(x_tile, xn, "sq_done", "ms_done", "rstd_done", "xn_done", "turn_x", "evac_xd",
                 "gain_in", 0, lambda i: dve.wait_ge(s["turn_x"], i - 1) if i >= 2 else None,
                 lambda i: tables() if i == 2 else None)
            for c in range(2):
                dve.wait_ge(s["sig_done"], c + 1)
                dve.wait_ge(s["z_mm"], 2 * c + 2)
                for n, (at, w) in enumerate(chunks):
                    for lo, hi, dst in ext_cols(glu, c, at, w, CB, GE, CB):
                        a, b = bank[3 + n][:, lo:hi], sig[:, at + lo:at + hi]
                        if lo:
                            a, b = (v.rearrange("p (b t) -> p b t", t=NS) for v in (a, b))
                        op = dve.tensor_tensor(dst, a, b, ALU.mult)
                op.then_inc(s["glu_done"], 1)
            dve.wait_ge(s["glu_done"], 2)
            dve.wait_ge(s["chan_in"], 96)
            dve.wait_ge(s["pzero"], 1)
            dve.wait_ge(s["turn_x"], NT + 1)
            for k in range(CW):
                for c in range(2):
                    y, x, w = ybuf[:, c, 0:Y_L], glu[:, c, k:k + Y_L], convw[:, c, k:k + 1]
                    if k == 0:
                        op = dve.tensor_scalar(y, x, w, convb[:, c:c + 1], ALU.mult, ALU.add)
                    else:
                        dve.wait_ge(s["dve"], chain[0] - 1)
                        op = dve.scalar_tensor_tensor(out=y, in0=x, scalar=w, in1=y, op0=ALU.mult, op1=ALU.add)
                    chain[0] += 1
                    op.then_inc(s["dve"], 1)
            dve.wait_ge(s["dve"], chain[0])
            dve.engine_nop().then_inc(s["conv_done"], 1)
            dve.wait_ge(s["mean_mm"], 1)
            for n, (at, w) in enumerate(lnchunks):
                for c in range(2):
                    y, b, o = ybuf[:, c, at:at + w], bank[4 + n][:, 0:w], yc[:, c, at:at + w]
                    if at == T:
                        y = smp(ybuf[:, c, :], CB + T, GE, 0, NS)
                        b, o = (v.rearrange("p (b t) -> p b t", t=NS) for v in (b, o))
                    op = dve.tensor_tensor(o, y, b, ALU.subtract)
            op.then_inc(s["yc_done"], 1)
            dve.wait_ge(s["std_done"], 1)
            link(dve.reciprocal(ystd, ystd))
            for c in range(2):
                dve.tensor_tensor(yc[:, c, :], yc[:, c, :], ystd, ALU.mult).then_inc(s["norm_done"], 1)
            for c in range(2):
                dve.wait_ge(s["pairsum"], c + 1)
                for hp in range(2):
                    r = slice(HD * hp, HD * hp + HD)
                    S = pl[r, hp, :]
                    link(dve.tensor_tensor(S[:, PB:2 * PB], S[:, PB:2 * PB], cpk[r, C_FX + PB * c:C_FX + PB * c + PB], ALU.mult))
                    dve.scalar_tensor_tensor(out=dT[r, c, 0:T], in0=S[:, PB:PB + T], scalar=cpk[r, C_IW + c:C_IW + c + 1],
                                             in1=uex[r, c, PB:PB + T], op0=ALU.mult, op1=ALU.subtract)
                    op = dve.scalar_tensor_tensor(
                        out=dT[r, c, T:TT].rearrange("p (b t) -> p b t", t=NS), in0=smp(S, PB + T, UE, PB, NS),
                        scalar=cpk[r, C_IW + c:C_IW + c + 1], in1=smp(uex[r, c, :], PB + T, UE, PB, NS),
                        op0=ALU.mult, op1=ALU.subtract)
                op.then_inc(s["pool_d"], 1)
            dve.wait_ge(s["gates_done"], 1)
            dve.tensor_scalar(kvtok[:, 0, KVC:KVC + NH], kvtok[:, 0, KVC:KVC + NH], cpk[:, C_VA:C_VA + 1], None, ALU.mult
                              ).then_inc(s["valid_done"], 1)
            for kv, dst in ((0, kcT), (1, vcT)):
                dve.wait_ge(s["cmpw_used"], 4 * (kv + 1))
                if kv == 0:
                    dve.wait_ge(s["late_zero"], 2)
                link(dve.tensor_copy(posk[:, kv:kv + 1], bank[kv][:, KC_N - 1:KC_N]))
                dve.tensor_scalar(dst[:, :], bank[kv][:, 0:KC_N - 1], posk[:, kv:kv + 1], None, ALU.add
                                  ).then_inc(s["cmp_ev"], 1)
            dve.wait_ge(s["gate_mm"], 1)
            for G in range(2):
                link(dve.tensor_tensor(gjunk[:, 24 * G:24 * G + 24], bank[2 + G][:, 0:24], cpk[:, C_GM:C_GM + 24], ALU.mult))
                op = dve.tensor_reduce(sgate[:, 3 * G:3 * G + 3], gjunk[:, 24 * G:24 * G + 24].rearrange(
                    "p (a h) -> p a h", h=NH), AX, ALU.add)
            op.then_inc(s["gate_ev"], 1)
            dve.wait_ge(s["gate_ev"], 1)
            dve.wait_ge(s["btab_in"], 16)
            dve.wait_ge(s["tri_in"], 16)

            def biased_max(job, sc, w, adds):
                dve.wait_ge(s["score_mm"], job + 1)
                for at, tab in adds:
                    n = tab.free_size()
                    op = dve.tensor_tensor(sc[:, at:at + n], sc[:, at:at + n], tab, ALU.add)
                link(op)
                if job >= 4:
                    dve.wait_ge(s["exp_done"], job - 3)
                dve.tensor_reduce(nmax[:, job % 4:job % 4 + 1], sc[:, 0:w], AX, ALU.max, negate=True
                                  ).then_inc(s["score_in"], 1)

            def s_biased_max(j):
                G, br = SJOBS[j]
                if br == 0:
                    adds = [(0, stab[:, 192:320])]
                else:
                    adds = [(384, stab[:, 0:128]), (512, stab[:, 128 + 32 * G:160 + 32 * G])]
                    if br == 2:
                        adds.append((0, cpk[:, C_MW:C_MW + 4]))
                biased_max(j, scores[j % 2], s_width(j), adds)

            def finish(G):
                su, rc, o, dst = sums[G][:, 0:3], rec[G][:, 0:3], bank[6 + G], osmp[G]
                dve.wait_ge(s["exp_done"], 3 * G + 3)
                link(dve.reciprocal(rc, su))
                link(dve.tensor_tensor(rc, rc, sgate[:, 3 * G:3 * G + 3], ALU.mult))
                dve.wait_ge(s["probT_used"], PUNIT[("P", 3 * G + 2, 1)] + 1)
                link(dve.tensor_scalar(dst, o[:, 0:P], rc[:, 0:1], None, ALU.mult))
                link(dve.scalar_tensor_tensor(out=dst, in0=o[:, P:2 * P], scalar=rc[:, 1:2], in1=dst, op0=ALU.mult, op1=ALU.add))
                dve.scalar_tensor_tensor(out=dst, in0=o[:, 2 * P:3 * P], scalar=rc[:, 2:3], in1=dst, op0=ALU.mult,
                                         op1=ALU.add).then_inc(s["out_done"], 1)

            for j in range(-2, NSJ):
                if j + 2 < NSJ:
                    s_biased_max(j + 2)
                if j == 3:
                    finish(0)
            finish(1)

            def p_biased_max(n, r):
                i, g, br = GROUPS[n]
                w, h = g_width(n), GQ * g + r
                if br == 0:
                    m = min(w, CMPN)
                    adds = [(w - m, ctab[:, h, CMPN - m:])]
                else:
                    m = min(w, 256)
                    adds = [(w - m, btab[:, h, 256 - m:])]
                    if br == 2 and i >= 4:
                        adds.append((0, tri[:, :]))
                biased_max(NSJ + GQ * n + r, p_scores(n, r), w, adds)

            def scale(n, r):
                i, g, br = GROUPS[n]
                rc = rec[n % 2]
                if r == 0:
                    dve.wait_ge(s["exp_done"], NSJ + GQ * (n + 1))
                    chain[0] += 1
                    dve.reciprocal(rc, sums[n % 2]).then_inc(s["rec_done"], 1)
                    dve.wait_ge(s["rec_done"], n + 1)
                    c = KVC + NH * br + GQ * g
                    link2(dve.tensor_tensor(rc, rc, kvtok[:, i, c:c + GQ], ALU.mult))
                w = g_width(n)
                p = prob(n, r)[:, 0:w]
                dve.tensor_scalar(p, p, rc[:, r:r + 1], None, ALU.mult).then_inc(s["scaled"], 1)

            def link2(op):
                op.then_inc(s["dve"], 1)
                dve.wait_ge(s["dve"], chain[0])

            def rest_w(w, par, nk):
                dve.wait_ge(s["wH_done"], w + 1)
                dve.tensor_tensor(wL[:, par, 0:nk, :], wraw[:, par, 0:nk, :], wH[:, par, 0:nk, :].bitcast(F32), ALU.subtract
                                  ).then_inc(s["wL_done"], 1)

            for scored, _ in steps():
                if scored:
                    p_biased_max(*scored)
                    n, r = scored
                if scored and n >= 1:
                    scale(n - 1, r)
            for r in range(GQ):
                scale(NG - 1, r)
            for w in range(2):
                rest_w(w, w, KD)

            def add_back(u0, m, par):
                cols = slice(P * m, P * m + P)
                for q in range(3):
                    dve.wait_ge(s["back_turn"], u0 + q + 1)
                    b = bank[6 + (u0 + q) % 2].rearrange("p (x n) -> p x n", n=P)
                    k = 3 if q < 2 else 2
                    x = xt[:, 3 * q:3 * q + k, cols]
                    op = dve.tensor_tensor(x, x, b[:, 0:k], ALU.add)
                    if q == 2:
                        op = dve.tensor_tensor(xt[0:TS, NT, cols], xt[0:TS, NT, cols], b[0:TS, 2], ALU.add)
                    op.then_inc(s["x_add"], 1)

            for k in range(KD):
                dve.wait_ge(s["mixH_done"], k + 1)
                dve.tensor_tensor(fL[:, k, :], featT[:, k, :], fH[:, k, :].bitcast(F32), ALU.subtract
                                  ).then_inc(s["mixL_done"], 1)
            dve.wait_ge(s["x2_in"], 16 * (NT + 1))
            for m in range(KD + 1):
                rest_w_at = m + 1
                if 1 <= m < KD:
                    rest_w(rest_w_at, rest_w_at % 2, KD)
                if m >= 1:
                    add_back(3 * (m - 1), m - 1, 0)
            dve.wait_ge(s["x_add"], 3 * KD)

            def rest_norm(i):
                n = tile_rows(i)
                dve.wait_ge(s["evac3a"], i + 1)
                for hf in range(2):
                    o = (slice(None), slice(4 * hf, 4 * hf + 4), slice(P * i, P * i + n))
                    op = dve.tensor_tensor(fL[o], bank[4 + 2 * (i % 2) + hf].rearrange("p (k t) -> p k t", k=4)[:, :, 0:n],
                                           fH[o].bitcast(F32), ALU.subtract)
                op.then_inc(s["evac3d"], 1)

            norm(lambda i: xt[:, i, :], [xn2[:, 0, :], xn2[:, 1, :]], "sq3", "ms3", "rstd3", "xn3", "turn3", rest_norm,
                 "gain2_in", 0, lambda i: dve.wait_ge(s["turn3"], i - 1) if i >= 2 else None)

            def gu(f, w):
                par = gu_par[0] % 2
                gu_par[0] += 1
                for x in range(2 * FT):
                    F = f * FT + x // 2
                    nxt_dn = x == 2 * FT - 1 and not (isinstance(f, int) and f == 0)
                    rest_w(w + (x + 1), (x + 1) % 2, FT if nxt_dn else KD)
                    if x % 2 == 0:
                        continue
                    dve.wait_ge(s["unit_mm"], w + (x + 1))
                    for y in range(4):
                        if y < 3:
                            dve.wait_ge(s["silu_done"], F * 3 + (y + 1))
                            dve.tensor_tensor(hid[:, y, :], bank[3 + y][:, 0:NCH], hid[:, y, :], ALU.mult
                                              ).then_inc(s["hid_done"], 1)
                        if y >= 1:
                            n = y - 1
                            at, cw = chunks[n]
                            dve.wait_ge(s["aH_done"], F * 3 + (n + 1))
                            dve.tensor_tensor(aL[:, par, x // 2, at:at + cw], hid[:, n, :],
                                              aH[:, par, x // 2, at:at + cw].bitcast(F32), ALU.subtract).then_inc(s["aL_done"], 1)

            def dn(f, w):
                for m in range(KD):
                    if m < KD - 1:
                        rest_w(w + (m + 1), (m + 1) % 2, FT)
                    elif not isinstance(f, int) or f < NF - 3 + 1:
                        rest_w(w + KD, 0, KD)
                    elif f < NF - 1:
                        rest_w(w + KD, 0, FT)
                    if isinstance(f, int) and f == NF - 1 and m >= 2:
                        add_back(3 * (KD + m - 2), m - 2, 0)
                    dve.wait_ge(s["unit_mm"], w + (m + 1))
                    dve.wait_ge(s["y_add"], (f * KD + m) * 3 + 1)
                    for n, (at, cw) in enumerate(chunks):
                        y = yT[:, m, at:at + cw]
                        dve.tensor_tensor(y, y, bank[3 * (m % 2) + n][:, 0:cw], ALU.add).then_inc(s["y_add"], 1)

            gu_par = [0]
            ffn_order(dve, gu, dn)
            add_back(3 * (2 * KD - 2), KD - 2, 0)
            add_back(3 * (2 * KD - 1), KD - 1, 0)
            dve.wait_ge(s["x_add"], 6 * KD)
            norm(lambda i: xt[:, i, :], yo, "sq3", "ms3", "rstd3", "y_done", None, None, "gain3_in", NT + 1,
                 lambda i: None, ahead=1)

        @block.gpsimd
        def _(pool):
            nst = [0]

            def store(dst, src_):
                nst[0] += 1
                pool.dma_start(dst, src_).then_inc(s["stores"], 16)

            for c in range(2):
                pool.memset(glu[:, c, 0:CB], 0.0)
                pool.memset(uex[:, c, 0:PB], 0.0)
            pool.memset(poolbd[:, :, :], 0.0).then_inc(s["pzero"], 1)
            pool.memset(tsel, 0.0).then_inc(s["pool"], 1)
            pool.wait_ge(s["table_in"], 96)
            pool.wait_ge(s["pool"], 1)
            ts = tsel.rearrange("p (b h t) -> p b h t", b=4, h=NH)
            for t in range(NS):
                r = slice(32 * t, 32 * t + 32)
                for b in range(4):
                    op = pool.tensor_copy(ts[r, b, :, t], rbias4[r, :])
            op.then_inc(s["tsel_done"], 1)

            def rstds(ms_, rs_, base):
                pool.wait_ge(s["prep"], 1)
                for i in range(NT + 1):
                    n = tile_rows(i)
                    pool.wait_ge(s[ms_], base + i + 1)
                    pool.tensor_tensor(rstd[0:n, i:i + 1], ms[0:n, i:i + 1], mhalf[0:n, :], ALU.pow).then_inc(s[rs_], 1)

            pool.wait_ge(s["tsel_done"], 1)
            rstds("ms_done", "rstd_done", 0)
            pool.wait_ge(s["fvec_ev"], 1)
            pool.dma_start(scratch.ap(), fvec[:, None, :].to_broadcast([NH, P, BAND])).then_inc(s["fvec_out"], 16)
            store(out["new_win_sample"][:, 0:WINDOW - NS], A["cache_win_kv"][0].rearrange("b t a g d -> b t (a g d)")[:, NS:])
            store(out["new_conv_sample"][:, 0:CB - NS], A["state_conv"][0][:, NS:])
            store(out["new_pool_sample"][:, 0:PB - NS], A["state_pool"][0][:, NS:])
            pool.wait_ge(s["zc_done"], 2)
            pool.wait_ge(s["state_ev"], 2)
            pool.wait_ge(s["glu_done"], 2)
            step = [1]
            for c in range(2):
                for k, src_ in ((c, smp(glu[:, c, :], CB + T, GE, CB, NS)), (2 + c, smp(uex[:, c, :], PB + T, UE, PB, NS))):
                    op = pool.tensor_copy(newcols[:, k, :].rearrange("p (b t) -> p b t", t=NS), src_)
            op.then_inc(s["newcols_done"], 1)

            def plink(op):
                step[0] += 1
                op.then_inc(s["pool"], 1)
                pool.wait_ge(s["pool"], step[0])

            a, b, hi = pl[:, 0, :], pl[:, 1, :], slice(HD, P)
            for c in range(2):
                if c:
                    pool.wait_ge(s["pool_d"], 1)
                u = uex[:, c, :]
                plink(pool.tensor_tensor(a[:, 1:], u[:, 1:], u[:, :-1], ALU.add))
                if c == 0:
                    pool.tensor_tensor(b[hi, 3:], a[hi, 3:], a[hi, 1:-2], ALU.add).then_inc(s["pairsum"], 1)
                    pool.wait_ge(s["last_ev"], 1)
                    pool.dma_start(out["new_conv_prompt"], lastT[0:CB, 0, :]).then_inc(s["last_out"], 16)
                    pool.dma_start(out["new_pool_prompt"], lastT[0:PB, 1, :]).then_inc(s["last_out"], 16)
                    for b_ in range(NB):
                        r = slice(NS * b_, NS * b_ + NS)
                        pool.dma_start(out["new_conv_sample"][b_, CB - NS:], lastT[r, 2, :]).then_inc(s["last_out"], 16)
                        pool.dma_start(out["new_pool_sample"][b_, PB - NS:], lastT[r, 3, :]).then_inc(s["last_out"], 16)
                else:
                    plink(pool.tensor_tensor(b[:, 3:], a[:, 3:], a[:, 1:-2], ALU.add))
                    plink(pool.tensor_tensor(a[:, 7:], b[:, 7:], b[:, 3:-4], ALU.add))
                    pool.tensor_tensor(b[hi, 15:], a[hi, 15:], a[hi, 7:-8], ALU.add).then_inc(s["pairsum"], 1)
            pool.wait_ge(s["pairsum"], 2)
            pool.memset(qbd[:, :, :], 0.0).then_inc(s["late_zero"], 1)
            pool.wait_ge(s["kv_mm"], NT + 1)
            pool.wait_ge(s["pool_mm"], 2)
            pool.memset(cmpw[:, :, :, :], 0.0).then_inc(s["late_zero"], 1)
            pool.wait_ge(s["late_zero"], 2)
            for g in range(KVH):
                gp = slice(HD * g, HD * g + HD)
                for G in range(2):
                    for b_ in range(4):
                        dst = qbd[gp, G, 32 * b_ + 16 * g:32 * b_ + 16 * g + 16].rearrange("p (r t) -> p r t", t=NS)
                        at = T + 16 * G + NS * b_
                        op = pool.tensor_copy(dst, qT[gp, :, at:at + NS])
            op.then_inc(s["qbd_done"], 1)
            pool.wait_ge(s["kv_ev"], NT + 1)
            for br, name in ((0, "cmp"), (1, "slc")):
                store(out[f"new_{name}_prompt"].rearrange("(i p) n -> p i n", p=P), kvtok[:, 0:NT, 256 * br:256 * br + 256])
                store(out[f"new_{name}_sample"], kvtok[0:TS, NT, 256 * br:256 * br + 256])
            store(out["new_win_prompt"].rearrange("(i p) n -> p i n", p=P), kvtok[:, NT - WINDOW // P:NT, 512:768])
            for b_ in range(NB):
                store(out["new_win_sample"][b_, WINDOW - NS:], kvtok[NS * b_:NS * b_ + NS, NT, 512:768])
            assert nst[0] == STORES
            pool.wait_ge(s["probT_used"], PUNIT[("P", 2, 1)] + 1)
            pool.wait_ge(s["turn_drain"], UNIT[("kT", 3, 1)] + 1)
            count = [step[0]]

            def in_turn(op):
                count[0] += 1
                op.then_inc(s["pool"], 1)
                pool.wait_ge(s["pool"], count[0])

            for i in range(NT):
                for g in range(KVH):
                    gp, other = slice(HD * g, HD * g + HD), slice(HD * (1 - g), HD * (1 - g) + HD)
                    cols = slice(P * i, P * i + P)
                    in_turn(pool.tensor_copy(kH[gp, :, g, cols], keysT[gp, :, cols]))
                    in_turn(pool.tensor_copy(kH[other, :, g, cols], keysT[gp, :, cols]))
                    in_turn(pool.tensor_tensor(kL[gp, :, cols], keysT[gp, :, cols], kH[gp, :, g, cols].bitcast(F32),
                                               ALU.subtract))
                if i >= 2:
                    pool.wait_ge(s["score_mm"], NSJ + GQ * 6 * (i - 1))
                for g in range(KVH):
                    gp, other = slice(HD * g, HD * g + HD), slice(HD * (1 - g), HD * (1 - g) + HD)
                    q = qT[gp, :, P * i:P * i + P]
                    in_turn(pool.tensor_copy(qS[gp, i % 2, g, :, :], q))
                    in_turn(pool.tensor_tensor(qS[other, i % 2, g, :, :], q, qS[gp, i % 2, g, :, :].bitcast(F32), ALU.subtract))
                pool.engine_nop().then_inc(s["tile_split"], 1)
            rstds("ms3", "rstd3", 0)
            pool.wait_ge(s["mixL_done"], KD)
            pool.wait_ge(s["sq3"], NT + 1)
            pool.memset(yT[:, :, :], 0.0).then_inc(s["y_add"], 1)
            rstds("ms3", "rstd3", NT + 1)


STORES = 3 + 4 + 1 + NB
LASTS = 2 + 2 * NB
NPHYS = 40

_INS = ["x_prompt", "x_sample", "cache_cmp_kv", "cache_slc_kv", "cache_win_kv", "state_conv", "state_pool",
        "page_table", "rel_bias", "norm1", "w_in", "conv_dw", "conv_b", "conv_ln_g", "conv_ln_b", "pool_w",
        "pool_scale", "cmp_pe_k", "cmp_wk", "cmp_pe_v", "cmp_wv", "w_out", "norm2", "w_gu", "w_down", "final_norm"]
_KVR = KVH * HD * 2
_OUTS = [("y_prompt", (1, T, D), None), ("y_sample", (NB, NS, D), None),
         ("new_cmp_prompt", (T, _KVR), (1, 1, T, 2, KVH, HD)), ("new_slc_prompt", (T, _KVR), (1, 1, T, 2, KVH, HD)),
         ("new_win_prompt", (WINDOW, _KVR), (1, 1, WINDOW, 2, KVH, HD)),
         ("new_conv_prompt", (CB, CONV_W), (1, 1, CB, CONV_W)), ("new_pool_prompt", (PB, POOL_W), (1, 1, PB, POOL_W)),
         ("new_cmp_sample", (TS, _KVR), (1, NB, NS, 2, KVH, HD)), ("new_slc_sample", (TS, _KVR), (1, NB, NS, 2, KVH, HD)),
         ("new_win_sample", (NB, WINDOW, _KVR), (1, NB, WINDOW, 2, KVH, HD)),
         ("new_conv_sample", (NB, CB, CONV_W), (1, NB, CB, CONV_W)),
         ("new_pool_sample", (NB, PB, POOL_W), (1, NB, PB, POOL_W))]


def kernel(**inputs):
    import concourse.bacc as bacc
    from concourse.bass_utils import run_bass_kernel_spmd

    nc = bacc.Bacc("TRN2", target_bir_lowering=False, num_devices=1)
    arrays = {n: np.ascontiguousarray(inputs[n]) for n in _INS}
    arrays.update(constants())
    feed, A = {}, {}
    for n, a in arrays.items():
        feed[f"in_{n}"] = a
        A[n] = nc.dram_tensor(f"in_{n}", a.shape, mybir.dt.from_np(a.dtype), kind="ExternalInput").ap()
    out = {n: nc.dram_tensor(f"out_{n}", shape, F32, kind="ExternalOutput").ap() for n, shape, _ in _OUTS}
    build(nc, A, out)
    r = run_bass_kernel_spmd(nc, [feed], core_ids=[0]).results[0]
    return tuple(r[f"out_{n}"].reshape(full or shape) for n, shape, full in _OUTS)
```
